# Optimizing a Trainium2 kernel written in Bass

```python
import math
import jax, jax.numpy as jnp
from jax import lax
import numpy as np

D_MODEL = 1024
BATCH = 1
SEQ = 512
DEPTH = 1

D_MIX = D_MODEL
HEAD_SIZE = 64
RWKV_DIM = D_MIX // 2
RWKV_HEADS = RWKV_DIM // HEAD_SIZE
POOL_DIM = D_MIX - RWKV_DIM
POOL_WINDOWS = (2, 4, 8, 16)
POOL_GROUPS = len(POOL_WINDOWS)
POOL_GROUP_DIM = POOL_DIM // POOL_GROUPS

DECAY_LORA = max(32, int(round(1.8 * D_MODEL ** 0.5 / 32)) * 32)
AAA_LORA = max(32, int(round(1.8 * D_MODEL ** 0.5 / 32)) * 32)
GATE_LORA = max(32, int(round(0.6 * D_MODEL ** 0.8 / 32)) * 32)
N_DIR = 2
RWKV_IN = 3 * RWKV_DIM + N_DIR * DECAY_LORA + N_DIR * AAA_LORA + GATE_LORA
D_IN = RWKV_IN + POOL_DIM
RWKV_SPLITS = (RWKV_DIM, 2 * RWKV_DIM, 3 * RWKV_DIM,
               3 * RWKV_DIM + N_DIR * DECAY_LORA,
               3 * RWKV_DIM + N_DIR * DECAY_LORA + N_DIR * AAA_LORA)
GN_EPS = 64e-5
RMS_EPS = 1e-5

N_KEYS = 128
N_EXPERTS = N_KEYS * N_KEYS
PEER_HEADS = 8
PEER_TOPK = 16
PEER_QDIM = 256
PEER_KHALF = PEER_QDIM // 2
PEER_BLOCK = 128


def rmsnorm(x, w):
    xf = x.astype(jnp.float32)
    y = xf * lax.rsqrt(jnp.mean(xf * xf, axis=-1, keepdims=True) + RMS_EPS)
    return (y * w.astype(jnp.float32)).astype(x.dtype)

def bi_token_shift(p, mu):
    prev = jnp.pad(p[:, :-1], ((0, 0), (1, 0), (0, 0)))
    nxt = jnp.pad(p[:, 1:], ((0, 0), (0, 1), (0, 0)))
    return p + mu[0] * (prev - p) + mu[1] * (nxt - p)

def wkv7_scan(r, w, k, v, kk, a, reverse):
    B, S, H, N = r.shape

    def step(state, inp):
        r_t, w_t, k_t, v_t, kk_t, a_t = inp
        sa = jnp.einsum('bhvk,bhk->bhv', state, -kk_t)
        state = (state * w_t[:, :, None, :]
                 + sa[..., :, None] * (kk_t * a_t)[..., None, :]
                 + v_t[..., :, None] * k_t[..., None, :])
        out = jnp.einsum('bhvk,bhk->bhv', state, r_t)
        return state, out

    xs = tuple(jnp.moveaxis(t, 1, 0) for t in (r, w, k, v, kk, a))
    state0 = jnp.zeros((B, H, N, N), jnp.float32)
    _, out = lax.scan(step, state0, xs, reverse=reverse)
    return jnp.moveaxis(out, 0, 1)

def multiscale_pool(p, pool_w, pool_scale):
    B, S, _ = p.shape
    pg = p.reshape(B, S, POOL_GROUPS, POOL_GROUP_DIM).astype(jnp.float32)
    cs = jnp.concatenate([jnp.zeros((B, 1, POOL_GROUPS, POOL_GROUP_DIM), jnp.float32),
                          jnp.cumsum(pg, axis=1)], axis=1)
    t = jnp.arange(S)
    outs = []
    for gi, win in enumerate(POOL_WINDOWS):
        half = win // 2
        lo = jnp.clip(t - half, 0, S)
        hi = jnp.clip(t + half, 0, S)
        cnt = (hi - lo).astype(jnp.float32)[None, :, None]
        cs_g = cs[:, :, gi]
        mean = (jnp.take(cs_g, hi, axis=1) - jnp.take(cs_g, lo, axis=1)) / cnt
        outs.append(mean - pg[:, :, gi])
    pooled = jnp.stack(outs, axis=2)
    mixed = jnp.einsum('bsgc,gcd->bsgd', pooled, pool_w.astype(jnp.float32))
    return (mixed.reshape(B, S, POOL_DIM) * pool_scale.astype(jnp.float32)).astype(p.dtype)

def hybrid_mixer(h, w_in, shift_mu, w0, w_up, a0, a_up, g_up, k_k, k_a, r_k,
                 ln_x_w, ln_x_b, pool_w, pool_scale, w_out):
    B, S, _ = h.shape
    f32 = jnp.float32
    p = h @ w_in
    p_rw = bi_token_shift(p[..., :RWKV_IN], shift_mu)
    p_pool = p[..., RWKV_IN:]

    r, k, v, wd, ad, gd = jnp.split(p_rw, RWKV_SPLITS, axis=-1)
    wd = wd.reshape(B, S, N_DIR, DECAY_LORA)
    ad = ad.reshape(B, S, N_DIR, AAA_LORA)

    def heads(t):
        return t.reshape(B, S, RWKV_HEADS, HEAD_SIZE).astype(f32)

    rh = heads(r)
    vh = heads(v)
    kk = heads(k * k_k)
    kk = kk / jnp.maximum(jnp.sqrt(jnp.sum(kk * kk, axis=-1, keepdims=True)), 1e-12)
    g = jax.nn.sigmoid(gd) @ g_up

    o = jnp.zeros((B, S, RWKV_HEADS, HEAD_SIZE), f32)
    bonus = jnp.zeros((B, S, RWKV_HEADS, HEAD_SIZE), f32)
    for d in range(N_DIR):
        wlog = -jax.nn.softplus(-(w0[d] + jnp.tanh(wd[:, :, d]) @ w_up[d])) - 0.5
        decay = jnp.exp(-jnp.exp(wlog.astype(f32)))
        a = jax.nn.sigmoid(a0[d] + ad[:, :, d] @ a_up[d])
        kd = heads(k * (1 + (a - 1) * k_a))
        o = o + wkv7_scan(rh, heads(decay), kd, vh, kk, heads(a), reverse=(d == 1))
        bonus = bonus + jnp.sum(rh * kd * r_k.astype(f32), axis=-1, keepdims=True) * vh

    mu = jnp.mean(o, axis=-1, keepdims=True)
    var = jnp.mean(jnp.square(o - mu), axis=-1, keepdims=True)
    o = ((o - mu) * lax.rsqrt(var + GN_EPS)).reshape(B, S, RWKV_DIM)
    o = o * ln_x_w.astype(f32) + ln_x_b.astype(f32) + bonus.reshape(B, S, RWKV_DIM)
    y_rwkv = (o * g.astype(f32)).astype(h.dtype)

    y_pool = multiscale_pool(p_pool, pool_w, pool_scale)
    return jnp.concatenate([y_rwkv, y_pool], axis=-1) @ w_out

def peer_ffn(h, wq, keys, u_tab, v_tab):
    B, S, D = h.shape
    hb = h.reshape(-1, PEER_BLOCK, D)

    def block_fn(xb):
        T = xb.shape[0]
        q = (xb @ wq).reshape(T, PEER_HEADS, 2, PEER_KHALF)
        s = jnp.einsum('thpc,hpnc->thpn', q.astype(jnp.float32), keys.astype(jnp.float32))
        v1, i1 = lax.top_k(s[:, :, 0], PEER_TOPK)
        v2, i2 = lax.top_k(s[:, :, 1], PEER_TOPK)
        cand = (v1[..., :, None] + v2[..., None, :]).reshape(T, PEER_HEADS, PEER_TOPK * PEER_TOPK)
        cidx = (i1[..., :, None] * N_KEYS + i2[..., None, :]).reshape(T, PEER_HEADS, PEER_TOPK * PEER_TOPK)
        sc, pos = lax.top_k(cand, PEER_TOPK)
        idx = jnp.take_along_axis(cidx, pos, axis=-1)
        gate = jax.nn.softmax(sc, axis=-1)
        ug = jnp.take(u_tab, idx, axis=0)
        act = jax.nn.gelu(jnp.einsum('td,thkd->thk', xb, ug).astype(jnp.float32), approximate=False)
        vg = jnp.take(v_tab, idx, axis=0)
        return jnp.einsum('thk,thkd->td', (gate * act).astype(xb.dtype), vg)

    return lax.map(block_fn, hb).reshape(B, S, D)

def first_inputs(seed: int = 0) -> dict:
    key = jax.random.key(seed)
    ks = jax.random.split(key, 24)
    L = DEPTH
    nrm = lambda k, shape, s: jax.random.normal(k, shape, jnp.float32) * s
    return {
        "x": nrm(ks[0], (BATCH, SEQ, D_MODEL), 1.0),
        "norm1_w": 1.0 + nrm(ks[1], (L, D_MODEL), 0.02),
        "w_in": nrm(ks[2], (L, D_MODEL, D_IN), D_MODEL ** -0.5),
        "shift_mu": jax.random.uniform(ks[3], (L, 2, RWKV_IN), jnp.float32, 0.0, 0.5),
        "w0": nrm(ks[4], (L, N_DIR, RWKV_DIM), 0.5) - 1.0,
        "w_up": nrm(ks[5], (L, N_DIR, DECAY_LORA, RWKV_DIM), 0.1),
        "a0": nrm(ks[6], (L, N_DIR, RWKV_DIM), 0.5),
        "a_up": nrm(ks[7], (L, N_DIR, AAA_LORA, RWKV_DIM), 0.1),
        "g_up": nrm(ks[8], (L, GATE_LORA, RWKV_DIM), GATE_LORA ** -0.5),
        "k_k": 0.85 + nrm(ks[9], (L, RWKV_DIM), 0.05),
        "k_a": 1.0 + nrm(ks[10], (L, RWKV_DIM), 0.05),
        "r_k": nrm(ks[11], (L, RWKV_HEADS, HEAD_SIZE), 0.1),
        "ln_x_w": 1.0 + nrm(ks[12], (L, RWKV_DIM), 0.02),
        "ln_x_b": nrm(ks[13], (L, RWKV_DIM), 0.02),
        "pool_w": nrm(ks[14], (L, POOL_GROUPS, POOL_GROUP_DIM, POOL_GROUP_DIM), POOL_GROUP_DIM ** -0.5),
        "pool_scale": 1.0 + nrm(ks[15], (L, POOL_DIM), 0.1),
        "w_out": nrm(ks[16], (L, D_MIX, D_MODEL), D_MIX ** -0.5),
        "norm2_w": 1.0 + nrm(ks[17], (L, D_MODEL), 0.02),
        "peer_wq": nrm(ks[18], (L, D_MODEL, PEER_HEADS * PEER_QDIM), D_MODEL ** -0.5),
        "peer_keys": nrm(ks[19], (L, PEER_HEADS, 2, N_KEYS, PEER_KHALF), PEER_KHALF ** -0.5),
        "peer_u": nrm(ks[20], (L, N_EXPERTS, D_MODEL), D_MODEL ** -0.5),
        "peer_v": nrm(ks[21], (L, N_EXPERTS, D_MODEL), PEER_HEADS ** -0.5),
        "norm_f_w": 1.0 + nrm(ks[22], (D_MODEL,), 0.02),
    }

def first_block(x, norm1_w, w_in, shift_mu, w0, w_up, a0, a_up, g_up, k_k, k_a, r_k,
              ln_x_w, ln_x_b, pool_w, pool_scale, w_out, norm2_w, peer_wq, peer_keys,
              peer_u, peer_v, norm_f_w):
    for l in range(DEPTH):
        h = rmsnorm(x, norm1_w[l])
        x = x + hybrid_mixer(h, w_in[l], shift_mu[l], w0[l], w_up[l], a0[l], a_up[l], g_up[l],
                             k_k[l], k_a[l], r_k[l], ln_x_w[l], ln_x_b[l], pool_w[l],
                             pool_scale[l], w_out[l])
        h = rmsnorm(x, norm2_w[l])
        x = x + peer_ffn(h, peer_wq[l], peer_keys[l], peer_u[l], peer_v[l])
    return rmsnorm(x, norm_f_w)


CHUNK = 64
N_PREV_CHUNKS = 8
HEAD_DIM = 64
N_HEADS_A = 8
REL_CLIP = 128
N_HEADS_B = 8
N_KV_B = 2
N_IDX_HEADS = 8
IDX_DIM = 64
TOPK_MAX = 256
Q_BLOCK = 128
ROPE_THETA = 500000.0
ROT_DIM = HEAD_DIM // 4
D_FF = 2816
EPS = 1e-6

WIDTH_A = N_HEADS_A * HEAD_DIM
WIDTH_B = N_HEADS_B * HEAD_DIM
WIDTH_KV_B = N_KV_B * HEAD_DIM
SPLIT_SIZES = (WIDTH_A, WIDTH_A, WIDTH_A,
               WIDTH_B, WIDTH_KV_B, WIDTH_KV_B,
               N_IDX_HEADS * IDX_DIM, IDX_DIM,
               N_IDX_HEADS,
               D_MODEL, D_MODEL)
D_IN_2 = sum(SPLIT_SIZES)


def _rmsnorm(x, g):
    xf = x.astype(jnp.float32)
    y = xf * lax.rsqrt(jnp.mean(xf * xf, axis=-1, keepdims=True) + EPS)
    return (y * g.astype(jnp.float32)).astype(x.dtype)

def _swiglu(x, w_in, w_out):
    gate, up = jnp.split(x @ w_in, 2, axis=-1)
    return (jax.nn.silu(gate) * up) @ w_out

def _rope_tables(seq):
    inv_freq = jnp.power(jnp.float32(ROPE_THETA), -jnp.arange(0, ROT_DIM, 2, dtype=jnp.float32) / ROT_DIM)
    ang = jnp.arange(seq, dtype=jnp.float32)[:, None] * inv_freq[None, :]
    return jnp.cos(ang)[:, None, :], jnp.sin(ang)[:, None, :]

def _partial_rope(t, cos, sin):
    tr = t[..., :ROT_DIM].astype(jnp.float32)
    t1, t2 = tr[..., :ROT_DIM // 2], tr[..., ROT_DIM // 2:]
    rot = jnp.concatenate([t1 * cos - t2 * sin, t2 * cos + t1 * sin], axis=-1)
    return jnp.concatenate([rot.astype(t.dtype), t[..., ROT_DIM:]], axis=-1)

def _mixer_a(q, k, v, rel_bias):
    B, S, H, Dh = q.shape
    nc = S // CHUNK
    band_len = (N_PREV_CHUNKS + 1) * CHUNK
    qc = q.reshape(B, nc, CHUNK, H, Dh)

    def band(t):
        tp = jnp.pad(t, ((0, 0), (N_PREV_CHUNKS * CHUNK, 0), (0, 0), (0, 0)))
        tp = tp.reshape(B, nc + N_PREV_CHUNKS, CHUNK, H, Dh)
        return jnp.concatenate([tp[:, j:j + nc] for j in range(N_PREV_CHUNKS + 1)], axis=2)

    kb, vb = band(k), band(v)
    s = jnp.einsum('bnqhd,bnkhd->bnhqk', qc, kb).astype(jnp.float32) * (Dh ** -0.5)
    qi = jnp.arange(CHUNK)
    kj = jnp.arange(band_len)
    dist = N_PREV_CHUNKS * CHUNK + qi[:, None] - kj[None, :]
    bias = rel_bias[:, jnp.clip(dist, -REL_CLIP, REL_CLIP) + REL_CLIP].astype(jnp.float32)
    key_pos = (jnp.arange(nc)[:, None] - N_PREV_CHUNKS) * CHUNK + kj[None, :]
    valid = (key_pos >= 0)[None, :, None, None, :]
    s = jnp.where(valid, s + bias[None, None], -jnp.inf)
    p = jax.nn.softmax(s, axis=-1).astype(vb.dtype)
    o = jnp.einsum('bnhqk,bnkhd->bnqhd', p, vb)
    return o.reshape(B, S, H * Dh)

def _to_blocks(a):
    B, S = a.shape[:2]
    return jnp.moveaxis(a.reshape((B, S // Q_BLOCK, Q_BLOCK) + a.shape[2:]), 1, 0)

def _mixer_b(q, k, v, q_idx, k_idx, w_idx):
    B, S, H, Dh = q.shape
    G = k.shape[2]
    R = H // G
    topk = min(TOPK_MAX, S // 4)
    nb = S // Q_BLOCK
    key_pos = jnp.arange(S)
    w_scaled = w_idx * (N_IDX_HEADS ** -0.5)

    def one_block(args):
        qb, qib, wb, pos_q = args
        sc = jnp.einsum('bqhd,bsd->bqhs', qib, k_idx).astype(jnp.float32) * (IDX_DIM ** -0.5)
        score = jnp.einsum('bqh,bqhs->bqs', wb.astype(jnp.float32), jax.nn.relu(sc))
        limit = (pos_q // CHUNK + 1) * CHUNK
        adm = key_pos[None, :] < limit[:, None]
        score = jnp.where(adm[None], score, -jnp.inf)
        _, idx = lax.top_k(score, topk)
        sel_ok = idx < limit[None, :, None]
        kg = jax.vmap(lambda t, i: t[i])(k, idx)
        vg = jax.vmap(lambda t, i: t[i])(v, idx)
        qg = qb.reshape(B, Q_BLOCK, G, R, Dh)
        s = jnp.einsum('bqgrd,bqkgd->bqgrk', qg, kg).astype(jnp.float32) * (Dh ** -0.5)
        s = jnp.where(sel_ok[:, :, None, None, :], s, -jnp.inf)
        p = jax.nn.softmax(s, axis=-1).astype(vg.dtype)
        o = jnp.einsum('bqgrk,bqkgd->bqgrd', p, vg)
        return o.reshape(B, Q_BLOCK, H * Dh)

    out = lax.map(one_block, (_to_blocks(q), _to_blocks(q_idx), _to_blocks(w_scaled),
                              key_pos.reshape(nb, Q_BLOCK)))
    return jnp.moveaxis(out, 0, 1).reshape(B, S, H * Dh)

def second_inputs(seed: int = 0) -> dict:
    key = jax.random.key(seed)
    ks = jax.random.split(key, 16)
    f32 = jnp.float32

    def w(k, shape, fan_in):
        return jax.random.normal(k, shape, f32) * (fan_in ** -0.5)

    def gain(k):
        return 1.0 + 0.02 * jax.random.normal(k, (DEPTH, D_MODEL), f32)

    return {
        'x': jax.random.normal(ks[0], (BATCH, SEQ, D_MODEL), f32),
        'n1_g': gain(ks[1]),
        'ffn1_w_in': w(ks[2], (DEPTH, D_MODEL, 2 * D_FF), D_MODEL),
        'ffn1_w_out': w(ks[3], (DEPTH, D_FF, D_MODEL), D_FF),
        'n2_g': gain(ks[4]),
        'w_in': w(ks[5], (DEPTH, D_MODEL, D_IN_2), D_MODEL),
        'rel_bias': 0.2 * jax.random.normal(ks[6], (DEPTH, N_HEADS_A, 2 * REL_CLIP + 1), f32),
        'w_branch_a': w(ks[7], (DEPTH, WIDTH_A, D_MODEL), WIDTH_A),
        'w_branch_b': w(ks[8], (DEPTH, WIDTH_B, D_MODEL), WIDTH_B),
        'w_out': w(ks[9], (DEPTH, D_MODEL, D_MODEL), D_MODEL),
        'n3_g': gain(ks[10]),
        'ffn2_w_in': w(ks[11], (DEPTH, D_MODEL, 2 * D_FF), D_MODEL),
        'ffn2_w_out': w(ks[12], (DEPTH, D_FF, D_MODEL), D_FF),
        'nf_g': 1.0 + 0.02 * jax.random.normal(ks[13], (D_MODEL,), f32),
    }

def second_block(x, n1_g, ffn1_w_in, ffn1_w_out, n2_g, w_in, rel_bias, w_branch_a, w_branch_b,
              w_out, n3_g, ffn2_w_in, ffn2_w_out, nf_g):
    B, S, _ = x.shape
    cos, sin = _rope_tables(S)
    split_points = list(np.cumsum(SPLIT_SIZES)[:-1])
    for l in range(DEPTH):
        x = x + 0.5 * _swiglu(_rmsnorm(x, n1_g[l]), ffn1_w_in[l], ffn1_w_out[l])
        h = _rmsnorm(x, n2_g[l])
        qa, ka, va, qb, kb, vb, qi, ki, wi, ga, gb = jnp.split(h @ w_in[l], split_points, axis=-1)
        qa = qa.reshape(B, S, N_HEADS_A, HEAD_DIM)
        ka = ka.reshape(B, S, N_HEADS_A, HEAD_DIM)
        va = va.reshape(B, S, N_HEADS_A, HEAD_DIM)
        qb = _partial_rope(qb.reshape(B, S, N_HEADS_B, HEAD_DIM), cos, sin)
        kb = _partial_rope(kb.reshape(B, S, N_KV_B, HEAD_DIM), cos, sin)
        vb = vb.reshape(B, S, N_KV_B, HEAD_DIM)
        qi = _partial_rope(qi.reshape(B, S, N_IDX_HEADS, IDX_DIM), cos, sin)
        ki = _partial_rope(ki.reshape(B, S, 1, IDX_DIM), cos, sin)[:, :, 0]
        o_a = _mixer_a(qa, ka, va, rel_bias[l])
        o_b = _mixer_b(qb, kb, vb, qi, ki, wi)
        merged = jax.nn.sigmoid(ga) * (o_a @ w_branch_a[l]) + jax.nn.sigmoid(gb) * (o_b @ w_branch_b[l])
        x = x + merged @ w_out[l]
        x = x + 0.5 * _swiglu(_rmsnorm(x, n3_g[l]), ffn2_w_in[l], ffn2_w_out[l])
    return _rmsnorm(x, nf_g)


def setup_inputs(seed=0):
    out = dict(first_inputs(seed))
    for name, value in second_inputs(seed + 1).items():
        if name != "x":
            out[name + "_2"] = value
    return out


def reference(
    x, norm1_w, w_in, shift_mu, w0, w_up, a0, a_up, g_up, k_k, k_a, r_k, ln_x_w, ln_x_b, pool_w,
    pool_scale, w_out, norm2_w, peer_wq, peer_keys, peer_u, peer_v, norm_f_w, n1_g_2,
    ffn1_w_in_2, ffn1_w_out_2, n2_g_2, w_in_2, rel_bias_2, w_branch_a_2, w_branch_b_2, w_out_2,
    n3_g_2, ffn2_w_in_2, ffn2_w_out_2, nf_g_2,
):
    x = first_block(
        x, norm1_w, w_in, shift_mu, w0, w_up, a0, a_up, g_up, k_k, k_a, r_k, ln_x_w, ln_x_b,
        pool_w, pool_scale, w_out, norm2_w, peer_wq, peer_keys, peer_u, peer_v, norm_f_w,
    )
    return second_block(
        x, n1_g_2, ffn1_w_in_2, ffn1_w_out_2, n2_g_2, w_in_2, rel_bias_2, w_branch_a_2,
        w_branch_b_2, w_out_2, n3_g_2, ffn2_w_in_2, ffn2_w_out_2, nf_g_2,
    )


_drawn_inputs = setup_inputs


def setup_inputs(seed=0):
    import zlib

    import numpy as np

    out = dict(_drawn_inputs(seed))
    spreads = {}
    factors = {'k_k': 3.299,
     'ln_x_w': 3.224,
     'ln_x_b': 3.119,
     'n1_g_2': 5.155,
     'n2_g_2': 5.327,
     'rel_bias_2': 4.732,
     'n3_g_2': 7.283,
     'nf_g_2': 2.781}
    for name, (base, spread) in spreads.items():
        noise = np.random.default_rng([zlib.crc32(name.encode()), seed]).standard_normal(out[name].shape)
        drawn = base * np.exp(spread * noise) if base else spread * noise
        out[name] = __import__('jax').numpy.asarray(drawn.astype(out[name].dtype))
    for name, factor in factors.items():
        out[name] = (out[name] * factor).astype(out[name].dtype)
    return out
```

```python
import numpy as np
from contextlib import ExitStack

import concourse.bass as bass
from concourse import mybir

F32 = mybir.dt.float32
U32 = mybir.dt.uint32
ALU = mybir.AluOpType
ACT = mybir.ActivationFunctionType
AX = mybir.AxisListType

P = 128
T = 512
TT = T // P
D = 1024
KD = D // P
HEAD = 64
PAIRS = 4
CHUNK = 64
NCHUNK = T // CHUNK
SUB = 16
DECAY = float(np.exp(-0.5))
GN_EPS = 64e-5
RMS_EPS1 = 1e-5
RMS_EPS2 = 1e-6
N_KEYS = 128
TOPK = 16
PH = 8
SLOTS = PH * TOPK
D_FF = 2816
KF = D_FF // P
IDX_TOPK = 128
NEG = -1.0e30
GONE = -3.0e38
DS = bass.ds

B_R, B_K, B_V, B_WD, B_AD, B_GD, B_POOL, N_IN1 = 0, 4, 8, 12, 13, 14, 16, 20
N_SHIFT = 16
GATE_REST = 32
C_QA, C_KA, C_VA, C_QB, C_KB, C_VB, C_QI, C_KI, C_WI, C_GA, C_GB, N_IN2 = 0, 4, 8, 12, 16, 17, 18, 22, 23, 24, 32, 40
WINDOWS = (2, 4, 8, 16)

VECTORS = [("norm1", 8), ("mu0", 16), ("mu1", 16), ("w0", 8), ("a0", 8), ("k_k", 4), ("k_a", 4),
           ("r_k", 4), ("lnw", 4), ("lnb", 4), ("pool_scale", 4), ("norm2", 8), ("norm_f", 8),
           ("n1", 8), ("n2", 8), ("n3", 8), ("nf", 8)]
V_AT, _at = {}, 0
for _name, _n in VECTORS:
    V_AT[_name] = (_at, _n)
    _at += _n
N_VEC = _at

CONSTS = [("ident", 128), ("ones", 128), ("heads", 128), ("stack", 64), ("swap", 128),
          ("low_near", 128), ("low_far", 128), ("up_near", 128), ("up_far", 128),
          ("low_strict", 128), ("up_strict", 128), ("low_incl", 64), ("up_incl", 64),
          ("reset", 512), ("slot", 16)]
C_AT, _at = {}, 0
for _name, _n in CONSTS:
    C_AT[_name] = (_at, _n)
    _at += _n
N_CONST = _at


class Signals:

    def __init__(self, nc, ctx):
        self.nc, self.used = nc, []
        ctx.callback(self.close)

    def __call__(self, name):
        self.used.append(self.nc.alloc_semaphore(name))
        return self.used[-1]

    def close(self):
        self.nc.clear_and_free_semaphores(self.used)
        self.nc.all_engine_barrier()


class Own:

    def __init__(self, eng, sem, base=0):
        self.eng, self.sem, self.base, self.n = eng, sem, base, 0

    def add(self, ins):
        ins.then_inc(self.sem, 1)
        self.n += 1

    def wait(self, back=0):
        self.eng.wait_ge(self.sem, self.base + (self.n - back))

    def link(self, ins):
        self.add(ins)
        self.wait()


def bcast(ap, axis, n):
    dims = [list(x) for x in ap.ap]
    dims.insert(axis, [0, n])
    return bass.AP(ap.tensor, ap.offset, dims)



def gemm(nc, tag, w, kt, rhs, nblocks, evacuate, ring=4):
    with ExitStack() as ctx:
        signal = Signals(nc, ctx)
        slots = ctx.enter_context(nc.sbuf_tensor(f"{tag}_w", [P, ring, kt, P], F32))
        out = ctx.enter_context(nc.psum_tensor(f"{tag}_out", [P, ring, T], F32))
        w_in = [signal(f"{tag}_weights{b}") for b in range(ring)]
        done = signal(f"{tag}_products")
        free = signal(f"{tag}_banks_free")
        own = signal(f"{tag}_own")
        rounds = nblocks // ring
        assert rounds * ring == nblocks
        block = ctx.enter_context(nc.Block())

        @block.sync
        def _(sp):
            for b in range(ring):
                sp.dma_start(slots[:, b], w[b * P:(b + 1) * P, :].rearrange("p (k n) -> p k n", n=P)).then_inc(w_in[b], 16)
            if rounds > 1:
                with sp.Fori(0, rounds - 1) as i:
                    for b in range(ring):
                        sp.wait_ge(done, ring * i + b + 1)
                        sp.dma_start(slots[:, b], w[DS((ring * i + ring + b) * P, P), :].rearrange(
                            "p (k n) -> p k n", n=P)).then_inc(w_in[b], 16)

        @block.tensor
        def _(pe):
            with pe.Fori(0, rounds) as i:
                for b in range(ring):
                    pe.wait_ge(w_in[b], 16 * i + 16)
                    pe.wait_ge(free, ring * i + b + 1)
                    for k in range(kt):
                        mm = nc.tensor.matmul(out[:, b], slots[:, b, k], rhs(b)[:, k], start=(k == 0), stop=(k == kt - 1))
                    mm.then_inc(done, 1)

        evacuate(nc, block, signal, out, done, free, own, rounds, ring)


def keep_plain(dst, rows=None):
    def evacuate(nc, block, signal, out, done, free, own, rounds, ring):
        @block.scalar
        def _(act):
            act.sem_inc(free, ring)
            with act.Fori(0, rounds) as i:
                for b in range(ring):
                    act.wait_ge(done, ring * i + b + 1)
                    nc.scalar.copy(dst(ring * i + b), out[:, b]).then_inc(free, 1)
    return evacuate


def add_to(x, scale=1.0):
    def evacuate(nc, block, signal, out, done, free, own, rounds, ring):
        @block.vector
        def _(dve):
            dve.sem_inc(free, ring)
            with dve.Fori(0, rounds) as i:
                for b in range(ring):
                    dve.wait_ge(done, ring * i + b + 1)
                    xb = x[:, DS(ring * i + b, 1), :].rearrange("p a t -> p (a t)")
                    nc.vector.scalar_tensor_tensor(out=xb, in0=out[:, b], scalar=float(scale), in1=xb,
                                                   op0=ALU.mult, op1=ALU.add).then_inc(free, 1)
    return evacuate


def swiglu_into(dst, gate):
    def evacuate(nc, block, signal, out, done, free, own, rounds, ring):
        @block.scalar
        def _(act):
            act.sem_inc(free, ring)
            with act.Fori(0, rounds) as i:
                for b in range(0, ring, 2):
                    act.wait_ge(done, ring * i + b + 1)
                    act.wait_ge(free, ring * i + b + 1)
                    nc.scalar.activation(gate[:, b // 2], out[:, b], ACT.Silu).then_inc(own, 1)

        @block.vector
        def _(dve):
            with dve.Fori(0, rounds) as i:
                for b in range(0, ring, 2):
                    dve.wait_ge(done, ring * i + b + 2)
                    dve.wait_ge(own, (ring // 2) * i + b // 2 + 1)
                    d = dst[:, DS((ring // 2) * i + b // 2, 1), :].rearrange("p a t -> p (a t)")
                    nc.vector.tensor_tensor(d, gate[:, b // 2], out[:, b + 1], ALU.mult).then_inc(free, 2)
    return evacuate



def rmsnorm(nc, tag, x, weight, ones, eps, out):
    with ExitStack() as ctx:
        signal = Signals(nc, ctx)
        sq = ctx.enter_context(nc.sbuf_tensor(f"{tag}_sq", [P, KD, T], F32))
        rstd = ctx.enter_context(nc.sbuf_tensor(f"{tag}_rstd", [P, T], F32))
        epst = ctx.enter_context(nc.sbuf_tensor(f"{tag}_eps", [P, 1], F32))
        total = ctx.enter_context(nc.psum_tensor(f"{tag}_total", [P, T], F32))
        squared = signal(f"{tag}_squared")
        summed = signal(f"{tag}_summed")
        rooted = signal(f"{tag}_rooted")
        own = signal(f"{tag}_own")
        block = ctx.enter_context(nc.Block())

        @block.scalar
        def _(act):
            for k in range(0, KD, 2):
                nc.scalar.activation(sq[:, k], x[:, k], ACT.Square).then_inc(squared, 1)
            act.wait_ge(summed, 1)
            act.wait_ge(own, 1)
            nc.scalar.activation(rstd[:, :], total[:, :], ACT.Sqrt, bias=epst[:, 0:1], scale=1.0 / D).then_inc(rooted, 1)

        @block.tensor
        def _(pe):
            pe.wait_ge(squared, KD // 2)
            pe.wait_ge(own, 1 + KD // 2)
            for k in range(KD):
                mm = nc.tensor.matmul(total[:, :], ones, sq[:, k], start=(k == 0), stop=(k == KD - 1))
            mm.then_inc(summed, 1)

        @block.vector
        def _(dve):
            nc.vector.memset(epst[:, :], eps).then_inc(own, 1)
            for k in range(1, KD, 2):
                nc.vector.tensor_tensor(sq[:, k], x[:, k], x[:, k], ALU.mult).then_inc(own, 1)
            dve.wait_ge(rooted, 1)
            nc.vector.reciprocal(rstd[:, :], rstd[:, :]).then_inc(own, 1)
            dve.wait_ge(own, 2 + KD // 2)
            for k in range(KD):
                nc.vector.scalar_tensor_tensor(out=out[:, k], in0=x[:, k], scalar=weight[:, k:k + 1],
                                               in1=rstd[:, :], op0=ALU.mult, op1=ALU.mult)



def token_shift(nc, p, q, mu0, mu1):
    with ExitStack() as ctx:
        signal = Signals(nc, ctx)
        rest = ctx.enter_context(nc.sbuf_tensor("shift_rest", [P, N_SHIFT], F32))
        pads = signal("shift_pads")
        kept = signal("shift_kept")
        own = signal("shift_own")
        block = ctx.enter_context(nc.Block())

        def flat(ap):
            return ap.rearrange("p a t -> p (a t)")

        @block.vector
        def _(dve):
            o = Own(dve, own)
            o.add(nc.vector.memset(p[:, :, 0:1], 0.0))
            o.add(nc.vector.memset(p[:, :, T + 1:T + 2], 0.0))
            o.link(nc.vector.tensor_tensor(rest[:, :], mu0, mu1, ALU.add))
            nc.vector.tensor_scalar(rest[:, :], rest[:, :], -1.0, 1.0, ALU.mult, ALU.add).then_inc(pads, 1)
            with dve.Fori(0, N_SHIFT) as i:
                dve.wait_ge(kept, i + 1)
                d = flat(q[:, DS(i, 1), :])
                nc.vector.scalar_tensor_tensor(out=d, in0=flat(p[:, DS(i, 1), 0:T]), scalar=mu0[:, DS(i, 1)], in1=d,
                                               op0=ALU.mult, op1=ALU.add).then_inc(own, 1)
                dve.wait_ge(own, i + 4)
                nc.vector.scalar_tensor_tensor(out=d, in0=flat(p[:, DS(i, 1), 2:T + 2]), scalar=mu1[:, DS(i, 1)], in1=d,
                                               op0=ALU.mult, op1=ALU.add)

        @block.scalar
        def _(act):
            act.wait_ge(pads, 1)
            with act.Fori(0, N_SHIFT) as i:
                nc.scalar.activation(flat(q[:, DS(i, 1), :]), flat(p[:, DS(i, 1), 1:T + 1]), ACT.Copy,
                                     scale=rest[:, DS(i, 1)]).then_inc(kept, 1)


def rwkv_operands(nc, q, lora, vec, consts, ar, bk, kk, kd_sum, w_end):
    with ExitStack() as ctx:
        signal = Signals(nc, ctx)
        omk = ctx.enter_context(nc.sbuf_tensor("omk", [P, PAIRS], F32))
        nrm = ctx.enter_context(nc.sbuf_tensor("nrm", [P, T], F32))
        sq = ctx.enter_context(nc.sbuf_tensor("kk_sq", [P, PAIRS, T], F32))
        sg = ctx.enter_context(nc.sbuf_tensor("sg", [P, 2, T], F32))
        aa = ctx.enter_context(nc.sbuf_tensor("aa", [P, 2, T], F32))
        cum = ctx.enter_context(nc.sbuf_tensor("cum", [P, 2, T], F32))
        cpre = ctx.enter_context(nc.sbuf_tensor("cpre", [P, 2, T], F32))
        wt = ctx.enter_context(nc.sbuf_tensor("wt", [P, 2, T], F32))
        wpre = ctx.enter_context(nc.sbuf_tensor("wpre", [P, 2, T], F32))
        winv = ctx.enter_context(nc.sbuf_tensor("winv", [P, 2, T], F32))
        kt_ = ctx.enter_context(nc.sbuf_tensor("kt_", [P, 2, T], F32))
        zp = ctx.enter_context(nc.psum_tensor("zp", [P, 2, 2, T], F32))
        np_ = ctx.enter_context(nc.psum_tensor("np_", [P, PAIRS, T], F32))
        tanhed = signal("tanhed")
        squares = signal("kk_squares")
        norms = signal("kk_norms")
        roots = signal("kk_roots")
        kk_done = signal("kk_done")
        zs = signal("lora_products")
        sigs = signal("lora_sigmoids")
        sums = signal("decay_sums")
        exps = signal("decay_exps")
        used = signal("operands_made")
        own = signal("operands_own")
        reset = consts("reset")
        block = ctx.enter_context(nc.Block())

        def row(ap, i):
            return ap[:, DS(i, 1), :].rearrange("p a t -> p (a t)")

        @block.scalar
        def _(act):
            nc.scalar.activation(q[:, B_WD], q[:, B_WD], ACT.Tanh).then_inc(tanhed, 1)
            act.wait_ge(squares, PAIRS)
            for p in range(PAIRS):
                act.wait_ge(norms, p + 1)
                nc.scalar.activation(sq[:, p], np_[:, p], ACT.Sqrt).then_inc(roots, 1)
            with act.Fori(0, PAIRS) as i:
                for d in range(2):
                    act.wait_ge(zs, 2 * i + d + 1)
                    act.wait_ge(used, 2 * i + d + 1)
                    nc.scalar.activation(sg[:, d], zp[:, d, 0], ACT.Sigmoid, bias=vec("w0")[:, DS(i + PAIRS * d, 1)])
                    nc.scalar.activation(aa[:, d], zp[:, d, 1], ACT.Sigmoid, bias=vec("a0")[:, DS(i + PAIRS * d, 1)]).then_inc(sigs, 1)
                for d in range(2):
                    act.wait_ge(sums, 2 * i + d + 1)
                    nc.scalar.activation(wt[:, d], cum[:, d], ACT.Exp, scale=-DECAY)
                    nc.scalar.activation(wpre[:, d], cpre[:, d], ACT.Exp, scale=-DECAY)
                    nc.scalar.activation(winv[:, d], cum[:, d], ACT.Exp, scale=DECAY).then_inc(exps, 1)

        @block.tensor
        def _(pe):
            for p in range(PAIRS):
                pe.wait_ge(squares, p + 1)
                nc.tensor.matmul(np_[:, p], consts("heads"), sq[:, p], start=True, stop=True).then_inc(norms, 1)
            pe.wait_ge(tanhed, 1)
            for p in range(PAIRS):
                for d in range(2):
                    n = 2 * p + d
                    if n >= 2:
                        pe.wait_ge(sigs, n - 1)
                    rows = slice(HEAD * d, HEAD * d + HEAD)
                    nc.tensor.matmul(zp[:, d, 0], lora[rows, 0, p * P:(p + 1) * P], q[rows, B_WD], start=True, stop=True)
                    nc.tensor.matmul(zp[:, d, 1], lora[rows, 1, p * P:(p + 1) * P], q[rows, B_AD],
                                     start=True, stop=True).then_inc(zs, 1)

        @block.vector
        def _(dve):
            dve.sem_inc(used, 2)
            nc.vector.tensor_scalar(omk[:, :], vec("k_a"), -1.0, 1.0, ALU.mult, ALU.add)
            for p in range(PAIRS):
                nc.vector.tensor_scalar(kk[:, p], q[:, B_K + p], vec("k_k")[:, p:p + 1], None, ALU.mult).then_inc(own, 1)
            for p in range(PAIRS):
                dve.wait_ge(own, p + 1)
                nc.vector.tensor_tensor(sq[:, p], kk[:, p], kk[:, p], ALU.mult).then_inc(squares, 1)
            n = PAIRS
            for p in range(PAIRS):
                dve.wait_ge(roots, p + 1)
                nc.vector.tensor_scalar(sq[:, p], sq[:, p], 1e-12, None, ALU.max).then_inc(own, 1)
                n += 1
                dve.wait_ge(own, n)
                nc.vector.reciprocal(nrm[:, :], sq[:, p]).then_inc(own, 1)
                n += 1
                dve.wait_ge(own, n)
                nc.vector.tensor_tensor(kk[:, p], kk[:, p], nrm[:, :], ALU.mult).then_inc(own, 1)
                n += 1
            dve.wait_ge(own, n)
            base = n
            per = 11
            with dve.Fori(0, PAIRS) as i:
                n = 0
                for d in range(2):
                    way = slice(None) if d == 0 else slice(None, None, -1)
                    dve.wait_ge(sigs, 2 * i + d + 1)
                    nc.vector.tensor_tensor_scan(out=cum[:, d, way], data0=reset, data1=sg[:, d, way], initial=0.0,
                                                 op0=ALU.mult, op1=ALU.add).then_inc(own, 1)
                    n += 1
                    nc.vector.tensor_scalar(kt_[:, d], aa[:, d], vec("k_a")[:, DS(i, 1)], omk[:, DS(i, 1)],
                                            ALU.mult, ALU.add).then_inc(own, 1)
                    n += 1
                    dve.wait_ge(own, per * i + base + n - 1)
                    nc.vector.tensor_tensor(cpre[:, d], cum[:, d], sg[:, d], ALU.subtract).then_inc(sums, 1)
                    dve.wait_ge(own, per * i + base + n)
                    nc.vector.tensor_tensor(kt_[:, d], kt_[:, d], row(q[:, B_K:B_K + PAIRS, :], i), ALU.mult).then_inc(own, 1)
                    n += 1
                    nc.vector.tensor_tensor(aa[:, d], aa[:, d], row(kk, i), ALU.mult).then_inc(own, 1)
                    n += 1
                dve.wait_ge(own, per * i + base + n)
                nc.vector.tensor_tensor(row(kd_sum, i), kt_[:, 0], kt_[:, 1], ALU.add).then_inc(own, 1)
                n += 1
                for d in range(2):
                    dve.wait_ge(exps, 2 * i + d + 1)
                    nc.vector.tensor_tensor(row(ar[:, d, 0], i), wpre[:, d], row(kk, i), ALU.mult)
                    nc.vector.tensor_tensor(row(ar[:, d, 1], i), wt[:, d], row(q[:, B_R:B_R + PAIRS, :], i), ALU.mult)
                    nc.vector.scalar_tensor_tensor(out=row(bk[:, d, 0], i), in0=aa[:, d], scalar=-1.0, in1=winv[:, d],
                                                   op0=ALU.mult, op1=ALU.mult)
                    nc.vector.tensor_tensor(row(bk[:, d, 1], i), kt_[:, d], winv[:, d], ALU.mult).then_inc(own, 1)
                    n += 1
                    ends = wt[:, d, CHUNK - 1::CHUNK] if d == 0 else wt[:, d, 0::CHUNK]
                    nc.vector.tensor_copy(w_end[:, d, :, DS(i, 1)].rearrange("p c a -> p (c a)"), ends).then_inc(used, 1)
                assert n == per, n


def recurrence(nc, ar, bk, v, w_end, consts, o):
    with ExitStack() as ctx:
        signal = Signals(nc, ctx)
        def sb(name, *shape):
            return ctx.enter_context(nc.sbuf_tensor(name, [P, 2, PAIRS, *shape], F32))

        a_w, b_w, k_w, v_w = (sb(f"{n}_wide_c", P) for n in "abkv")
        DT, Dm, E, LkT = sb("DT", P), sb("Dm", P), sb("E", P), sb("LkT", P)
        PbT, PkT, V, B = sb("PbT", HEAD), sb("PkT", HEAD), sb("V", HEAD), sb("B", HEAD)
        Vw, Bw, Kw = sb("Vw", P), sb("Bw", P), sb("Kw", P)
        D2, D2T, R1, R2, X = sb("D2", P), sb("D2T", P), sb("R1", P), sb("R2", P), sb("X", P)
        D4, D4T, D8, N, NT, N2T, X1, X2, Y = Dm, DT, D2, D2T, Dm, DT, LkT, E, R1
        Aw, Uw, MTw, RT = sb("Aw", P), sb("Uw", P), sb("MTw", P), sb("RT", HEAD)
        S, Sw, Sn = sb("S", HEAD), sb("Sw", P), sb("Sn", HEAD)
        banks = ctx.enter_context(nc.psum_tensor("rec_banks", [P, 2, 4, PAIRS, P], F32))

        pe_done = [signal(f"rec_products{d}") for d in range(2)]
        by_dve = [signal(f"rec_by_vector{d}") for d in range(2)]
        by_act = [signal(f"rec_by_scalar{d}") for d in range(2)]
        loaded = [signal(f"rec_wide{d}") for d in range(2)]
        sw_done = [signal(f"rec_state_wide{d}") for d in range(2)]
        own = signal("rec_own")

        STEPS = [("LbT", "v"), ("LkT", "v"), ("Lb", "v"), ("VB", "a"), ("KG", "a"), ("D2", "a"), ("D2T", "a"),
                 ("R2", "v"), ("D4", "a"), ("D4T", "a"), ("R3", "v"), ("D8", "a"), ("R4", "v"),
                 ("N", "a"), ("NT", "a"), ("X1", "a"), ("N2T", "a"), ("X2", "v"), ("Y", "v"),
                 ("MR", "v"), ("out", "a"), ("S", "v")]
        AT = {name: n for n, (name, _) in enumerate(STEPS)}
        NS = len(STEPS)
        ORD, PER = {}, {"v": 0, "a": 0}
        for name, e in STEPS:
            PER[e] += 1
            ORD[name] = (e, PER[e])
        WIDE_Y, WIDE_M = ORD["N2T"][1] + 1, ORD["N2T"][1] + 2
        ORD["out"] = ("a", WIDE_M + 1)
        PER["a"] += 2

        with nc.Block() as block:
            @block.vector
            def _(dve):
                for w in (Vw, Bw, Kw, Aw, Uw, MTw):
                    nc.vector.memset(w[:, :, :, :], 0.0)

            @block.gpsimd
            def _(pool):
                for w in (a_w, b_w, k_w, v_w, Sw, S):
                    nc.gpsimd.memset(w[:, :, :, :], 0.0)

        block = ctx.enter_context(nc.Block())

        def chunk(c, d):
            return c * CHUNK if d == 0 else c * -CHUNK + (NCHUNK - 1) * CHUNK

        halves = [(slice(0, HEAD), slice(0, HEAD)), (slice(HEAD, P), slice(HEAD, P))]

        @block.gpsimd
        def _(pool):
            def widen(c, d):
                at = chunk(c, d)
                for w, src in ((b_w, bk[:, d, 0]), (a_w, ar[:, d, 0]), (k_w, bk[:, d, 1]), (v_w, v)):
                    for rows, cols in halves:
                        ins = nc.gpsimd.tensor_copy(w[rows, d, :, cols], src[rows, :, DS(at, CHUNK)])
                ins.then_inc(loaded[d], 1)

            for d in range(2):
                widen(0, d)
            with pool.Fori(0, NCHUNK - 1) as c:
                for d in range(2):
                    pool.wait_ge(pe_done[d], NS * c + AT["KG"] + 1)
                    widen(c + 1, d)

        @block.tensor
        def _(pe):
            def after(c, d, name):
                e, n = ORD[name]
                pe.wait_ge((by_dve if e == "v" else by_act)[d], 1 + PER[e] * c + n)

            with pe.Fori(0, NCHUNK) as c:
                def each(name, d, parts):
                    n = AT[name]
                    for p in range(PAIRS):
                        for cols, products in parts(p):
                            for j, (lhs, rhs) in enumerate(products):
                                mm = nc.tensor.matmul(banks[:, d, n % 4, p, cols], lhs, rhs,
                                                      start=(j == 0), stop=(j == len(products) - 1))
                    mm.then_inc(pe_done[d], 1)

                full, left, right = slice(0, P), slice(0, HEAD), slice(HEAD, P)
                stack = consts("stack")
                both = (0, 1)
                for d in both:
                    at = chunk(c, d)
                    pe.wait_ge(loaded[d], c + 1)
                    pe.wait_ge(by_act[d], 1 + PER["a"] * c)
                    pe.wait_ge(by_dve[d], 1 + PER["v"] * c)
                    each("LbT", d, lambda p: [(full, [(b_w[:, d, p], ar[:, d, :, p, DS(at, CHUNK)])])])
                    each("LkT", d, lambda p: [(full, [(k_w[:, d, p], ar[:, d, :, p, DS(at, CHUNK)])])])
                    each("Lb", d, lambda p: [(left, [(a_w[:, d, p], bk[:, d, 0, p, DS(at, CHUNK)])]),
                                             (right, [(a_w[:, d, p], stack)])])
                    each("VB", d, lambda p: [(left, [(v_w[:, d, p], stack)]), (right, [(b_w[:, d, p], stack)])])
                for d in both:
                    after(c, d, "LbT")
                    after(c, d, "LkT")
                    after(c, d, "VB")
                    each("KG", d, lambda p: [(left, [(k_w[:, d, p], stack)]), (right, [(LkT[:, d, p], V[:, d, p])])])
                for d in both:
                    after(c, d, "Lb")
                    each("D2", d, lambda p: [(full, [(DT[:, d, p], Dm[:, d, p])])])
                    each("D2T", d, lambda p: [(full, [(Dm[:, d, p], DT[:, d, p])])])
                for d in both:
                    after(c, d, "D2")
                    each("R2", d, lambda p: [(full, [(D2[:, d, p], R1[:, d, p])])])
                    after(c, d, "D2T")
                    each("D4", d, lambda p: [(full, [(D2T[:, d, p], D2[:, d, p])])])
                    each("D4T", d, lambda p: [(full, [(D2[:, d, p], D2T[:, d, p])])])
                for d in both:
                    after(c, d, "R2")
                    after(c, d, "D4")
                    each("R3", d, lambda p: [(full, [(D4[:, d, p], R2[:, d, p])])])
                    after(c, d, "D4T")
                    each("D8", d, lambda p: [(full, [(D4T[:, d, p], D4[:, d, p])])])
                for d in both:
                    after(c, d, "R3")
                    after(c, d, "D8")
                    each("R4", d, lambda p: [(full, [(D8[:, d, p], R1[:, d, p])])])
                for d in both:
                    after(c, d, "R4")
                    each("N", d, lambda p: [(full, [(R2[:, d, p], E[:, d, p])])])
                    each("NT", d, lambda p: [(full, [(E[:, d, p], R2[:, d, p])])])
                    after(c, d, "KG")
                    each("X1", d, lambda p: [(full, [(R2[:, d, p], X[:, d, p])])])
                for d in both:
                    after(c, d, "NT")
                    each("N2T", d, lambda p: [(full, [(N[:, d, p], NT[:, d, p])])])
                for d in both:
                    after(c, d, "N2T")
                    each("X2", d, lambda p: [(full, [(N2T[:, d, p], X1[:, d, p])])])
                for d in both:
                    after(c, d, "X2")
                    each("Y", d, lambda p: [(full, [(NT[:, d, p], X2[:, d, p])])])
                for d in both:
                    pe.wait_ge(by_act[d], 1 + PER["a"] * c + WIDE_Y)
                    each("MR", d, lambda p: [(left, [(Aw[:, d, p], B[:, d, p])]), (right, [(Aw[:, d, p], PbT[:, d, p])])])
                for d in both:
                    after(c, d, "MR")
                    pe.wait_ge(by_act[d], 1 + PER["a"] * c + WIDE_M)
                    pe.wait_ge(sw_done[d], c + 1)
                    each("out", d, lambda p: [(left, [(Sw[:, d, p], RT[:, d, p]), (Uw[:, d, p], PbT[:, d, p]),
                                                      (Vw[:, d, p], PkT[:, d, p])])])
                    each("S", d, lambda p: [(left, [(MTw[:, d, p], S[:, d, p]), (Bw[:, d, p], Y[:, d, p, HEAD:P]),
                                                    (Kw[:, d, p], V[:, d, p])])])

        @block.scalar
        def _(act):
            for d in range(2):
                act.sem_inc(by_act[d], 1)
            with act.Fori(0, NCHUNK) as c:
                def ready(d, name):
                    act.wait_ge(pe_done[d], NS * c + AT[name] + 1)

                def bank(d, name):
                    return banks[:, d, AT[name] % 4]

                def wide(dst, src, d):
                    for rows, cols in halves:
                        ins = nc.scalar.copy(dst[rows, d, :, cols], src[rows])
                    return ins

                def plain(dst, name, d):
                    ready(d, name)
                    nc.scalar.copy(dst[:, d], bank(d, name)).then_inc(by_act[d], 1)

                both = (0, 1)
                for d in both:
                    ready(d, "VB")
                    b = bank(d, "VB")
                    nc.scalar.copy(V[:, d], b[:, :, 0:HEAD])
                    nc.scalar.copy(B[:, d], b[:, :, HEAD:P])
                    wide(Vw, b[:, :, 0:HEAD], d)
                    wide(Bw, b[:, :, HEAD:P], d).then_inc(by_act[d], 1)
                for d in both:
                    ready(d, "KG")
                    b = bank(d, "KG")
                    wide(Kw, b[:, :, 0:HEAD], d)
                    nc.scalar.copy(X[:, d, :, HEAD:P], b[:, :, HEAD:P]).then_inc(by_act[d], 1)
                for d in both:
                    plain(D2, "D2", d)
                    plain(D2T, "D2T", d)
                for d in both:
                    plain(D4, "D4", d)
                    plain(D4T, "D4T", d)
                for d in both:
                    plain(D8, "D8", d)
                for d in both:
                    plain(N, "N", d)
                    plain(NT, "NT", d)
                    plain(X1, "X1", d)
                for d in both:
                    plain(N2T, "N2T", d)
                for d in both:
                    act.wait_ge(by_dve[d], 1 + PER["v"] * c + ORD["Y"][1])
                    wide(Aw, Y[:, d, :, 0:HEAD], d)
                    wide(Uw, Y[:, d, :, HEAD:P], d).then_inc(by_act[d], 1)
                for d in both:
                    ready(d, "MR")
                    wide(MTw, bank(d, "MR")[:, :, 0:HEAD], d).then_inc(by_act[d], 1)
                for d in both:
                    ready(d, "out")
                    nc.scalar.copy(o[:, d, :, DS(chunk(c, d), CHUNK)], bank(d, "out")[:, :, 0:HEAD]).then_inc(by_act[d], 1)
                for d in both:
                    act.wait_ge(by_dve[d], 1 + PER["v"] * c + PER["v"])
                    act.wait_ge(pe_done[d], NS * c + NS)
                    wide(Sw, S[:, d], d).then_inc(sw_done[d], 1)

        @block.vector
        def _(dve):
            for d in range(2):
                dve.sem_inc(sw_done[d], 1)
                dve.sem_inc(by_dve[d], 1)
            per_own = 2
            with dve.Fori(0, NCHUNK) as c:
                k = [0]

                def link(ins):
                    ins.then_inc(own, 1)
                    k[0] += 1
                    dve.wait_ge(own, per_own * c + k[0])

                def ready(d, name):
                    dve.wait_ge(pe_done[d], NS * c + AT[name] + 1)

                def bank(d, name):
                    return banks[:, d, AT[name] % 4]

                def spread(src):
                    return bcast(src, 2, 2)

                def mask(m, n=P):
                    m = consts(m)
                    if n == P:
                        return bcast(m, 1, PAIRS).rearrange("p a (b s) -> p a b s", b=2)
                    return bcast(m, 1, PAIRS)

                def wide(t, d):
                    return t[:, d].rearrange("p a (b s) -> p a b s", b=2)

                both = (0, 1)
                for d in both:
                    lt, l, inc = (("up", "low", "up_incl") if d == 0 else ("low", "up", "low_incl"))
                    ready(d, "LbT")
                    b = bank(d, "LbT")
                    nc.vector.tensor_tensor(wide(DT, d), spread(b[:, :, 0:HEAD]), mask(lt + "_near"), ALU.mult)
                    nc.vector.tensor_tensor(PbT[:, d], b[:, :, HEAD:P], mask(inc, HEAD), ALU.mult).then_inc(by_dve[d], 1)
                    ready(d, "LkT")
                    b = bank(d, "LkT")
                    nc.vector.tensor_tensor(wide(LkT, d), spread(b[:, :, 0:HEAD]), mask(lt + "_strict"), ALU.mult)
                    nc.vector.tensor_tensor(PkT[:, d], b[:, :, HEAD:P], mask(inc, HEAD), ALU.mult).then_inc(by_dve[d], 1)
                    dve.wait_ge(by_dve[d], 1 + PER["v"] * c + 1)
                    nc.vector.tensor_tensor(R1[:, d], DT[:, d], bcast(consts("ident"), 1, PAIRS), ALU.add)
                    ready(d, "Lb")
                    b = bank(d, "Lb")
                    nc.vector.tensor_tensor(wide(Dm, d), spread(b[:, :, 0:HEAD]), mask(l + "_near"), ALU.mult)
                    nc.vector.tensor_tensor(wide(E, d), spread(b[:, :, 0:HEAD]), mask(l + "_far"), ALU.mult)
                    nc.vector.tensor_copy(X[:, d, :, 0:HEAD], b[:, :, HEAD:P]).then_inc(by_dve[d], 1)

                for name, old, new in (("R2", R1, R2), ("R3", R2, R1), ("R4", R1, R2)):
                    for d in both:
                        ready(d, name)
                        nc.vector.tensor_tensor(new[:, d], bank(d, name), old[:, d], ALU.add).then_inc(by_dve[d], 1)
                for name, old, new in (("X2", X1, X2), ("Y", X2, Y)):
                    for d in both:
                        ready(d, name)
                        nc.vector.tensor_tensor(new[:, d], bank(d, name), old[:, d], ALU.add).then_inc(by_dve[d], 1)
                for d in both:
                    dve.wait_ge(by_act[d], 1 + PER["a"] * c + WIDE_M)
                    nc.vector.tensor_tensor(RT[:, d], bank(d, "MR")[:, :, HEAD:P],
                                            ar[:, d, 1, :, DS(chunk(c, d), CHUNK)], ALU.add).then_inc(by_dve[d], 1)
                for d in both:
                    ready(d, "S")
                    link(nc.vector.tensor_tensor(Sn[:, d], bank(d, "S")[:, :, 0:HEAD], S[:, d], ALU.add))
                    ends = bcast(w_end[:, d, DS(c if d == 0 else c * -1 + (NCHUNK - 1), 1), :].rearrange("p a b -> p (a b)"), 2, HEAD)
                    nc.vector.tensor_tensor(S[:, d], Sn[:, d], ends, ALU.mult).then_inc(by_dve[d], 1)
                assert k[0] == per_own


def pool_branch(nc, p, pool_w, inv_counts, scale, y_dram):
    pad = max(WINDOWS) // 2
    with ExitStack() as ctx:
        signal = Signals(nc, ctx)
        L = T + 2 * pad
        wide = ctx.enter_context(nc.sbuf_tensor("pool_in", [P, 4, L], F32))
        s = ctx.enter_context(nc.sbuf_tensor("pool_sums", [P, 2, L], F32))
        pooled = ctx.enter_context(nc.sbuf_tensor("pooled", [P, 4, T], F32))
        mixed = ctx.enter_context(nc.sbuf_tensor("pool_mixed", [P, 4, T], F32))
        w_sb = ctx.enter_context(nc.sbuf_tensor("pool_w_sb", [P, 4, P], F32))
        ic = ctx.enter_context(nc.sbuf_tensor("inv_counts_sb", [P, 4, T], F32))
        out = ctx.enter_context(nc.psum_tensor("pool_out", [P, 4, T], F32))
        got = signal("pool_constants")
        padded = signal("pool_padded")
        pooled_s = signal("pool_pooled")
        mixed_s = signal("pool_products")
        scaled = signal("pool_scaled")
        stored = signal("pool_stored")
        own = signal("pool_own")
        block = ctx.enter_context(nc.Block())

        @block.sync
        def _(sp):
            sp.dma_start(w_sb[:, :, :], pool_w.rearrange("p (g n) -> p g n", g=4)).then_inc(got, 16)
            sp.dma_start(ic[:, :, :], inv_counts.rearrange("p (g n) -> p g n", g=4)).then_inc(got, 16)
            sp.wait_ge(scaled, 4)
            sp.dma_start(y_dram, mixed[:, :, :].rearrange("p g t -> p (g t)")).then_inc(stored, 16)
            sp.wait_ge(stored, 16)

        @block.scalar
        def _(act):
            act.wait_ge(own, 1)
            nc.scalar.copy(wide[:, :, pad:pad + T], p[:, B_POOL:B_POOL + 4, 1:T + 1]).then_inc(padded, 1)
            for g in range(4):
                act.wait_ge(mixed_s, g + 1)
                nc.scalar.activation(mixed[:, g], out[:, g], ACT.Copy, scale=scale[:, g:g + 1]).then_inc(scaled, 1)

        @block.vector
        def _(dve):
            o = Own(dve, own)
            o.add(nc.vector.memset(wide[:, :, :], 0.0))
            dve.wait_ge(padded, 1)
            dve.wait_ge(got, 32)
            for g, window in enumerate(WINDOWS):
                src, n, step, j = wide[:, g], L, 1, 0
                while step < window:
                    n -= step
                    dst = s[:, j]
                    o.link(nc.vector.tensor_tensor(dst[:, 0:n], src[:, 0:n], src[:, step:step + n], ALU.add))
                    src, j, step = dst, 1 - j, 2 * step
                first = pad - window // 2
                o.link(nc.vector.tensor_tensor(pooled[:, g], src[:, first:first + T], ic[:, g], ALU.mult))
                nc.vector.tensor_tensor(pooled[:, g], pooled[:, g], wide[:, g, pad:pad + T], ALU.subtract).then_inc(pooled_s, 1)

        @block.tensor
        def _(pe):
            pe.wait_ge(got, 32)
            for g in range(4):
                pe.wait_ge(pooled_s, g + 1)
                nc.tensor.matmul(out[:, g], w_sb[:, g], pooled[:, g], start=True, stop=True).then_inc(mixed_s, 1)


def gate_and_bonus(nc, q, kd_sum, g_up, r_k, consts, v, gate_dram, bonus_dram):
    with ExitStack() as ctx:
        signal = Signals(nc, ctx)
        up = ctx.enter_context(nc.sbuf_tensor("g_up_sb", [P, 2, PAIRS * P], F32))
        gate = ctx.enter_context(nc.sbuf_tensor("gate_sb", [P, PAIRS, T], F32))
        rk = ctx.enter_context(nc.sbuf_tensor("rk", [P, PAIRS, T], F32))
        out = ctx.enter_context(nc.psum_tensor("gb_out", [P, 2, PAIRS, T], F32))
        got = signal("g_up_in")
        sig = signal("gate_sigmoids")
        gates = signal("gate_products")
        sums = signal("bonus_sums")
        made = signal("gates_made")
        rks = signal("bonus_terms")
        bonuses = signal("bonuses_made")
        stored = signal("gate_bonus_stored")
        own = signal("gb_own")
        block = ctx.enter_context(nc.Block())

        @block.sync
        def _(sp):
            sp.dma_start(up[:, :, :], g_up.rearrange("p (a n) -> p a n", a=2)).then_inc(got, 16)
            sp.wait_ge(made, PAIRS)
            sp.dma_start(gate_dram, gate[:, :, :].rearrange("p a t -> p (a t)")).then_inc(stored, 16)
            sp.wait_ge(bonuses, PAIRS)
            sp.dma_start(bonus_dram, rk[:, :, :].rearrange("p a t -> p (a t)")).then_inc(stored, 16)
            sp.wait_ge(stored, 32)

        @block.scalar
        def _(act):
            nc.scalar.activation(q[:, B_GD:B_GD + 2], q[:, B_GD:B_GD + 2], ACT.Sigmoid).then_inc(sig, 1)
            nc.scalar.copy(v[:, :, :], q[:, B_V:B_V + PAIRS])
            for p in range(PAIRS):
                act.wait_ge(gates, p + 1)
                nc.scalar.copy(gate[:, p], out[:, 0, p]).then_inc(made, 1)

        @block.tensor
        def _(pe):
            pe.wait_ge(got, 16)
            pe.wait_ge(sig, 1)
            for p in range(PAIRS):
                cols = slice(p * P, (p + 1) * P)
                nc.tensor.matmul(out[:, 0, p], up[:, 0, cols], q[:, B_GD], start=True, stop=False)
                nc.tensor.matmul(out[:, 0, p], up[0:GATE_REST, 1, cols], q[0:GATE_REST, B_GD + 1],
                                 start=False, stop=True).then_inc(gates, 1)
            for p in range(PAIRS):
                pe.wait_ge(rks, p + 1)
                nc.tensor.matmul(out[:, 1, p], consts("heads"), rk[:, p], start=True, stop=True).then_inc(sums, 1)

        @block.vector
        def _(dve):
            for p in range(PAIRS):
                nc.vector.scalar_tensor_tensor(out=rk[:, p], in0=q[:, B_R + p], scalar=r_k[:, p:p + 1], in1=kd_sum[:, p],
                                               op0=ALU.mult, op1=ALU.mult).then_inc(rks, 1)
            for p in range(PAIRS):
                dve.wait_ge(sums, p + 1)
                nc.vector.tensor_tensor(rk[:, p], out[:, 1, p], q[:, B_V + p], ALU.mult).then_inc(bonuses, 1)


def head_norm(nc, o, lnw, lnb, consts, saved, y):
    with ExitStack() as ctx:
        signal = Signals(nc, ctx)
        c = ctx.enter_context(nc.sbuf_tensor("centred", [P, PAIRS, T], F32))
        sq = ctx.enter_context(nc.sbuf_tensor("centred_sq", [P, PAIRS, T], F32))
        gate = ctx.enter_context(nc.sbuf_tensor("gate_again", [P, PAIRS, T], F32))
        bonus = ctx.enter_context(nc.sbuf_tensor("bonus_again", [P, PAIRS, T], F32))
        epst = ctx.enter_context(nc.sbuf_tensor("gn_eps", [P, 1], F32))
        out = ctx.enter_context(nc.psum_tensor("gn_out", [P, 2, PAIRS, T], F32))
        got = signal("saved_in")
        added = signal("directions_added")
        means = signal("head_means")
        squares = signal("head_squares")
        variances = signal("head_variances")
        roots = signal("head_roots")
        own = signal("gn_own")
        block = ctx.enter_context(nc.Block())

        @block.sync
        def _(sp):
            for dst, src in ((gate[:, :, :], saved[0]), (bonus[:, :, :], saved[1]), (y[:, PAIRS:2 * PAIRS], saved[2])):
                sp.dma_start(dst, src.rearrange("p (a t) -> p a t", a=PAIRS)).then_inc(got, 16)
            sp.wait_ge(got, 48)

        @block.tensor
        def _(pe):
            for p in range(PAIRS):
                pe.wait_ge(added, p + 1)
                nc.tensor.matmul(out[:, 0, p], consts("heads"), o[:, 0, p], start=True, stop=True).then_inc(means, 1)
            for p in range(PAIRS):
                pe.wait_ge(squares, p + 1)
                nc.tensor.matmul(out[:, 1, p], consts("heads"), sq[:, p], start=True, stop=True).then_inc(variances, 1)

        @block.scalar
        def _(act):
            act.wait_ge(own, 1)
            for p in range(PAIRS):
                act.wait_ge(variances, p + 1)
                nc.scalar.activation(sq[:, p], out[:, 1, p], ACT.Sqrt, bias=epst[:, 0:1], scale=1.0 / HEAD).then_inc(roots, 1)

        @block.vector
        def _(dve):
            k = Own(dve, own)
            k.add(nc.vector.memset(epst[:, :], GN_EPS))
            for p in range(PAIRS):
                nc.vector.tensor_tensor(o[:, 0, p], o[:, 0, p], o[:, 1, p], ALU.add).then_inc(added, 1)
            for p in range(PAIRS):
                dve.wait_ge(means, p + 1)
                k.link(nc.vector.scalar_tensor_tensor(out=c[:, p], in0=out[:, 0, p], scalar=-1.0 / HEAD, in1=o[:, 0, p],
                                                      op0=ALU.mult, op1=ALU.add))
                nc.vector.tensor_tensor(sq[:, p], c[:, p], c[:, p], ALU.mult).then_inc(squares, 1)
            dve.wait_ge(got, 48)
            for p in range(PAIRS):
                dve.wait_ge(roots, p + 1)
                k.link(nc.vector.reciprocal(o[:, 0, p], sq[:, p]))
                k.link(nc.vector.tensor_tensor(c[:, p], c[:, p], o[:, 0, p], ALU.mult))
                k.link(nc.vector.scalar_tensor_tensor(out=c[:, p], in0=c[:, p], scalar=lnw[:, p:p + 1], in1=bonus[:, p],
                                                      op0=ALU.mult, op1=ALU.add))
                nc.vector.scalar_tensor_tensor(out=y[:, p], in0=c[:, p], scalar=lnb[:, p:p + 1], in1=gate[:, p],
                                               op0=ALU.add, op1=ALU.mult)



def turn(nc, tag, pairs, ident, width=P):
    groups = len(pairs)
    with ExitStack() as ctx:
        signal = Signals(nc, ctx)
        out = ctx.enter_context(nc.psum_tensor(f"{tag}_turned", [P, 4, 4, P], F32))
        turned = signal(f"{tag}_turned_s")
        taken = [signal(f"{tag}_taken{e}") for e in range(2)]
        block = ctx.enter_context(nc.Block())

        @block.tensor
        def _(pe):
            for g, (srcs, _) in enumerate(pairs):
                if g >= 4:
                    pe.wait_ge(taken[g % 2], (g - 4) // 2 + 1)
                for j, s in enumerate(srcs):
                    mm = nc.tensor.transpose(out[:, g % 4, j, :], s, ident)
                mm.then_inc(turned, 1)

        def take(e):
            def body(eng):
                for g in range(e, groups, 2):
                    eng.wait_ge(turned, g + 1)
                    dst = pairs[g][1]
                    src = out[:, g % 4, :, 0:dst.shape[-1]]
                    (nc.scalar.copy if e else nc.vector.tensor_copy)(dst, src).then_inc(taken[e], 1)
            return body

        block.vector(take(0))
        block.scalar(take(1))


def hold(eng, sem, value, pace):
    eng.wait_ge(sem, value)
    eng.sem_inc(pace, 1)


def peer_route(nc, qT, keys, consts, idx, gate):
    with ExitStack() as ctx:
        signal = Signals(nc, ctx)
        def sb(name, *shape, dt=F32):
            return ctx.enter_context(nc.sbuf_tensor(name, [P, *shape], dt))

        kT = sb("keys_sb", 2 * PH, P)
        s = sb("key_scores", 2 * PH, N_KEYS)
        s2 = sb("key_scores2", 2 * PH, N_KEYS)
        val = sb("key_vals", PH, 2, TOPK)
        ix = sb("key_idx", PH, 2, TOPK, dt=U32)
        ixf = sb("key_idxf", PH, 2, TOPK)
        cand = sb("cand", PH, TOPK, TOPK)
        cand2 = sb("cand2", PH, TOPK, TOPK)
        sc = sb("cand_vals", PH, TOPK)
        pos = sb("cand_pos", PH, TOPK, dt=U32)
        part = sb("cand_part", 2, PH, TOPK, dt=U32)
        partf = sb("cand_partf", 2, PH, TOPK)
        hot = sb("hot", PH, TOPK, TOPK)
        hot2 = sb("hot2", PH, TOPK, TOPK)
        pick = sb("pick", 2, PH, TOPK)
        flat = sb("flat_idx", SLOTS)
        ssum = sb("gate_sum", PH)
        rsum = sb("gate_rsum", PH)
        e = sb("gate_e", PH, TOPK)
        out = ctx.enter_context(nc.psum_tensor("score_out", [P, 2, 2 * PH, N_KEYS], F32))
        got = signal("keys_in")
        scored = signal("scores_ready")
        copied = signal("scores_copied")
        routed = signal("tile_routed")
        shifted = signal("gate_shifted")
        exped = signal("gate_exped")
        own = signal("route_own")
        pace = signal("route_pace")
        block = ctx.enter_context(nc.Block())

        @block.sync
        def _(sp):
            sp.dma_start(kT[:, :, :], keys.rearrange("p (a n) -> p a n", n=P)).then_inc(got, 16)

        @block.tensor
        def _(pe):
            pe.wait_ge(got, 16)
            for t in range(TT):
                if t >= 2:
                    pe.wait_ge(copied, t - 1)
                for j in range(2 * PH):
                    mm = nc.tensor.matmul(out[:, t % 2, j], qT[:, j, t * P:(t + 1) * P], kT[:, j], start=True, stop=True)
                mm.then_inc(scored, 1)

        @block.scalar
        def _(act):
            for t in range(TT):
                act.wait_ge(scored, t + 1)
                act.wait_ge(routed, t + 1)
                for j in range(0, 2 * PH, 4):
                    ins = nc.scalar.copy(s[:, j:j + 4], out[:, t % 2, j:j + 4])
                ins.then_inc(copied, 1)
                act.wait_ge(shifted, t + 1)
                nc.scalar.activation(e[:, :, :], e[:, :, :], ACT.Exp).then_inc(exped, 1)

        @block.vector
        def _(dve):
            dve.sem_inc(routed, 1)
            per = 20
            with dve.Fori(0, TT) as t:
                n = [0]

                def step(ins):
                    ins.then_inc(own, 1)
                    n[0] += 1
                    hold(dve, own, per * t + n[0], pace)

                hold(dve, copied, t + 1, pace)
                a = nc.vector
                lists = [(h, p) for h in range(PH) for p in range(2)]
                for h, p in lists:
                    ins = a.max(val[:, h, p, 0:8], s[:, 2 * h + p])
                step(ins)
                for h, p in lists:
                    a.max_index(ix[:, h, p, 0:8], val[:, h, p, 0:8], s[:, 2 * h + p])
                    ins = a.match_replace(s2[:, 2 * h + p], val[:, h, p, 0:8], s[:, 2 * h + p], GONE)
                step(ins)
                for h, p in lists:
                    ins = a.max(val[:, h, p, 8:16], s2[:, 2 * h + p])
                step(ins)
                for h, p in lists:
                    ins = a.max_index(ix[:, h, p, 8:16], val[:, h, p, 8:16], s2[:, 2 * h + p])
                step(ins)
                a.tensor_copy(ixf[:, :, :, :], ix[:, :, :, :])
                step(a.tensor_tensor(cand[:, :, :, :], bcast(val[:, :, 0, :], 3, TOPK), bcast(val[:, :, 1, :], 2, TOPK), ALU.add))

                def row(x, h):
                    return x[:, h].rearrange("p a b -> p (a b)")

                for h in range(PH):
                    ins = a.max(sc[:, h, 0:8], row(cand, h))
                step(ins)
                for h in range(PH):
                    a.max_index(pos[:, h, 0:8], sc[:, h, 0:8], row(cand, h))
                    ins = a.match_replace(row(cand2, h), sc[:, h, 0:8], row(cand, h), GONE)
                step(ins)
                for h in range(PH):
                    ins = a.max(sc[:, h, 8:16], row(cand2, h))
                step(ins)
                for h in range(PH):
                    ins = a.max_index(pos[:, h, 8:16], sc[:, h, 8:16], row(cand2, h))
                step(ins)
                ins = a.tensor_tensor(e[:, :, :], sc[:, :, :], bcast(sc[:, :, 0], 2, TOPK), ALU.subtract)
                ins.then_inc(shifted, 1)
                a.tensor_scalar(part[:, 0], pos[:, :, :], 4, None, ALU.logical_shift_right)
                step(a.tensor_scalar(part[:, 1], pos[:, :, :], 15, None, ALU.bitwise_and))
                step(a.tensor_copy(partf[:, :, :, :], part[:, :, :, :]))
                slot = bcast(bcast(consts("slot"), 1, TOPK), 1, PH)
                for p, h_ in ((0, hot), (1, hot2)):
                    ins = a.tensor_tensor(h_[:, :, :, :], bcast(partf[:, p], 3, TOPK), slot, ALU.is_equal)
                step(ins)
                for p, h_ in ((0, hot), (1, hot2)):
                    ins = a.tensor_tensor(h_[:, :, :, :], h_[:, :, :, :], bcast(ixf[:, :, p, :], 2, TOPK), ALU.mult)
                step(ins)
                for p, h_ in ((0, hot), (1, hot2)):
                    ins = a.tensor_reduce(pick[:, p], h_[:, :, :, :], AX.X, ALU.add)
                step(ins)
                step(a.scalar_tensor_tensor(out=flat[:, :], in0=pick[:, 0].rearrange("p a b -> p (a b)"), scalar=float(N_KEYS),
                                            in1=pick[:, 1].rearrange("p a b -> p (a b)"), op0=ALU.mult, op1=ALU.add))
                a.tensor_copy(idx[:, DS(t, 1), :].rearrange("p a s -> p (a s)"), flat[:, :])
                hold(dve, exped, t + 1, pace)
                step(a.tensor_reduce(ssum[:, :], e[:, :, :], AX.X, ALU.add))
                step(a.reciprocal(rsum[:, :], ssum[:, :]))
                ins = a.tensor_tensor(gate[:, DS(t, 1), :].rearrange("p a (h k) -> p (a h) k", k=TOPK), e[:, :, :],
                                      bcast(rsum[:, :], 2, TOPK), ALU.mult)
                ins.then_inc(routed, 1)
                assert n[0] <= per, n
                while n[0] < per:
                    dve.sem_inc(own, 1)
                    n[0] += 1


GROUP = 4


def peer_experts(nc, h_tok, idx, gate, u_tab, v_tab, acc):
    with ExitStack() as ctx:
        signal = Signals(nc, ctx)
        u = ctx.enter_context(nc.sbuf_tensor("u_rows", [P, 2, GROUP, D], F32))
        v = ctx.enter_context(nc.sbuf_tensor("v_rows", [P, 2, GROUP, D], F32))
        ids = ctx.enter_context(nc.sbuf_tensor("expert_ids", [P, 2, GROUP], U32))
        dot = ctx.enter_context(nc.sbuf_tensor("expert_dots", [P, 2, GROUP], F32))
        part = ctx.enter_context(nc.sbuf_tensor("expert_parts", [P, 2, D], F32))
        u_in = [signal(f"u_rows_in{b}") for b in range(2)]
        v_in = [signal(f"v_rows_in{b}") for b in range(2)]
        dots = signal("dots_ready")
        gelus = signal("gelus_ready")
        weights = signal("weights_ready")
        adds = signal("expert_adds")
        copied = signal("ids_copied")
        own = signal("experts_own")
        pace = signal("experts_pace")
        rounds = SLOTS // (2 * GROUP)
        DOTS0, ADDS0 = 2, 2 * GROUP
        block = ctx.enter_context(nc.Block())

        @block.gpsimd
        def _(pool):
            with pool.Fori(0, TT * rounds) as r:
                for b in range(2):
                    g = 2 * r + b
                    hold(pool, dots, g - 1 + DOTS0, pace)
                    hold(pool, adds, g * GROUP + (ADDS0 - GROUP), pace)
                    nc.gpsimd.tensor_copy(ids[:, b], idx.rearrange("p t s -> p (t s)")[:, DS(g * GROUP, GROUP)]).then_inc(copied, 1)
                    hold(pool, copied, g + 1, pace)
                    for tab, rows, sem in ((u_tab, u, u_in), (v_tab, v, v_in)):
                        for j in range(GROUP):
                            nc.gpsimd.indirect_dma_start(
                                out=rows[:, b, j], out_offset=None, in_=tab,
                                in_offset=bass.IndirectOffsetOnAxis(ap=ids[:, b, j:j + 1], axis=0)).then_inc(sem[b], 16)

        @block.scalar
        def _(act):
            with act.Fori(0, TT * rounds) as r:
                for b in range(2):
                    act.wait_ge(dots, 2 * r + b + 1 + DOTS0)
                    nc.scalar.activation(dot[:, b], dot[:, b], ACT.Gelu).then_inc(gelus, 1)

        @block.vector
        def _(dve):
            dve.sem_inc(dots, DOTS0)
            dve.sem_inc(adds, ADDS0)
            for t in range(TT):
                nc.vector.memset(part[:, :, :], 0.0).then_inc(own, 1)
                dve.wait_ge(own, 2 * t + 1)
                with dve.Fori(0, rounds) as i:
                    for b in range(2):
                        dve.wait_ge(u_in[b], i * (16 * GROUP) + 16 * GROUP * (rounds * t + 1))
                        for j in range(GROUP):
                            ins = nc.vector.tensor_tensor_reduce(out=u[:, b, j], in0=u[:, b, j], in1=h_tok[:, t], scale=1.0,
                                                                 scalar=0.0, op0=ALU.mult, op1=ALU.add,
                                                                 accum_out=dot[:, b, j:j + 1])
                        ins.then_inc(dots, 1)
                    for b in range(2):
                        g = 2 * i + (b + 2 * rounds * t)
                        dve.wait_ge(gelus, g + 1)
                        nc.vector.tensor_tensor(dot[:, b], dot[:, b],
                                                gate.rearrange("p t s -> p (t s)")[:, DS(g * GROUP, GROUP)],
                                                ALU.mult).then_inc(weights, 1)
                        dve.wait_ge(v_in[b], i * (16 * GROUP) + 16 * GROUP * (rounds * t + 1))
                        dve.wait_ge(weights, g + 1)
                        for j in range(GROUP):
                            dve.wait_ge(adds, g * GROUP + j + ADDS0 - 1)
                            nc.vector.scalar_tensor_tensor(out=part[:, j % 2], in0=v[:, b, j], scalar=dot[:, b, j:j + 1],
                                                           in1=part[:, j % 2], op0=ALU.mult, op1=ALU.add).then_inc(adds, 1)
                dve.wait_ge(adds, (t + 1) * SLOTS + ADDS0)
                nc.vector.tensor_tensor(acc[:, t], part[:, 0], part[:, 1], ALU.add).then_inc(own, 1)
                dve.wait_ge(own, 2 * t + 2)


def add_turned(nc, tag, x, tok, ident):
    with ExitStack() as ctx:
        signal = Signals(nc, ctx)
        out = ctx.enter_context(nc.psum_tensor(f"{tag}_back", [P, 4, T], F32))
        turned = signal(f"{tag}_back_turned")
        added = signal(f"{tag}_back_added")
        block = ctx.enter_context(nc.Block())

        @block.tensor
        def _(pe):
            for k in range(KD):
                if k >= 4:
                    pe.wait_ge(added, k - 3)
                for t in range(TT):
                    mm = nc.tensor.transpose(out[:, k % 4, t * P:(t + 1) * P], tok[:, t, k * P:(k + 1) * P], ident)
                mm.then_inc(turned, 1)

        @block.vector
        def _(dve):
            for k in range(KD):
                dve.wait_ge(turned, k + 1)
                nc.vector.tensor_tensor(x[:, k], out[:, k % 4], x[:, k], ALU.add).then_inc(added, 1)



def rope(nc, pr, swap, tables):
    with ExitStack() as ctx:
        signal = Signals(nc, ctx)
        tab = ctx.enter_context(nc.sbuf_tensor("rope_tab", [P, 2, T], F32))
        tmp = ctx.enter_context(nc.sbuf_tensor("rope_tmp", [P, 2, T], F32))
        out = ctx.enter_context(nc.psum_tensor("rope_out", [P, 2, T], F32))
        got = signal("rope_in")
        swapped = signal("rope_swapped")
        free = signal("rope_free")
        own = signal("rope_own")
        rounds = 5
        first = (C_QB, C_QI)
        block = ctx.enter_context(nc.Block())

        def blk(b, i):
            return pr[:, DS(i + first[b], 1), :].rearrange("p a t -> p (a t)")

        @block.sync
        def _(sp):
            sp.dma_start(tab[:, :, :], tables.rearrange("p (a t) -> p a t", a=2)).then_inc(got, 16)

        @block.tensor
        def _(pe):
            with pe.Fori(0, rounds) as i:
                for b in range(2):
                    pe.wait_ge(free, 2 * i + b + 1)
                    nc.tensor.matmul(out[:, b], swap, blk(b, i), start=True, stop=True).then_inc(swapped, 1)

        @block.vector
        def _(dve):
            dve.sem_inc(free, 2)
            dve.wait_ge(got, 16)
            with dve.Fori(0, rounds) as i:
                for b in range(2):
                    dve.wait_ge(swapped, 2 * i + b + 1)
                    nc.vector.tensor_tensor(tmp[:, b], out[:, b], tab[:, 1], ALU.mult).then_inc(free, 1)
                    nc.vector.tensor_tensor(blk(b, i), blk(b, i), tab[:, 0], ALU.mult).then_inc(own, 1)
                for b in range(2):
                    dve.wait_ge(own, 4 * i + 2)
                    nc.vector.tensor_tensor(blk(b, i), blk(b, i), tmp[:, b], ALU.add).then_inc(own, 1)
                dve.wait_ge(own, 4 * i + 4)


def index_mask(nc, pr, w_tok, m):
    with ExitStack() as ctx:
        signal = Signals(nc, ctx)
        score = ctx.enter_context(nc.sbuf_tensor("index_scores", [P, 3, T], F32))
        relu = ctx.enter_context(nc.sbuf_tensor("index_relu", [P, 4, T], F32))
        ws = ctx.enter_context(nc.sbuf_tensor("index_w", [P, TT, 8], F32))
        top = ctx.enter_context(nc.sbuf_tensor("index_top", [P, 3, 8], F32))
        out = ctx.enter_context(nc.psum_tensor("index_out", [P, 4, T], F32))
        dots = signal("index_dots")
        relus = signal("index_relus")
        added = signal("index_added")
        own = signal("index_own")
        pace = signal("index_pace")
        units = [(t, h) for h in range(8) for t in range(1, TT)]
        block = ctx.enter_context(nc.Block())

        @block.tensor
        def _(pe):
            for n, (t, h) in enumerate(units):
                if n >= 4:
                    pe.wait_ge(relus, n - 3)
                rows = slice(HEAD * (h % 2), HEAD * (h % 2) + HEAD)
                keys = P * (t + 1)
                nc.tensor.matmul(out[:, n % 4, 0:keys], pr[rows, C_QI + h // 2, t * P:(t + 1) * P], pr[rows, C_KI, 0:keys],
                                 start=True, stop=True).then_inc(dots, 1)

        @block.scalar
        def _(act):
            for n, (t, h) in enumerate(units):
                act.wait_ge(dots, n + 1)
                if n >= 4:
                    act.wait_ge(added, n - 3)
                keys = P * (t + 1)
                nc.scalar.activation(relu[:, n % 4, 0:keys], out[:, n % 4, 0:keys], ACT.Relu, scale=HEAD ** -0.5).then_inc(relus, 1)

        @block.vector
        def _(dve):
            a = nc.vector
            k = Own(dve, own)
            a.memset(score[:, :, :], 0.0)
            a.memset(m[:, :, :], 0.0)
            k.link(a.tensor_scalar(ws[:, :, :], w_tok[:, :, 0:8], 8 ** -0.5, None, ALU.mult))
            a.memset(m[0:HEAD, 0, HEAD:P], NEG)
            for n, (t, h) in enumerate(units):
                keys = P * (t + 1)
                dve.wait_ge(relus, n + 1)
                if n >= 3:
                    dve.wait_ge(added, n - 2)
                a.scalar_tensor_tensor(out=score[:, t - 1, 0:keys], in0=relu[:, n % 4, 0:keys], scalar=ws[:, t, h:h + 1],
                                       in1=score[:, t - 1, 0:keys], op0=ALU.mult, op1=ALU.add).then_inc(added, 1)
            dve.wait_ge(added, len(units))
            for t in range(1, TT):
                ins = a.memset(score[0:HEAD, t - 1, P * (t + 1) - HEAD:P * (t + 1)], NEG)
            k.link(ins)
            base = k.n
            with dve.Fori(0, IDX_TOPK // 8) as i:
                for t in range(1, TT):
                    ins = a.max(top[:, t - 1], score[:, t - 1, 0:P * (t + 1)])
                ins.then_inc(own, 1)
                hold(dve, own, 2 * i + base + 1, pace)
                for t in range(1, TT):
                    s = score[:, t - 1, 0:P * (t + 1)]
                    ins = a.match_replace(s, top[:, t - 1], s, GONE)
                ins.then_inc(own, 1)
                hold(dve, own, 2 * i + base + 2, pace)
            k.n += 2 * (IDX_TOPK // 8)
            for t in range(1, TT):
                s = score[:, t - 1, 0:P * (t + 1)]
                ins = a.tensor_scalar(s, s, GONE, -1.0, ALU.is_equal, ALU.add)
            k.link(ins)
            for t in range(1, TT):
                s = score[:, t - 1, 0:P * (t + 1)]
                a.tensor_scalar(m[:, t, 0:P * (t + 1)], s, -NEG, None, ALU.mult)


def attention(nc, tag, q_of, k_of, v_of, bias_of, ident, o):
    SB, PB = 4, 4
    with ExitStack() as ctx:
        signal = Signals(nc, ctx)
        qs = ctx.enter_context(nc.sbuf_tensor(f"{tag}_q", [P, T], F32))
        ks = ctx.enter_context(nc.sbuf_tensor(f"{tag}_k", [P, T], F32))
        vs = ctx.enter_context(nc.sbuf_tensor(f"{tag}_v", [P, TT, P], F32))
        prob = ctx.enter_context(nc.sbuf_tensor(f"{tag}_p", [P, SB, T], F32))
        pT = ctx.enter_context(nc.sbuf_tensor(f"{tag}_pT", [P, 2, T], F32))
        mx = ctx.enter_context(nc.sbuf_tensor(f"{tag}_mx", [P, SB], F32))
        nm = ctx.enter_context(nc.sbuf_tensor(f"{tag}_nm", [P, SB], F32))
        sm = ctx.enter_context(nc.sbuf_tensor(f"{tag}_sm", [P, SB], F32))
        rc = ctx.enter_context(nc.sbuf_tensor(f"{tag}_rc", [P, SB], F32))
        s_ps = ctx.enter_context(nc.psum_tensor(f"{tag}_s_ps", [P, PB, T], F32))
        t_ps = ctx.enter_context(nc.psum_tensor(f"{tag}_t_ps", [P, 2, T], F32))
        o_ps = ctx.enter_context(nc.psum_tensor(f"{tag}_o_ps", [P, T], F32))

        def sem(name):
            return signal(f"{tag}_{name}")

        qk_in, v_in, scored, biased, shifted, exped, normed = map(
            sem, ("qk_in", "v_in", "scored", "biased", "shifted", "exped", "normed"))
        turned, taken, summed, stored, own, pace = map(sem, ("turned", "taken", "summed", "stored", "own", "pace"))
        units = [(hh, t) for hh in range(2) for t in range(TT)]
        NU = len(units)
        block = ctx.enter_context(nc.Block())

        @block.gpsimd
        def _(pool):
            def load(i, after=None):
                if after is not None:
                    pool.wait_ge(scored, NU * after + NU)
                nc.gpsimd.tensor_copy(qs[:, :], q_of(i))
                nc.gpsimd.tensor_copy(ks[:, :], k_of(i)).then_inc(qk_in, 1)
                if after is not None:
                    hold(pool, summed, NU * after + NU + 2, pace)
                nc.gpsimd.tensor_copy(vs[:, :, :], v_of(i)).then_inc(v_in, 1)

            load(0)
            with pool.Fori(0, PAIRS - 1) as i:
                load(i + 1, i)

        @block.tensor
        def _(pe):
            pe.sem_inc(turned, SB)
            pe.sem_inc(summed, 2)
            with pe.Fori(0, PAIRS) as i:
                pe.wait_ge(qk_in, i + 1)
                for step in range(NU + 3):
                    if step < NU:
                        u = step
                        hh, t = units[u]
                        rows = slice(HEAD * hh, HEAD * hh + HEAD)
                        keys = P * (t + 1)
                        pe.wait_ge(biased, NU * i + u + 1)
                        nc.tensor.matmul(s_ps[:, u % PB, 0:keys],
                                         qs[rows, t * P:(t + 1) * P], ks[rows, 0:keys],
                                         start=True, stop=True).then_inc(scored, 1)
                    if 2 <= step < NU + 2:
                        u = step - 2
                        hh, t = units[u]
                        pe.wait_ge(normed, NU * i + u + 1)
                        pe.wait_ge(taken, NU * i + u + 1)
                        for j in range(t + 1):
                            mm = nc.tensor.transpose(t_ps[:, u % 2, j * P:(j + 1) * P], prob[:, u % SB, j * P:(j + 1) * P], ident)
                        mm.then_inc(turned, 1)
                    if 3 <= step:
                        u = step - 3
                        hh, t = units[u]
                        rows = slice(HEAD * hh, HEAD * hh + HEAD)
                        if u == 0:
                            pe.wait_ge(v_in, i + 1)
                            pe.wait_ge(stored, i + 1)
                        pe.wait_ge(taken, NU * i + u + 3)
                        for j in range(t + 1):
                            mm = nc.tensor.matmul(o_ps[rows, t * P:(t + 1) * P], vs[:, j, rows], pT[:, u % 2, j * P:(j + 1) * P],
                                                  start=(j == 0), stop=(j == t))
                        mm.then_inc(summed, 1)

        @block.scalar
        def _(act):
            act.sem_inc(taken, 2)
            act.sem_inc(stored, 1)
            with act.Fori(0, PAIRS) as i:
                for step in range(NU + 2):
                    if step < NU:
                        u = step
                        hh, t = units[u]
                        keys = P * (t + 1)
                        act.wait_ge(shifted, NU * i + u + 1)
                        nc.scalar.activation(prob[:, u % SB, 0:keys], prob[:, u % SB, 0:keys], ACT.Exp,
                                             bias=nm[:, u % SB:u % SB + 1], accum_out=sm[:, u % SB:u % SB + 1]).then_inc(exped, 1)
                    if 2 <= step:
                        u = step - 2
                        hh, t = units[u]
                        keys = P * (t + 1)
                        act.wait_ge(turned, NU * i + u + SB + 1)
                        act.wait_ge(summed, NU * i + u + 1)
                        nc.scalar.copy(pT[:, u % 2, 0:keys], t_ps[:, u % 2, 0:keys]).then_inc(taken, 1)
                act.wait_ge(summed, NU * i + NU + 2)
                nc.scalar.copy(o[:, DS(i, 1), :].rearrange("p a t -> p (a t)"), o_ps[:, :]).then_inc(stored, 1)

        @block.vector
        def _(dve):
            dve.sem_inc(biased, PB)
            per = 2 * NU
            with dve.Fori(0, PAIRS) as i:
                n = 0
                for step in range(NU + 1):
                    if step < NU:
                        u = step
                        hh, t = units[u]
                        keys = P * (t + 1)
                        c = slice(u % SB, u % SB + 1)
                        dve.wait_ge(scored, NU * i + u + 1)
                        dve.wait_ge(turned, NU * i + u + 1)
                        nc.vector.scalar_tensor_tensor(out=prob[:, u % SB, 0:keys], in0=s_ps[:, u % PB, 0:keys],
                                                       scalar=HEAD ** -0.5, in1=bias_of(i, hh, t), op0=ALU.mult,
                                                       op1=ALU.add).then_inc(biased, 1)
                        dve.wait_ge(biased, NU * i + u + 1 + PB)
                        nc.vector.tensor_reduce(mx[:, c], prob[:, u % SB, 0:keys], AX.X, ALU.max).then_inc(own, 1)
                        n += 1
                        dve.wait_ge(own, per * i + n)
                        nc.vector.tensor_scalar(nm[:, c], mx[:, c], -1.0, None, ALU.mult).then_inc(shifted, 1)
                    if 1 <= step:
                        u = step - 1
                        hh, t = units[u]
                        keys = P * (t + 1)
                        c = slice(u % SB, u % SB + 1)
                        dve.wait_ge(exped, NU * i + u + 1)
                        nc.vector.reciprocal(rc[:, c], sm[:, c]).then_inc(own, 1)
                        n += 1
                        dve.wait_ge(own, per * i + n)
                        nc.vector.tensor_scalar(prob[:, u % SB, 0:keys], prob[:, u % SB, 0:keys], rc[:, c], None,
                                                ALU.mult).then_inc(normed, 1)
                assert n == per


def merge_into(m, pr):
    def evacuate(nc, block, signal, out, done, free, own, rounds, ring):
        gates = signal("merge_gates")

        def gate(first, n):
            return pr[:, DS(n + first, 1), :].rearrange("p a t -> p (a t)")

        @block.scalar
        def _(act):
            act.sem_inc(free, ring)
            with act.Fori(0, rounds) as i:
                for b in range(ring // 2):
                    nc.scalar.activation(gate(C_GA, 2 * i + b), gate(C_GA, 2 * i + b), ACT.Sigmoid)
                    nc.scalar.activation(gate(C_GB, 2 * i + b), gate(C_GB, 2 * i + b), ACT.Sigmoid).then_inc(gates, 1)

        @block.vector
        def _(dve):
            with dve.Fori(0, rounds) as i:
                for b in range(ring // 2):
                    n = 2 * i + b
                    dve.wait_ge(gates, n + 1)
                    dve.wait_ge(done, ring * i + 2 * b + 2)
                    nc.vector.tensor_tensor(gate(C_GA, n), out[:, 2 * b], gate(C_GA, n), ALU.mult)
                    nc.vector.tensor_tensor(gate(C_GB, n), out[:, 2 * b + 1], gate(C_GB, n), ALU.mult).then_inc(free, 2)
                    dve.wait_ge(free, ring * i + ring + 2 * b + 2)
                    nc.vector.tensor_tensor(m[:, DS(n, 1), :].rearrange("p a t -> p (a t)"), gate(C_GA, n), gate(C_GB, n), ALU.add)
    return evacuate



def load(nc, tag, *copies):
    with ExitStack() as ctx:
        signal = Signals(nc, ctx)
        got = signal(f"{tag}_loaded")
        block = ctx.enter_context(nc.Block())

        @block.sync
        def _(sp):
            for dst, src in copies:
                sp.dma_start(dst, src).then_inc(got, 16)
            sp.wait_ge(got, 16 * len(copies))


def swiglu_ffn(nc, tag, x, weight, consts, w_in, w_out):
    with (nc.sbuf_tensor(f"{tag}_h", [P, KD, T], F32) as h, nc.sbuf_tensor(f"{tag}_a", [P, KF, T], F32) as a,
          nc.sbuf_tensor(f"{tag}_silu", [P, 2, T], F32) as silu):
        rmsnorm(nc, f"{tag}_norm", x, weight, consts("ones"), RMS_EPS2, h)
        gemm(nc, f"{tag}_in", w_in, KD, lambda b: h, 2 * KF, swiglu_into(a, silu))
        gemm(nc, f"{tag}_out", w_out, KF, lambda b: a, KD, add_to(x, 0.5))


def token_groups(src, blocks, dst):
    n = dst.shape[-1]
    return [([src[:, b, t * P:(t + 1) * P] for t in range(TT)], dst[:, :, j * P:min(n, (j + 1) * P)])
            for j, b in enumerate(blocks)]


def build(nc, io):
    out = io["out"]
    gate_dram = nc.dram_tensor("gate_kept", [P, PAIRS * T], F32).ap()
    bonus_dram = nc.dram_tensor("bonus_kept", [P, PAIRS * T], F32).ap()
    pool_dram = nc.dram_tensor("pool_kept", [P, PAIRS * T], F32).ap()
    x_in = io["x"].rearrange("p (k t) -> p k t", k=KD)

    with ExitStack() as whole:
        const_sb = whole.enter_context(nc.sbuf_tensor("const_sb", [P, N_CONST], F32))
        vec_sb = whole.enter_context(nc.sbuf_tensor("vec_sb", [P, N_VEC], F32))

        def consts(name):
            at, n = C_AT[name]
            return const_sb[:, at:at + n]

        def vec(name):
            at, n = V_AT[name]
            return vec_sb[:, at:at + n]

        y_o = ExitStack()
        with y_o:
            with ExitStack() as s1:
                o = y_o.enter_context(nc.sbuf_tensor("o", [P, 2, PAIRS, T], F32))
                ar = s1.enter_context(nc.sbuf_tensor("ar", [P, 2, 2, PAIRS, T], F32))
                bk = s1.enter_context(nc.sbuf_tensor("bk", [P, 2, 2, PAIRS, T], F32))
                v = s1.enter_context(nc.sbuf_tensor("v_kept", [P, PAIRS, T], F32))
                w_end = s1.enter_context(nc.sbuf_tensor("w_end", [P, 2, NCHUNK, PAIRS], F32))
                with nc.sbuf_tensor("q", [P, N_SHIFT, T], F32) as q:
                    x = bk[:, :, :, :, :].rearrange("p a b c t -> p (a b c) t")[:, 0:KD]
                    h = ar[:, :, :, :, :].rearrange("p a b c t -> p (a b c) t")[:, 0:KD]
                    load(nc, "start", (const_sb[:, :], io["consts"]), (vec_sb[:, :], io["vec"]), (x, x_in))
                    with nc.sbuf_tensor("p_in", [P, N_IN1, T + 2], F32) as p:
                        rmsnorm(nc, "norm1", x, vec("norm1"), consts("ones"), RMS_EPS1, h)
                        gemm(nc, "w_in", io["w_in"], KD, lambda b: h, N_IN1,
                             keep_plain(lambda n: p[:, DS(n, 1), 1:T + 1].rearrange("p a t -> p (a t)")))
                        token_shift(nc, p, q, vec("mu0"), vec("mu1"))
                        pool_branch(nc, p, io["pool_w"], io["inv_counts"], vec("pool_scale"), pool_dram)
                    with (nc.sbuf_tensor("kd_sum", [P, PAIRS, T], F32) as kd_sum,):
                        with (nc.sbuf_tensor("kk", [P, PAIRS, T], F32) as kk, nc.sbuf_tensor("lora", [P, 2, PAIRS * P], F32) as lora):
                            load(nc, "lora", (lora[:, :, :], io["lora"].rearrange("p (a n) -> p a n", a=2)))
                            rwkv_operands(nc, q, lora, vec, consts, ar, bk, kk, kd_sum, w_end)
                        gate_and_bonus(nc, q, kd_sum, io["g_up"], vec("r_k"), consts, v, gate_dram, bonus_dram)
                recurrence(nc, ar, bk, v, w_end, consts, o)
            y = y_o.enter_context(nc.sbuf_tensor("y", [P, 2 * PAIRS, T], F32))
            x = y_o.enter_context(nc.sbuf_tensor("x_mix", [P, KD, T], F32))
            head_norm(nc, o, vec("lnw"), vec("lnb"), consts, (gate_dram, bonus_dram, pool_dram), y)
            load(nc, "x_again", (x[:, :, :], x_in))
            gemm(nc, "w_out", io["w_out"], KD, lambda b: y, KD, add_to(x))
            x_dram = nc.dram_tensor("x_kept", [P, KD * T], F32).ap()
            load(nc, "x_store", (x_dram, x[:, :, :].rearrange("p k t -> p (k t)")))

        x = whole.enter_context(nc.sbuf_tensor("x", [P, KD, T], F32))
        load(nc, "x_back", (x[:, :, :], x_dram.rearrange("p (k t) -> p k t", k=KD)))
        with ExitStack() as s2:
            def sb(name, shape, dt=F32):
                return s2.enter_context(nc.sbuf_tensor(name, shape, dt))

            idx = sb("expert_idx", [P, TT, SLOTS], U32)
            gate = sb("expert_gate", [P, TT, SLOTS])
            h_tok = sb("h_tok", [P, TT, D])
            acc = sb("peer_acc", [P, TT, D])
            with nc.sbuf_tensor("h2", [P, KD, T], F32) as h2, nc.sbuf_tensor("qT", [P, 2 * PH, T], F32) as qT:
                rmsnorm(nc, "norm2", x, vec("norm2"), consts("ones"), RMS_EPS1, h2)
                gemm(nc, "wq", io["peer_wq"], KD, lambda b: h2, 2 * PH,
                     keep_plain(lambda n: qT[:, DS(n, 1), :].rearrange("p a t -> p (a t)")))
                turn(nc, "h", token_groups(h2, range(KD), h_tok), consts("ident"))
                peer_route(nc, qT, io["peer_keys"], consts, idx, gate)
            peer_experts(nc, h_tok, idx, gate, io["peer_u"], io["peer_v"], acc)
            add_turned(nc, "peer", x, acc, consts("ident"))
            rmsnorm(nc, "norm_f", x, vec("norm_f"), consts("ones"), RMS_EPS1, x)

        swiglu_ffn(nc, "ffn1", x, vec("n1"), consts, io["ffn1_w_in"], io["ffn1_w_out"])
        with ExitStack() as s3:
            def sb(name, shape, dt=F32):
                return s3.enter_context(nc.sbuf_tensor(name, shape, dt))

            pr = sb("pr", [P, N_IN2, T])
            va, vb, wi = sb("va_tok", [P, TT, PAIRS * P]), sb("vb_tok", [P, TT, P]), sb("wi_tok", [P, TT, 8])
            oa, ob = sb("oa", [P, PAIRS, T]), sb("ob", [P, PAIRS, T])
            with nc.sbuf_tensor("h_mix", [P, KD, T], F32) as h:
                rmsnorm(nc, "n2", x, vec("n2"), consts("ones"), RMS_EPS2, h)
                gemm(nc, "w_in2", io["w_in_2"], KD, lambda b: h, N_IN2,
                     keep_plain(lambda n: pr[:, DS(n, 1), :].rearrange("p a t -> p (a t)")))
            rope(nc, pr, consts("swap"), io["rope"])
            turn(nc, "values", token_groups(pr, range(C_VA, C_VA + 4), va) + token_groups(pr, [C_VB], vb)
                 + token_groups(pr, [C_WI], wi), consts("ident"))
            blk = lambda b: pr[:, b, :].rearrange("p a t -> p (a t)")
            with nc.sbuf_tensor("toeplitz", [P, 8, T], F32) as toe:
                line = io["bias_line"]
                L = line.shape[1]
                lines = nc.dram_tensor("bias_lines", [8 * P, L], F32).ap()
                load(nc, "lines", (bass.AP(lines.tensor, 0, [[P * L, 8], [L, P], [1, L]]),
                                   bass.AP(line.tensor, 0, [[L, 8], [0, P], [1, L]])))
                load(nc, "bias", (toe[:, :, :], bass.AP(lines.tensor, P - 1, [[L - 1, P], [P * L, 8], [1, T]])))
                with nc.Block() as block:
                    @block.vector
                    def _(dve):
                        nc.vector.memset(toe[0:HEAD, :, T - HEAD:T], NEG)
                attention(nc, "atta", lambda i: blk(DS(i + C_QA, 1)), lambda i: blk(DS(i + C_KA, 1)),
                          lambda i: va[:, :, DS(i * P, P)],
                          lambda i, hh, t: toe[:, DS(2 * i + hh, 1), 3 * P - P * t:T].rearrange("p a t -> p (a t)"),
                          consts("ident"), oa)
            with nc.sbuf_tensor("mask_b", [P, TT, T], F32) as m:
                index_mask(nc, pr, wi, m)
                attention(nc, "attb", lambda i: blk(DS(i + C_QB, 1)), lambda i: pr[:, C_KB, :],
                          lambda i: vb[:, :, :], lambda i, hh, t: m[:, t, 0:P * (t + 1)], consts("ident"), ob)
            with nc.sbuf_tensor("merged", [P, KD, T], F32) as merged:
                gemm(nc, "branches", io["w_branches"], PAIRS, lambda b: ob if b % 2 else oa, 2 * KD, merge_into(merged, pr))
                gemm(nc, "w_out2", io["w_out_2"], KD, lambda b: merged, KD, add_to(x))
        swiglu_ffn(nc, "ffn2", x, vec("n3"), consts, io["ffn2_w_in"], io["ffn2_w_out"])
        rmsnorm(nc, "nf", x, vec("nf"), consts("ones"), RMS_EPS2, x)
        load(nc, "result", (out, x[:, :, :].rearrange("p k t -> p (k t)")))



def _shape_constants():
    n = np.arange(P)
    head, tok = n // HEAD, n % HEAD
    same = head[:, None] == head[None, :]
    near = (tok[:, None] // SUB) == (tok[None, :] // SUB)
    low = same & (tok[:, None] > tok[None, :])
    up = same & (tok[:, None] < tok[None, :])
    c = np.arange(HEAD)
    swap = np.zeros((P, P))
    for i in range(P):
        j = i % HEAD
        if j < 8:
            swap[i + 8, i] = 1
        elif j < 16:
            swap[i - 8, i] = 1
    parts = {
        "ident": np.eye(P), "ones": np.ones((P, P)), "heads": same,
        "stack": (tok[:, None] == c[None, :]), "swap": swap,
        "low_near": low & near, "low_far": low & ~near, "up_near": up & near, "up_far": up & ~near,
        "low_strict": low, "up_strict": up,
        "low_incl": tok[:, None] >= c[None, :], "up_incl": tok[:, None] <= c[None, :],
        "reset": np.broadcast_to((np.arange(T) % CHUNK != 0)[None, :], (P, T)),
        "slot": np.broadcast_to(np.arange(TOPK)[None, :], (P, TOPK)),
    }
    consts = np.concatenate([np.asarray(parts[k], np.float32) for k, _ in CONSTS], axis=1)
    t = np.arange(T)
    inv = [1.0 / (np.minimum(t + w // 2, T) - np.maximum(t - w // 2, 0)) for w in WINDOWS]
    inv_counts = np.broadcast_to(np.concatenate(inv).astype(np.float32)[None, :], (P, 4 * T))
    freq = np.power(np.float32(500000.0), -np.arange(0, 16, 2, dtype=np.float32) / np.float32(16))
    ang = (t.astype(np.float32)[:, None] * freq[None, :]).astype(np.float32)
    cos, sin = np.cos(ang).T, np.sin(ang).T
    table = np.zeros((P, 2, T), np.float32)
    table[:, 0] = 1
    for h in range(2):
        for half, sign in ((0, -1), (1, 1)):
            rows = slice(HEAD * h + 8 * half, HEAD * h + 8 * half + 8)
            table[rows, 0] = cos
            table[rows, 1] = sign * sin
    return consts, np.ascontiguousarray(inv_counts), table.reshape(P, 2 * T)


def _blocks(w):
    k, n = w.shape
    return np.ascontiguousarray(w.reshape(k // P, P, n // P, P).transpose(2, 1, 0, 3).reshape(n, k))


def _channels(a):
    return a.reshape(-1, P).T


def _widen(w, n):
    return np.concatenate([w, np.zeros((w.shape[0], n - w.shape[1]), w.dtype)], axis=1)


def _layout(inp):
    a = {k: np.asarray(v) for k, v in inp.items()}
    one = {k: v[0] for k, v in a.items() if v.ndim > 1}
    consts, inv_counts, rope = _shape_constants()
    rw = 12 * P + 2 * P + P + GATE_REST
    w_in = one["w_in"]
    w_in1 = np.concatenate([_widen(w_in[:, :rw], N_SHIFT * P), w_in[:, rw:]], axis=1)
    mu = _widen(one["shift_mu"], N_SHIFT * P)
    vectors = dict(norm1=one["norm1_w"], mu0=mu[0], mu1=mu[1], w0=one["w0"], a0=one["a0"], k_k=one["k_k"], k_a=one["k_a"],
                   r_k=one["r_k"], lnw=one["ln_x_w"], lnb=one["ln_x_b"], pool_scale=one["pool_scale"], norm2=one["norm2_w"],
                   norm_f=a["norm_f_w"], n1=one["n1_g_2"], n2=one["n2_g_2"], n3=one["n3_g_2"], nf=a["nf_g_2"])
    io = {
        "x": one["x"].T.reshape(KD, P, T).transpose(1, 0, 2).reshape(P, KD * T),
        "consts": consts, "inv_counts": inv_counts, "rope": rope,
        "vec": np.concatenate([_channels(vectors[k]) for k, _ in VECTORS], axis=1),
        "w_in": _blocks(w_in1),
        "lora": np.concatenate([one["w_up"].reshape(P, -1), one["a_up"].reshape(P, -1)], axis=1),
        "pool_w": one["pool_w"].transpose(1, 0, 2).reshape(P, 4 * P),
        "g_up": np.concatenate([one["g_up"], np.zeros((2 * P - P - GATE_REST, PAIRS * P), np.float32)]).reshape(
            2, P, PAIRS * P).transpose(1, 0, 2).reshape(P, -1),
        "w_out": _blocks(one["w_out"]),
        "peer_wq": _blocks(one["peer_wq"]),
        "peer_keys": one["peer_keys"].transpose(3, 0, 1, 2).reshape(P, -1),
        "peer_u": one["peer_u"], "peer_v": one["peer_v"],
    }
    for f in ("ffn1", "ffn2"):
        w = one[f"{f}_w_in_2"].reshape(D, 2, KF, P).transpose(0, 2, 1, 3).reshape(D, 2 * D_FF)
        io[f"{f}_w_in"] = _blocks(w)
        io[f"{f}_w_out"] = _blocks(one[f"{f}_w_out_2"])
    w = one["w_in_2"]
    sizes = (512, 512, 512, 512, 128, 128, 512, 64, 8, D, D)
    qa, ka, va, qb, kb, vb, qi, ki, wi, ga, gb = np.split(w, np.cumsum(sizes)[:-1], axis=1)
    order = [h * HEAD + c for j in range(4) for h in (j, j + 4) for c in range(HEAD)]
    io["w_in_2"] = _blocks(np.concatenate([qa, ka, va, qb[:, order], kb, vb, qi, ki, ki, _widen(wi, P), ga, gb], axis=1))
    ab = np.stack([_blocks(one["w_branch_a_2"]).reshape(KD, P, -1), _blocks(one["w_branch_b_2"][order]).reshape(KD, P, -1)], axis=1)
    io["w_branches"] = ab.reshape(2 * D, PAIRS * P)
    io["w_out_2"] = _blocks(one["w_out_2"])
    dist = np.clip(511 - np.arange(5 * P - 1), -128, 128) + 128
    io["bias_line"] = one["rel_bias_2"][:, dist]
    return {k: np.ascontiguousarray(v) for k, v in io.items()}


def kernel(**inputs):
    import concourse.bacc as _bacc
    from concourse.bass_utils import run_bass_kernel_spmd as _run

    nc = _bacc.Bacc("TRN2", target_bir_lowering=False, num_devices=1)
    arrays = _layout(inputs)
    io = {k: nc.dram_tensor(f"in_{k}", v.shape, mybir.dt.from_np(v.dtype), kind="ExternalInput").ap() for k, v in arrays.items()}
    io["out"] = nc.dram_tensor("out", (P, KD * T), F32, kind="ExternalOutput").ap()
    build(nc, io)
    r = _run(nc, [{f"in_{k}": v for k, v in arrays.items()}], core_ids=[0])
    y = r.results[0]["out"]
    return np.ascontiguousarray(y.reshape(P, KD, T).transpose(2, 1, 0).reshape(1, T, D))
```

```python
import numpy as np
from contextlib import ExitStack

import concourse.bass as bass
from concourse import mybir

F32 = mybir.dt.float32
F32R = mybir.dt.float32r
U32 = mybir.dt.uint32
ALU = mybir.AluOpType
ACT = mybir.ActivationFunctionType
AX = mybir.AxisListType

P = 128
T = 512
TT = T // P
D = 1024
KD = D // P
HEAD = 64
PAIRS = 4
CHUNK = 64
NCHUNK = T // CHUNK
SUB = 16
DECAY = float(np.exp(-0.5))
GN_EPS = 64e-5
RMS_EPS1 = 1e-5
RMS_EPS2 = 1e-6
N_KEYS = 128
TOPK = 16
PH = 8
SLOTS = PH * TOPK
D_FF = 2816
KF = D_FF // P
IDX_TOPK = 128
NEG = -1.0e30
GONE = -3.0e38
DS = bass.ds

B_R, B_K, B_V, B_WD, B_AD, B_GD, B_POOL, N_IN1 = 0, 4, 8, 12, 13, 14, 16, 20
N_SHIFT = 16
GATE_REST = 32
C_QA, C_KA, C_VA, C_QB, C_KB, C_VB, C_QI, C_KI, C_WI, C_GA, C_GB, N_IN2 = 0, 4, 8, 12, 16, 17, 18, 22, 23, 24, 32, 40
WINDOWS = (2, 4, 8, 16)

VECTORS = [("norm1", 8), ("mu0", 16), ("mu1", 16), ("w0", 8), ("a0", 8), ("k_k", 4), ("k_a", 4),
           ("r_k", 4), ("lnw", 4), ("lnb", 4), ("pool_scale", 4), ("norm2", 8), ("norm_f", 8),
           ("n1", 8), ("n2", 8), ("n3", 8), ("nf", 8)]
V_AT, _at = {}, 0
for _name, _n in VECTORS:
    V_AT[_name] = (_at, _n)
    _at += _n
N_VEC = _at

CONSTS = [("ident", 128), ("ones", 128), ("heads", 128), ("stack", 64), ("swap", 128),
          ("low_near", 128), ("low_far", 128), ("up_near", 128), ("up_far", 128),
          ("low_strict", 128), ("up_strict", 128), ("low_incl", 64), ("up_incl", 64),
          ("reset", 512), ("slot", 16)]
C_AT, _at = {}, 0
for _name, _n in CONSTS:
    C_AT[_name] = (_at, _n)
    _at += _n
N_CONST = _at


class Signals:

    def __init__(self, nc, ctx):
        self.nc, self.used = nc, []
        ctx.callback(self.close)

    def __call__(self, name):
        self.used.append(self.nc.alloc_semaphore(name))
        return self.used[-1]

    def close(self):
        self.nc.clear_and_free_semaphores(self.used)
        self.nc.all_engine_barrier()


class Own:

    def __init__(self, eng, sem, base=0):
        self.eng, self.sem, self.base, self.n = eng, sem, base, 0

    def add(self, ins):
        ins.then_inc(self.sem, 1)
        self.n += 1

    def wait(self, back=0):
        self.eng.wait_ge(self.sem, self.base + (self.n - back))

    def link(self, ins):
        self.add(ins)
        self.wait()


def hold(eng, sem, value, pace):
    eng.wait_ge(sem, value)
    eng.sem_inc(pace, 1)


def bcast(ap, axis, n):
    dims = [list(x) for x in ap.ap]
    dims.insert(axis, [0, n])
    return bass.AP(ap.tensor, ap.offset, dims)



def split(nc, tag, src, hi, lo):
    with ExitStack() as ctx:
        signal = Signals(nc, ctx)
        rounded = signal(f"{tag}_rounded")
        block = ctx.enter_context(nc.Block())
        n = src.shape[1]

        @block.scalar
        def _(act):
            for k in range(n):
                nc.scalar.copy(hi[:, k], src[:, k]).then_inc(rounded, 1)

        @block.vector
        def _(dve):
            for k in range(n):
                dve.wait_ge(rounded, k + 1)
                nc.vector.tensor_tensor(lo[:, k], src[:, k], hi[:, k].bitcast(F32), ALU.subtract)


RING = 4
SLOT = 2


def gemm(nc, tag, w, kt, rhs, nblocks, evacuation):
    with ExitStack() as ctx:
        signal = Signals(nc, ctx)
        raw = ctx.enter_context(nc.sbuf_tensor(f"{tag}_w", [P, SLOT, kt, P], F32))
        w_hi = ctx.enter_context(nc.sbuf_tensor(f"{tag}_w_hi", [P, SLOT, kt, P], F32R))
        w_lo = ctx.enter_context(nc.sbuf_tensor(f"{tag}_w_lo", [P, SLOT, kt, P], F32R))
        out = ctx.enter_context(nc.psum_tensor(f"{tag}_out", [P, RING, T], F32))
        w_in = [signal(f"{tag}_weights{b}") for b in range(SLOT)]
        rounded = signal(f"{tag}_rounded")
        parted = signal(f"{tag}_parted")
        ev = evacuation
        ev.out, ev.done, ev.free, ev.own, ev.half = out, signal(f"{tag}_products"), signal(f"{tag}_banks_free"), signal(
            f"{tag}_own"), signal(f"{tag}_half")
        done = ev.done
        rounds = nblocks // RING
        assert rounds * RING == nblocks and rounds > 1
        block = ctx.enter_context(nc.Block())

        def source(n):
            return w[DS(n * P, P), :].rearrange("p (k n) -> p k n", n=P)

        def turns(eng, start, step):
            for b in range(SLOT):
                start(b)
            with eng.Fori(0, rounds - 1) as i:
                for b in range(RING):
                    step(i, b, True)
            for b in range(RING):
                step(rounds - 1, b, b + SLOT < RING)

        @block.sync
        def _(sp):
            def first(b):
                sp.dma_start(raw[:, b], source(b)).then_inc(w_in[b], 16)

            def step(i, b, more):
                if more:
                    sp.wait_ge(parted, RING * i + b + 1)
                    sp.dma_start(raw[:, b % SLOT], source(i * RING + (b + SLOT))).then_inc(w_in[b % SLOT], 16)

            turns(sp, first, step)

        @block.tensor
        def _(pe):
            with pe.Fori(0, rounds) as i:
                for b in range(RING):
                    pe.wait_ge(parted, RING * i + b + 1)
                    pe.wait_ge(ev.free, RING * i + b + 1)
                    hi, lo = rhs(b)
                    s = b % SLOT
                    for k in range(kt):
                        nc.tensor.matmul(out[:, b], w_hi[:, s, k], hi[:, k], start=(k == 0), stop=False)
                        nc.tensor.matmul(out[:, b], w_hi[:, s, k], lo[:, k], start=False, stop=False)
                        mm = nc.tensor.matmul(out[:, b], w_lo[:, s, k], hi[:, k], start=False, stop=(k == kt - 1))
                    mm.then_inc(done, 1)

        @block.scalar
        def _(act):
            def high(n, turn):
                act.wait_ge(w_in[n % SLOT], 16 * turn)
                nc.scalar.copy(w_hi[:, n % SLOT], raw[:, n % SLOT]).then_inc(rounded, 1)

            def step(i, b, more):
                act.wait_ge(done, RING * i + b + 1)
                ev.scalar(nc, act, i, b)
                if more:
                    high(b + SLOT, i * (RING // SLOT) + (b // SLOT + 2))

            act.sem_inc(ev.free, RING)
            turns(act, lambda b: high(b, 1), step)

        @block.vector
        def _(dve):
            def low(n, count):
                dve.wait_ge(rounded, count)
                nc.vector.tensor_tensor(w_lo[:, n % SLOT], raw[:, n % SLOT], w_hi[:, n % SLOT].bitcast(F32),
                                        ALU.subtract).then_inc(parted, 1)

            def step(i, b, more):
                dve.wait_ge(done, RING * i + b + 1)
                ev.vector(nc, dve, i, b)
                if more:
                    low(b + SLOT, RING * i + (b + SLOT + 1))

            turns(dve, lambda b: low(b, b + 1), step)


def at_block(x, n):
    return x[:, DS(n, 1), :].rearrange("p a t -> p (a t)")


class Keep:

    def __init__(self, dst):
        self.dst = dst

    def scalar(self, nc, act, i, b):
        nc.scalar.copy(self.dst(i * RING + b), self.out[:, b]).then_inc(self.free, 1)

    def vector(self, nc, dve, i, b):
        pass


class AddTo:

    def __init__(self, x, scale=1.0):
        self.x, self.scale = x, scale

    def scalar(self, nc, act, i, b):
        pass

    def vector(self, nc, dve, i, b):
        xb = at_block(self.x, i * RING + b)
        nc.vector.scalar_tensor_tensor(out=xb, in0=self.out[:, b], scalar=float(self.scale), in1=xb,
                                       op0=ALU.mult, op1=ALU.add).then_inc(self.free, 1)


class Swiglu:

    def __init__(self, hi, lo, silu, product):
        self.hi, self.lo, self.silu, self.product = hi, lo, silu, product

    def scalar(self, nc, act, i, b):
        if b % 2 == 0:
            act.wait_ge(self.free, RING * i + b + 1)
            nc.scalar.activation(self.silu[:, b // 2], self.out[:, b], ACT.Silu).then_inc(self.half, 1)

    def vector(self, nc, dve, i, b):
        if b % 2:
            n, j = i * (RING // 2) + b // 2, b // 2
            dve.wait_ge(self.half, n + 1)
            nc.vector.tensor_tensor(self.product[:, j], self.silu[:, j], self.out[:, b], ALU.mult).then_inc(self.free, 2)
            dve.wait_ge(self.free, RING * i + (RING + b + 1))
            hi = at_block(self.hi, n)
            nc.vector.tensor_copy(hi, self.product[:, j]).then_inc(self.own, 1)
            dve.wait_ge(self.own, n * 2 + 1)
            nc.vector.tensor_tensor(at_block(self.lo, n), self.product[:, j], hi.bitcast(F32), ALU.subtract).then_inc(self.own, 1)
            dve.wait_ge(self.own, n * 2 + 2)


class Merge:

    def __init__(self, m, pr):
        self.m, self.pr = m, pr

    def scalar(self, nc, act, i, b):
        if b % 2 == 0:
            n = i * (RING // 2) + b // 2
            for first in (C_GA, C_GB):
                g = at_block(self.pr, n + first)
                ins = nc.scalar.activation(g, g, ACT.Sigmoid)
            ins.then_inc(self.half, 1)

    def vector(self, nc, dve, i, b):
        if b % 2:
            n = i * (RING // 2) + b // 2
            dve.wait_ge(self.half, n + 1)
            ga, gb = at_block(self.pr, n + C_GA), at_block(self.pr, n + C_GB)
            nc.vector.tensor_tensor(ga, self.out[:, b - 1], ga, ALU.mult)
            nc.vector.tensor_tensor(gb, self.out[:, b], gb, ALU.mult).then_inc(self.free, 2)
            dve.wait_ge(self.free, RING * i + (RING + b + 1))
            nc.vector.tensor_tensor(at_block(self.m, n), ga, gb, ALU.add)



def rmsnorm(nc, tag, x, weight, ones, eps, out=None, parts=None):
    with ExitStack() as ctx:
        signal = Signals(nc, ctx)
        sq = ctx.enter_context(nc.sbuf_tensor(f"{tag}_sq", [P, KD, T], F32))
        rstd = ctx.enter_context(nc.sbuf_tensor(f"{tag}_rstd", [P, T], F32))
        epst = ctx.enter_context(nc.sbuf_tensor(f"{tag}_eps", [P, 1], F32))
        total = ctx.enter_context(nc.psum_tensor(f"{tag}_total", [P, T], F32))
        squared, summed, rooted, own, normed, rounded = (
            signal(f"{tag}_{n}") for n in ("squared", "summed", "rooted", "own", "normed", "rounded"))
        block = ctx.enter_context(nc.Block())
        dst = sq if out is None else out

        @block.scalar
        def _(act):
            for k in range(0, KD, 2):
                nc.scalar.activation(sq[:, k], x[:, k], ACT.Square).then_inc(squared, 1)
            act.wait_ge(summed, 1)
            act.wait_ge(own, 1)
            nc.scalar.activation(rstd[:, :], total[:, :], ACT.Sqrt, bias=epst[:, 0:1], scale=1.0 / D).then_inc(rooted, 1)
            if parts:
                for k in range(KD):
                    act.wait_ge(normed, k + 1)
                    nc.scalar.copy(parts[0][:, k], dst[:, k]).then_inc(rounded, 1)

        @block.tensor
        def _(pe):
            for k in range(KD):
                if k % 2:
                    pe.wait_ge(own, 1 + (k + 1) // 2)
                else:
                    pe.wait_ge(squared, k // 2 + 1)
                mm = nc.tensor.matmul(total[:, :], ones, sq[:, k], start=(k == 0), stop=(k == KD - 1))
            mm.then_inc(summed, 1)

        @block.gpsimd
        def _(pool):
            if parts:
                for k in range(1, KD, 2):
                    pool.wait_ge(rounded, k + 1)
                    nc.gpsimd.tensor_tensor(parts[1][:, k], dst[:, k], parts[0][:, k].bitcast(F32), ALU.subtract)

        @block.vector
        def _(dve):
            nc.vector.memset(epst[:, :], eps).then_inc(own, 1)
            for k in range(1, KD, 2):
                nc.vector.tensor_tensor(sq[:, k], x[:, k], x[:, k], ALU.mult).then_inc(own, 1)
            dve.wait_ge(rooted, 1)
            nc.vector.reciprocal(rstd[:, :], rstd[:, :]).then_inc(own, 1)
            dve.wait_ge(own, 2 + KD // 2)
            for k in range(KD):
                nc.vector.scalar_tensor_tensor(out=dst[:, k], in0=x[:, k], scalar=weight[:, k:k + 1],
                                               in1=rstd[:, :], op0=ALU.mult, op1=ALU.mult).then_inc(normed, 1)
            if parts:
                for k in range(0, KD, 2):
                    dve.wait_ge(rounded, k + 1)
                    nc.vector.tensor_tensor(parts[1][:, k], dst[:, k], parts[0][:, k].bitcast(F32), ALU.subtract)



def token_shift(nc, p, mu0, mu1):
    with ExitStack() as ctx:
        signal = Signals(nc, ctx)
        rest = ctx.enter_context(nc.sbuf_tensor("shift_rest", [P, N_SHIFT], F32))
        q = ctx.enter_context(nc.sbuf_tensor("shift_sum", [P, 4, T], F32))
        factors, kept, added, put, own, pace = (
            signal(f"shift_{n}") for n in ("factors", "kept", "added", "put", "own", "pace"))
        rounds = N_SHIFT // 4
        block = ctx.enter_context(nc.Block())

        def cols(n, first):
            return p[:, DS(n, 1), first:first + T].rearrange("p a t -> p (a t)")

        @block.vector
        def _(dve):
            o = Own(dve, own)
            o.add(nc.vector.memset(p[:, :, 0:1], 0.0))
            o.add(nc.vector.memset(p[:, :, T + 1:T + 2], 0.0))
            o.link(nc.vector.tensor_tensor(rest[:, :], mu0, mu1, ALU.add))
            nc.vector.tensor_scalar(rest[:, :], rest[:, :], -1.0, 1.0, ALU.mult, ALU.add).then_inc(factors, 1)
            with dve.Fori(0, rounds) as i:
                for b in range(4):
                    n = 4 * i + b
                    dve.wait_ge(kept, n + 1)
                    nc.vector.scalar_tensor_tensor(out=q[:, b], in0=cols(n, 0), scalar=mu0[:, DS(n, 1)], in1=q[:, b],
                                                   op0=ALU.mult, op1=ALU.add).then_inc(own, 1)
                for b in range(4):
                    n = 4 * i + b
                    dve.wait_ge(own, n + 4)
                    nc.vector.scalar_tensor_tensor(out=q[:, b], in0=cols(n, 2), scalar=mu1[:, DS(n, 1)], in1=q[:, b],
                                                   op0=ALU.mult, op1=ALU.add).then_inc(added, 1)

        @block.scalar
        def _(act):
            act.wait_ge(factors, 1)
            with act.Fori(0, rounds) as i:
                for b in range(4):
                    n = 4 * i + b
                    nc.scalar.activation(q[:, b], cols(n, 1), ACT.Copy, scale=rest[:, DS(n, 1)]).then_inc(kept, 1)
                for b in range(4):
                    n = 4 * i + b
                    hold(act, added, n + 1, pace)
                    nc.scalar.copy(cols(n, 1), q[:, b]).then_inc(put, 1)
                act.wait_ge(put, 4 * i + 4)


def rwkv_operands(nc, q, lora, vec, consts, ar, bk, kk, kd_sum, w_end):
    with ExitStack() as ctx:
        signal = Signals(nc, ctx)
        omk = ctx.enter_context(nc.sbuf_tensor("omk", [P, PAIRS], F32))
        nrm = ctx.enter_context(nc.sbuf_tensor("nrm", [P, T], F32))
        sq = ctx.enter_context(nc.sbuf_tensor("kk_sq", [P, PAIRS, T], F32))
        sg = ctx.enter_context(nc.sbuf_tensor("sg", [P, 2, T], F32))
        aa = ctx.enter_context(nc.sbuf_tensor("aa", [P, 2, T], F32))
        cum = ctx.enter_context(nc.sbuf_tensor("cum", [P, 2, T], F32))
        cpre = ctx.enter_context(nc.sbuf_tensor("cpre", [P, 2, T], F32))
        wt = ctx.enter_context(nc.sbuf_tensor("wt", [P, 2, T], F32))
        wpre = ctx.enter_context(nc.sbuf_tensor("wpre", [P, 2, T], F32))
        winv = ctx.enter_context(nc.sbuf_tensor("winv", [P, 2, T], F32))
        kt_ = ctx.enter_context(nc.sbuf_tensor("kt_", [P, 2, T], F32))
        zp = ctx.enter_context(nc.psum_tensor("zp", [P, 2, 2, T], F32))
        np_ = ctx.enter_context(nc.psum_tensor("np_", [P, PAIRS, T], F32))
        tanhed = signal("tanhed")
        squares = signal("kk_squares")
        norms = signal("kk_norms")
        roots = signal("kk_roots")
        kk_done = signal("kk_done")
        zs = signal("lora_products")
        sigs = signal("lora_sigmoids")
        sums = signal("decay_sums")
        exps = signal("decay_exps")
        used = signal("operands_made")
        own = signal("operands_own")
        reset = consts("reset")
        block = ctx.enter_context(nc.Block())

        def row(ap, i):
            return ap[:, DS(i, 1), :].rearrange("p a t -> p (a t)")

        @block.scalar
        def _(act):
            nc.scalar.activation(q[:, B_WD], q[:, B_WD], ACT.Tanh).then_inc(tanhed, 1)
            act.wait_ge(squares, PAIRS)
            for p in range(PAIRS):
                act.wait_ge(norms, p + 1)
                nc.scalar.activation(sq[:, p], np_[:, p], ACT.Sqrt).then_inc(roots, 1)
            with act.Fori(0, PAIRS) as i:
                for d in range(2):
                    act.wait_ge(zs, 2 * i + d + 1)
                    act.wait_ge(used, 2 * i + d + 1)
                    nc.scalar.activation(sg[:, d], zp[:, d, 0], ACT.Sigmoid, bias=vec("w0")[:, DS(i + PAIRS * d, 1)])
                    nc.scalar.activation(aa[:, d], zp[:, d, 1], ACT.Sigmoid, bias=vec("a0")[:, DS(i + PAIRS * d, 1)]).then_inc(sigs, 1)
                for d in range(2):
                    act.wait_ge(sums, 2 * i + d + 1)
                    nc.scalar.activation(wt[:, d], cum[:, d], ACT.Exp, scale=-DECAY)
                    nc.scalar.activation(wpre[:, d], cpre[:, d], ACT.Exp, scale=-DECAY)
                    nc.scalar.activation(winv[:, d], cum[:, d], ACT.Exp, scale=DECAY).then_inc(exps, 1)

        @block.tensor
        def _(pe):
            for p in range(PAIRS):
                pe.wait_ge(squares, p + 1)
                nc.tensor.matmul(np_[:, p], consts("heads"), sq[:, p], start=True, stop=True).then_inc(norms, 1)
            pe.wait_ge(tanhed, 1)
            for p in range(PAIRS):
                for d in range(2):
                    n = 2 * p + d
                    if n >= 2:
                        pe.wait_ge(sigs, n - 1)
                    rows = slice(HEAD * d, HEAD * d + HEAD)
                    nc.tensor.matmul(zp[:, d, 0], lora[rows, 0, p * P:(p + 1) * P], q[rows, B_WD], start=True, stop=True)
                    nc.tensor.matmul(zp[:, d, 1], lora[rows, 1, p * P:(p + 1) * P], q[rows, B_AD],
                                     start=True, stop=True).then_inc(zs, 1)

        @block.vector
        def _(dve):
            dve.sem_inc(used, 2)
            nc.vector.tensor_scalar(omk[:, :], vec("k_a"), -1.0, 1.0, ALU.mult, ALU.add)
            for p in range(PAIRS):
                nc.vector.tensor_scalar(kk[:, p], q[:, B_K + p], vec("k_k")[:, p:p + 1], None, ALU.mult).then_inc(own, 1)
            for p in range(PAIRS):
                dve.wait_ge(own, p + 1)
                nc.vector.tensor_tensor(sq[:, p], kk[:, p], kk[:, p], ALU.mult).then_inc(squares, 1)
            n = PAIRS
            for p in range(PAIRS):
                dve.wait_ge(roots, p + 1)
                nc.vector.tensor_scalar(sq[:, p], sq[:, p], 1e-12, None, ALU.max).then_inc(own, 1)
                n += 1
                dve.wait_ge(own, n)
                nc.vector.reciprocal(nrm[:, :], sq[:, p]).then_inc(own, 1)
                n += 1
                dve.wait_ge(own, n)
                nc.vector.tensor_tensor(kk[:, p], kk[:, p], nrm[:, :], ALU.mult).then_inc(own, 1)
                n += 1
            dve.wait_ge(own, n)
            base = n
            per = 11
            with dve.Fori(0, PAIRS) as i:
                n = 0
                for d in range(2):
                    way = slice(None) if d == 0 else slice(None, None, -1)
                    dve.wait_ge(sigs, 2 * i + d + 1)
                    nc.vector.tensor_tensor_scan(out=cum[:, d, way], data0=reset, data1=sg[:, d, way], initial=0.0,
                                                 op0=ALU.mult, op1=ALU.add).then_inc(own, 1)
                    n += 1
                    nc.vector.tensor_scalar(kt_[:, d], aa[:, d], vec("k_a")[:, DS(i, 1)], omk[:, DS(i, 1)],
                                            ALU.mult, ALU.add).then_inc(own, 1)
                    n += 1
                    dve.wait_ge(own, per * i + base + n - 1)
                    nc.vector.tensor_tensor(cpre[:, d], cum[:, d], sg[:, d], ALU.subtract).then_inc(sums, 1)
                    dve.wait_ge(own, per * i + base + n)
                    nc.vector.tensor_tensor(kt_[:, d], kt_[:, d], row(q[:, B_K:B_K + PAIRS, :], i), ALU.mult).then_inc(own, 1)
                    n += 1
                    nc.vector.tensor_tensor(aa[:, d], aa[:, d], row(kk, i), ALU.mult).then_inc(own, 1)
                    n += 1
                dve.wait_ge(own, per * i + base + n)
                nc.vector.tensor_tensor(row(kd_sum, i), kt_[:, 0], kt_[:, 1], ALU.add).then_inc(own, 1)
                n += 1
                for d in range(2):
                    dve.wait_ge(exps, 2 * i + d + 1)
                    nc.vector.tensor_tensor(row(ar[:, d, 0], i), wpre[:, d], row(kk, i), ALU.mult)
                    nc.vector.tensor_tensor(row(ar[:, d, 1], i), wt[:, d], row(q[:, B_R:B_R + PAIRS, :], i), ALU.mult)
                    nc.vector.scalar_tensor_tensor(out=row(bk[:, d, 0], i), in0=aa[:, d], scalar=-1.0, in1=winv[:, d],
                                                   op0=ALU.mult, op1=ALU.mult)
                    nc.vector.tensor_tensor(row(bk[:, d, 1], i), kt_[:, d], winv[:, d], ALU.mult).then_inc(own, 1)
                    n += 1
                    ends = wt[:, d, CHUNK - 1::CHUNK] if d == 0 else wt[:, d, 0::CHUNK]
                    nc.vector.tensor_copy(w_end[:, d, :, DS(i, 1)].rearrange("p c a -> p (c a)"), ends).then_inc(used, 1)
                assert n == per, n


def recurrence(nc, ar, bk, v, w_end, consts, o):
    with ExitStack() as ctx:
        signal = Signals(nc, ctx)
        def sb(name, *shape):
            return ctx.enter_context(nc.sbuf_tensor(name, [P, 2, PAIRS, *shape], F32))

        a_w, b_w, k_w, v_w = (sb(f"{n}_wide_c", P) for n in "abkv")
        DT, Dm, E, LkT = sb("DT", P), sb("Dm", P), sb("E", P), sb("LkT", P)
        PbT, PkT, V, B = sb("PbT", HEAD), sb("PkT", HEAD), sb("V", HEAD), sb("B", HEAD)
        Vw, Bw, Kw = sb("Vw", P), sb("Bw", P), sb("Kw", P)
        D2, D2T, R1, R2, X = sb("D2", P), sb("D2T", P), sb("R1", P), sb("R2", P), sb("X", P)
        D4, D4T, D8, N, NT, N2T, X1, X2, Y = Dm, DT, D2, D2T, Dm, DT, LkT, E, R1
        Aw, Uw, MTw, RT = sb("Aw", P), sb("Uw", P), sb("MTw", P), sb("RT", HEAD)
        S, Sw, Sn = sb("S", HEAD), sb("Sw", P), sb("Sn", HEAD)
        banks = ctx.enter_context(nc.psum_tensor("rec_banks", [P, 2, 4, PAIRS, P], F32))

        pe_done = [signal(f"rec_products{d}") for d in range(2)]
        by_dve = [signal(f"rec_by_vector{d}") for d in range(2)]
        by_act = [signal(f"rec_by_scalar{d}") for d in range(2)]
        loaded = [signal(f"rec_wide{d}") for d in range(2)]
        sw_done = [signal(f"rec_state_wide{d}") for d in range(2)]
        own = signal("rec_own")

        STEPS = [("LbT", "v"), ("LkT", "v"), ("Lb", "v"), ("VB", "a"), ("KG", "a"), ("D2", "a"), ("D2T", "a"),
                 ("R2", "v"), ("D4", "a"), ("D4T", "a"), ("R3", "v"), ("D8", "a"), ("R4", "v"),
                 ("N", "a"), ("NT", "a"), ("X1", "a"), ("N2T", "a"), ("X2", "v"), ("Y", "v"),
                 ("MR", "v"), ("out", "a"), ("S", "v")]
        AT = {name: n for n, (name, _) in enumerate(STEPS)}
        NS = len(STEPS)
        ORD, PER = {}, {"v": 0, "a": 0}
        for name, e in STEPS:
            PER[e] += 1
            ORD[name] = (e, PER[e])
        WIDE_Y, WIDE_M = ORD["N2T"][1] + 1, ORD["N2T"][1] + 2
        ORD["out"] = ("a", WIDE_M + 1)
        PER["a"] += 2

        with nc.Block() as block:
            @block.vector
            def _(dve):
                for w in (Vw, Bw, Kw, Aw, Uw, MTw):
                    nc.vector.memset(w[:, :, :, :], 0.0)

            @block.gpsimd
            def _(pool):
                for w in (a_w, b_w, k_w, v_w, Sw, S):
                    nc.gpsimd.memset(w[:, :, :, :], 0.0)

        block = ctx.enter_context(nc.Block())

        def chunk(c, d):
            return c * CHUNK if d == 0 else c * -CHUNK + (NCHUNK - 1) * CHUNK

        halves = [(slice(0, HEAD), slice(0, HEAD)), (slice(HEAD, P), slice(HEAD, P))]

        @block.gpsimd
        def _(pool):
            def widen(c, d):
                at = chunk(c, d)
                for w, src in ((b_w, bk[:, d, 0]), (a_w, ar[:, d, 0]), (k_w, bk[:, d, 1]), (v_w, v)):
                    for rows, cols in halves:
                        ins = nc.gpsimd.tensor_copy(w[rows, d, :, cols], src[rows, :, DS(at, CHUNK)])
                ins.then_inc(loaded[d], 1)

            for d in range(2):
                widen(0, d)
            with pool.Fori(0, NCHUNK - 1) as c:
                for d in range(2):
                    pool.wait_ge(pe_done[d], NS * c + AT["KG"] + 1)
                    widen(c + 1, d)

        @block.tensor
        def _(pe):
            def after(c, d, name):
                e, n = ORD[name]
                pe.wait_ge((by_dve if e == "v" else by_act)[d], 1 + PER[e] * c + n)

            with pe.Fori(0, NCHUNK) as c:
                def each(name, d, parts):
                    n = AT[name]
                    for p in range(PAIRS):
                        for cols, products in parts(p):
                            for j, (lhs, rhs) in enumerate(products):
                                mm = nc.tensor.matmul(banks[:, d, n % 4, p, cols], lhs, rhs,
                                                      start=(j == 0), stop=(j == len(products) - 1))
                    mm.then_inc(pe_done[d], 1)

                full, left, right = slice(0, P), slice(0, HEAD), slice(HEAD, P)
                stack = consts("stack")
                both = (0, 1)
                for d in both:
                    at = chunk(c, d)
                    pe.wait_ge(loaded[d], c + 1)
                    pe.wait_ge(by_act[d], 1 + PER["a"] * c)
                    pe.wait_ge(by_dve[d], 1 + PER["v"] * c)
                    each("LbT", d, lambda p: [(full, [(b_w[:, d, p], ar[:, d, :, p, DS(at, CHUNK)])])])
                    each("LkT", d, lambda p: [(full, [(k_w[:, d, p], ar[:, d, :, p, DS(at, CHUNK)])])])
                    each("Lb", d, lambda p: [(left, [(a_w[:, d, p], bk[:, d, 0, p, DS(at, CHUNK)])]),
                                             (right, [(a_w[:, d, p], stack)])])
                    each("VB", d, lambda p: [(left, [(v_w[:, d, p], stack)]), (right, [(b_w[:, d, p], stack)])])
                for d in both:
                    after(c, d, "LbT")
                    after(c, d, "LkT")
                    after(c, d, "VB")
                    each("KG", d, lambda p: [(left, [(k_w[:, d, p], stack)]), (right, [(LkT[:, d, p], V[:, d, p])])])
                for d in both:
                    after(c, d, "Lb")
                    each("D2", d, lambda p: [(full, [(DT[:, d, p], Dm[:, d, p])])])
                    each("D2T", d, lambda p: [(full, [(Dm[:, d, p], DT[:, d, p])])])
                for d in both:
                    after(c, d, "D2")
                    each("R2", d, lambda p: [(full, [(D2[:, d, p], R1[:, d, p])])])
                    after(c, d, "D2T")
                    each("D4", d, lambda p: [(full, [(D2T[:, d, p], D2[:, d, p])])])
                    each("D4T", d, lambda p: [(full, [(D2[:, d, p], D2T[:, d, p])])])
                for d in both:
                    after(c, d, "R2")
                    after(c, d, "D4")
                    each("R3", d, lambda p: [(full, [(D4[:, d, p], R2[:, d, p])])])
                    after(c, d, "D4T")
                    each("D8", d, lambda p: [(full, [(D4T[:, d, p], D4[:, d, p])])])
                for d in both:
                    after(c, d, "R3")
                    after(c, d, "D8")
                    each("R4", d, lambda p: [(full, [(D8[:, d, p], R1[:, d, p])])])
                for d in both:
                    after(c, d, "R4")
                    each("N", d, lambda p: [(full, [(R2[:, d, p], E[:, d, p])])])
                    each("NT", d, lambda p: [(full, [(E[:, d, p], R2[:, d, p])])])
                    after(c, d, "KG")
                    each("X1", d, lambda p: [(full, [(R2[:, d, p], X[:, d, p])])])
                for d in both:
                    after(c, d, "NT")
                    each("N2T", d, lambda p: [(full, [(N[:, d, p], NT[:, d, p])])])
                for d in both:
                    after(c, d, "N2T")
                    each("X2", d, lambda p: [(full, [(N2T[:, d, p], X1[:, d, p])])])
                for d in both:
                    after(c, d, "X2")
                    each("Y", d, lambda p: [(full, [(NT[:, d, p], X2[:, d, p])])])
                for d in both:
                    pe.wait_ge(by_act[d], 1 + PER["a"] * c + WIDE_Y)
                    each("MR", d, lambda p: [(left, [(Aw[:, d, p], B[:, d, p])]), (right, [(Aw[:, d, p], PbT[:, d, p])])])
                for d in both:
                    after(c, d, "MR")
                    pe.wait_ge(by_act[d], 1 + PER["a"] * c + WIDE_M)
                    pe.wait_ge(sw_done[d], c + 1)
                    each("out", d, lambda p: [(left, [(Sw[:, d, p], RT[:, d, p]), (Uw[:, d, p], PbT[:, d, p]),
                                                      (Vw[:, d, p], PkT[:, d, p])])])
                    each("S", d, lambda p: [(left, [(MTw[:, d, p], S[:, d, p]), (Bw[:, d, p], Y[:, d, p, HEAD:P]),
                                                    (Kw[:, d, p], V[:, d, p])])])

        @block.scalar
        def _(act):
            for d in range(2):
                act.sem_inc(by_act[d], 1)
            with act.Fori(0, NCHUNK) as c:
                def ready(d, name):
                    act.wait_ge(pe_done[d], NS * c + AT[name] + 1)

                def bank(d, name):
                    return banks[:, d, AT[name] % 4]

                def wide(dst, src, d):
                    for rows, cols in halves:
                        ins = nc.scalar.copy(dst[rows, d, :, cols], src[rows])
                    return ins

                def plain(dst, name, d):
                    ready(d, name)
                    nc.scalar.copy(dst[:, d], bank(d, name)).then_inc(by_act[d], 1)

                both = (0, 1)
                for d in both:
                    ready(d, "VB")
                    b = bank(d, "VB")
                    nc.scalar.copy(V[:, d], b[:, :, 0:HEAD])
                    nc.scalar.copy(B[:, d], b[:, :, HEAD:P])
                    wide(Vw, b[:, :, 0:HEAD], d)
                    wide(Bw, b[:, :, HEAD:P], d).then_inc(by_act[d], 1)
                for d in both:
                    ready(d, "KG")
                    b = bank(d, "KG")
                    wide(Kw, b[:, :, 0:HEAD], d)
                    nc.scalar.copy(X[:, d, :, HEAD:P], b[:, :, HEAD:P]).then_inc(by_act[d], 1)
                for d in both:
                    plain(D2, "D2", d)
                    plain(D2T, "D2T", d)
                for d in both:
                    plain(D4, "D4", d)
                    plain(D4T, "D4T", d)
                for d in both:
                    plain(D8, "D8", d)
                for d in both:
                    plain(N, "N", d)
                    plain(NT, "NT", d)
                    plain(X1, "X1", d)
                for d in both:
                    plain(N2T, "N2T", d)
                for d in both:
                    act.wait_ge(by_dve[d], 1 + PER["v"] * c + ORD["Y"][1])
                    wide(Aw, Y[:, d, :, 0:HEAD], d)
                    wide(Uw, Y[:, d, :, HEAD:P], d).then_inc(by_act[d], 1)
                for d in both:
                    ready(d, "MR")
                    wide(MTw, bank(d, "MR")[:, :, 0:HEAD], d).then_inc(by_act[d], 1)
                for d in both:
                    ready(d, "out")
                    nc.scalar.copy(o[:, d, :, DS(chunk(c, d), CHUNK)], bank(d, "out")[:, :, 0:HEAD]).then_inc(by_act[d], 1)
                for d in both:
                    act.wait_ge(by_dve[d], 1 + PER["v"] * c + PER["v"])
                    act.wait_ge(pe_done[d], NS * c + NS)
                    wide(Sw, S[:, d], d).then_inc(sw_done[d], 1)

        @block.vector
        def _(dve):
            for d in range(2):
                dve.sem_inc(sw_done[d], 1)
                dve.sem_inc(by_dve[d], 1)
            per_own = 2
            with dve.Fori(0, NCHUNK) as c:
                k = [0]

                def link(ins):
                    ins.then_inc(own, 1)
                    k[0] += 1
                    dve.wait_ge(own, per_own * c + k[0])

                def ready(d, name):
                    dve.wait_ge(pe_done[d], NS * c + AT[name] + 1)

                def bank(d, name):
                    return banks[:, d, AT[name] % 4]

                def spread(src):
                    return bcast(src, 2, 2)

                def mask(m, n=P):
                    m = consts(m)
                    if n == P:
                        return bcast(m, 1, PAIRS).rearrange("p a (b s) -> p a b s", b=2)
                    return bcast(m, 1, PAIRS)

                def wide(t, d):
                    return t[:, d].rearrange("p a (b s) -> p a b s", b=2)

                both = (0, 1)
                for d in both:
                    lt, l, inc = (("up", "low", "up_incl") if d == 0 else ("low", "up", "low_incl"))
                    ready(d, "LbT")
                    b = bank(d, "LbT")
                    nc.vector.tensor_tensor(wide(DT, d), spread(b[:, :, 0:HEAD]), mask(lt + "_near"), ALU.mult)
                    nc.vector.tensor_tensor(PbT[:, d], b[:, :, HEAD:P], mask(inc, HEAD), ALU.mult).then_inc(by_dve[d], 1)
                    ready(d, "LkT")
                    b = bank(d, "LkT")
                    nc.vector.tensor_tensor(wide(LkT, d), spread(b[:, :, 0:HEAD]), mask(lt + "_strict"), ALU.mult)
                    nc.vector.tensor_tensor(PkT[:, d], b[:, :, HEAD:P], mask(inc, HEAD), ALU.mult).then_inc(by_dve[d], 1)
                    dve.wait_ge(by_dve[d], 1 + PER["v"] * c + 1)
                    nc.vector.tensor_tensor(R1[:, d], DT[:, d], bcast(consts("ident"), 1, PAIRS), ALU.add)
                    ready(d, "Lb")
                    b = bank(d, "Lb")
                    nc.vector.tensor_tensor(wide(Dm, d), spread(b[:, :, 0:HEAD]), mask(l + "_near"), ALU.mult)
                    nc.vector.tensor_tensor(wide(E, d), spread(b[:, :, 0:HEAD]), mask(l + "_far"), ALU.mult)
                    nc.vector.tensor_copy(X[:, d, :, 0:HEAD], b[:, :, HEAD:P]).then_inc(by_dve[d], 1)

                for name, old, new in (("R2", R1, R2), ("R3", R2, R1), ("R4", R1, R2)):
                    for d in both:
                        ready(d, name)
                        nc.vector.tensor_tensor(new[:, d], bank(d, name), old[:, d], ALU.add).then_inc(by_dve[d], 1)
                for name, old, new in (("X2", X1, X2), ("Y", X2, Y)):
                    for d in both:
                        ready(d, name)
                        nc.vector.tensor_tensor(new[:, d], bank(d, name), old[:, d], ALU.add).then_inc(by_dve[d], 1)
                for d in both:
                    dve.wait_ge(by_act[d], 1 + PER["a"] * c + WIDE_M)
                    nc.vector.tensor_tensor(RT[:, d], bank(d, "MR")[:, :, HEAD:P],
                                            ar[:, d, 1, :, DS(chunk(c, d), CHUNK)], ALU.add).then_inc(by_dve[d], 1)
                for d in both:
                    ready(d, "S")
                    link(nc.vector.tensor_tensor(Sn[:, d], bank(d, "S")[:, :, 0:HEAD], S[:, d], ALU.add))
                    ends = bcast(w_end[:, d, DS(c if d == 0 else c * -1 + (NCHUNK - 1), 1), :].rearrange("p a b -> p (a b)"), 2, HEAD)
                    nc.vector.tensor_tensor(S[:, d], Sn[:, d], ends, ALU.mult).then_inc(by_dve[d], 1)
                assert k[0] == per_own


def pool_branch(nc, p, pool_w, inv_counts, scale, y_dram):
    pad = max(WINDOWS) // 2
    with ExitStack() as ctx:
        signal = Signals(nc, ctx)
        L = T + 2 * pad
        wide = ctx.enter_context(nc.sbuf_tensor("pool_in", [P, 4, L], F32))
        s = ctx.enter_context(nc.sbuf_tensor("pool_sums", [P, 2, L], F32))
        pooled = ctx.enter_context(nc.sbuf_tensor("pooled", [P, 4, T], F32))
        mixed = ctx.enter_context(nc.sbuf_tensor("pool_mixed", [P, 4, T], F32))
        w_sb = ctx.enter_context(nc.sbuf_tensor("pool_w_sb", [P, 4, P], F32))
        ic = ctx.enter_context(nc.sbuf_tensor("inv_counts_sb", [P, 4, T], F32))
        out = ctx.enter_context(nc.psum_tensor("pool_out", [P, 4, T], F32))
        got = signal("pool_constants")
        padded = signal("pool_padded")
        pooled_s = signal("pool_pooled")
        mixed_s = signal("pool_products")
        scaled = signal("pool_scaled")
        stored = signal("pool_stored")
        own = signal("pool_own")
        block = ctx.enter_context(nc.Block())

        @block.sync
        def _(sp):
            sp.dma_start(w_sb[:, :, :], pool_w.rearrange("p (g n) -> p g n", g=4)).then_inc(got, 16)
            sp.dma_start(ic[:, :, :], inv_counts.rearrange("p (g n) -> p g n", g=4)).then_inc(got, 16)
            sp.wait_ge(scaled, 4)
            sp.dma_start(y_dram, mixed[:, :, :].rearrange("p g t -> p (g t)")).then_inc(stored, 16)
            sp.wait_ge(stored, 16)

        @block.scalar
        def _(act):
            act.wait_ge(own, 1)
            nc.scalar.copy(wide[:, :, pad:pad + T], p[:, B_POOL:B_POOL + 4, 1:T + 1]).then_inc(padded, 1)
            for g in range(4):
                act.wait_ge(mixed_s, g + 1)
                nc.scalar.activation(mixed[:, g], out[:, g], ACT.Copy, scale=scale[:, g:g + 1]).then_inc(scaled, 1)

        @block.vector
        def _(dve):
            o = Own(dve, own)
            o.add(nc.vector.memset(wide[:, :, :], 0.0))
            dve.wait_ge(padded, 1)
            dve.wait_ge(got, 32)
            for g, window in enumerate(WINDOWS):
                src, n, step, j = wide[:, g], L, 1, 0
                while step < window:
                    n -= step
                    dst = s[:, j]
                    o.link(nc.vector.tensor_tensor(dst[:, 0:n], src[:, 0:n], src[:, step:step + n], ALU.add))
                    src, j, step = dst, 1 - j, 2 * step
                first = pad - window // 2
                o.link(nc.vector.tensor_tensor(pooled[:, g], src[:, first:first + T], ic[:, g], ALU.mult))
                nc.vector.tensor_tensor(pooled[:, g], pooled[:, g], wide[:, g, pad:pad + T], ALU.subtract).then_inc(pooled_s, 1)

        @block.tensor
        def _(pe):
            pe.wait_ge(got, 32)
            for g in range(4):
                pe.wait_ge(pooled_s, g + 1)
                nc.tensor.matmul(out[:, g], w_sb[:, g], pooled[:, g], start=True, stop=True).then_inc(mixed_s, 1)


def gate_and_bonus(nc, q, kd_sum, g_up, r_k, consts, v, gate_dram, bonus_dram):
    with ExitStack() as ctx:
        signal = Signals(nc, ctx)
        up = ctx.enter_context(nc.sbuf_tensor("g_up_sb", [P, 2, PAIRS * P], F32))
        gate = ctx.enter_context(nc.sbuf_tensor("gate_sb", [P, PAIRS, T], F32))
        rk = ctx.enter_context(nc.sbuf_tensor("rk", [P, PAIRS, T], F32))
        out = ctx.enter_context(nc.psum_tensor("gb_out", [P, 2, PAIRS, T], F32))
        got = signal("g_up_in")
        sig = signal("gate_sigmoids")
        gates = signal("gate_products")
        sums = signal("bonus_sums")
        made = signal("gates_made")
        rks = signal("bonus_terms")
        bonuses = signal("bonuses_made")
        stored = signal("gate_bonus_stored")
        own = signal("gb_own")
        block = ctx.enter_context(nc.Block())

        @block.sync
        def _(sp):
            sp.dma_start(up[:, :, :], g_up.rearrange("p (a n) -> p a n", a=2)).then_inc(got, 16)
            sp.wait_ge(made, PAIRS)
            sp.dma_start(gate_dram, gate[:, :, :].rearrange("p a t -> p (a t)")).then_inc(stored, 16)
            sp.wait_ge(bonuses, PAIRS)
            sp.dma_start(bonus_dram, rk[:, :, :].rearrange("p a t -> p (a t)")).then_inc(stored, 16)
            sp.wait_ge(stored, 32)

        @block.scalar
        def _(act):
            nc.scalar.activation(q[:, B_GD:B_GD + 2], q[:, B_GD:B_GD + 2], ACT.Sigmoid).then_inc(sig, 1)
            nc.scalar.copy(v[:, :, :], q[:, B_V:B_V + PAIRS])
            for p in range(PAIRS):
                act.wait_ge(gates, p + 1)
                nc.scalar.copy(gate[:, p], out[:, 0, p]).then_inc(made, 1)

        @block.tensor
        def _(pe):
            pe.wait_ge(got, 16)
            pe.wait_ge(sig, 1)
            for p in range(PAIRS):
                cols = slice(p * P, (p + 1) * P)
                nc.tensor.matmul(out[:, 0, p], up[:, 0, cols], q[:, B_GD], start=True, stop=False)
                nc.tensor.matmul(out[:, 0, p], up[0:GATE_REST, 1, cols], q[0:GATE_REST, B_GD + 1],
                                 start=False, stop=True).then_inc(gates, 1)
            for p in range(PAIRS):
                pe.wait_ge(rks, p + 1)
                nc.tensor.matmul(out[:, 1, p], consts("heads"), rk[:, p], start=True, stop=True).then_inc(sums, 1)

        @block.vector
        def _(dve):
            for p in range(PAIRS):
                nc.vector.scalar_tensor_tensor(out=rk[:, p], in0=q[:, B_R + p], scalar=r_k[:, p:p + 1], in1=kd_sum[:, p],
                                               op0=ALU.mult, op1=ALU.mult).then_inc(rks, 1)
            for p in range(PAIRS):
                dve.wait_ge(sums, p + 1)
                nc.vector.tensor_tensor(rk[:, p], out[:, 1, p], q[:, B_V + p], ALU.mult).then_inc(bonuses, 1)


def head_norm(nc, o, lnw, lnb, consts, saved, y):
    with ExitStack() as ctx:
        signal = Signals(nc, ctx)
        c = ctx.enter_context(nc.sbuf_tensor("centred", [P, PAIRS, T], F32))
        sq = ctx.enter_context(nc.sbuf_tensor("centred_sq", [P, PAIRS, T], F32))
        gate = ctx.enter_context(nc.sbuf_tensor("gate_again", [P, PAIRS, T], F32))
        bonus = ctx.enter_context(nc.sbuf_tensor("bonus_again", [P, PAIRS, T], F32))
        epst = ctx.enter_context(nc.sbuf_tensor("gn_eps", [P, 1], F32))
        out = ctx.enter_context(nc.psum_tensor("gn_out", [P, 2, PAIRS, T], F32))
        got = signal("saved_in")
        added = signal("directions_added")
        means = signal("head_means")
        squares = signal("head_squares")
        variances = signal("head_variances")
        roots = signal("head_roots")
        own = signal("gn_own")
        block = ctx.enter_context(nc.Block())

        @block.sync
        def _(sp):
            for dst, src in ((gate[:, :, :], saved[0]), (bonus[:, :, :], saved[1]), (y[:, PAIRS:2 * PAIRS], saved[2])):
                sp.dma_start(dst, src.rearrange("p (a t) -> p a t", a=PAIRS)).then_inc(got, 16)
            sp.wait_ge(got, 48)

        @block.tensor
        def _(pe):
            for p in range(PAIRS):
                pe.wait_ge(added, p + 1)
                nc.tensor.matmul(out[:, 0, p], consts("heads"), o[:, 0, p], start=True, stop=True).then_inc(means, 1)
            for p in range(PAIRS):
                pe.wait_ge(squares, p + 1)
                nc.tensor.matmul(out[:, 1, p], consts("heads"), sq[:, p], start=True, stop=True).then_inc(variances, 1)

        @block.scalar
        def _(act):
            act.wait_ge(own, 1)
            for p in range(PAIRS):
                act.wait_ge(variances, p + 1)
                nc.scalar.activation(sq[:, p], out[:, 1, p], ACT.Sqrt, bias=epst[:, 0:1], scale=1.0 / HEAD).then_inc(roots, 1)

        @block.vector
        def _(dve):
            k = Own(dve, own)
            k.add(nc.vector.memset(epst[:, :], GN_EPS))
            for p in range(PAIRS):
                nc.vector.tensor_tensor(o[:, 0, p], o[:, 0, p], o[:, 1, p], ALU.add).then_inc(added, 1)
            for p in range(PAIRS):
                dve.wait_ge(means, p + 1)
                k.link(nc.vector.scalar_tensor_tensor(out=c[:, p], in0=out[:, 0, p], scalar=-1.0 / HEAD, in1=o[:, 0, p],
                                                      op0=ALU.mult, op1=ALU.add))
                nc.vector.tensor_tensor(sq[:, p], c[:, p], c[:, p], ALU.mult).then_inc(squares, 1)
            dve.wait_ge(got, 48)
            for p in range(PAIRS):
                dve.wait_ge(roots, p + 1)
                k.link(nc.vector.reciprocal(o[:, 0, p], sq[:, p]))
                k.link(nc.vector.tensor_tensor(c[:, p], c[:, p], o[:, 0, p], ALU.mult))
                k.link(nc.vector.scalar_tensor_tensor(out=c[:, p], in0=c[:, p], scalar=lnw[:, p:p + 1], in1=bonus[:, p],
                                                      op0=ALU.mult, op1=ALU.add))
                nc.vector.scalar_tensor_tensor(out=y[:, p], in0=c[:, p], scalar=lnb[:, p:p + 1], in1=gate[:, p],
                                               op0=ALU.add, op1=ALU.mult)



def turn(nc, tag, pairs, ident, width=P):
    groups = len(pairs)
    with ExitStack() as ctx:
        signal = Signals(nc, ctx)
        out = ctx.enter_context(nc.psum_tensor(f"{tag}_turned", [P, 4, 4, P], F32))
        turned = signal(f"{tag}_turned_s")
        taken = [signal(f"{tag}_taken{e}") for e in range(2)]
        block = ctx.enter_context(nc.Block())

        @block.tensor
        def _(pe):
            for g, (srcs, _) in enumerate(pairs):
                if g >= 4:
                    pe.wait_ge(taken[g % 2], (g - 4) // 2 + 1)
                for j, s in enumerate(srcs):
                    mm = nc.tensor.transpose(out[:, g % 4, j, :], s, ident)
                mm.then_inc(turned, 1)

        def take(e):
            def body(eng):
                for g in range(e, groups, 2):
                    eng.wait_ge(turned, g + 1)
                    dst = pairs[g][1]
                    src = out[:, g % 4, :, 0:dst.shape[-1]]
                    (nc.scalar.copy if e else nc.vector.tensor_copy)(dst, src).then_inc(taken[e], 1)
            return body

        block.vector(take(0))
        block.scalar(take(1))


SLOTS_IN_GROUP = 2
GROUPS = 4
ROUND = SLOTS_IN_GROUP * GROUPS
SEGMENTS = 8
ID_SLOTS = 16


def peer(nc, h_tok, qT, keys, consts, u_tab, v_tab):
    with ExitStack() as ctx:
        signal = Signals(nc, ctx)

        def sb(name, *shape, dt=F32):
            return ctx.enter_context(nc.sbuf_tensor(name, [P, *shape], dt))

        kT = sb("keys_sb", 2 * PH, P)
        s = sb("key_scores", 2 * PH, N_KEYS)
        s2 = sb("key_scores2", 2 * PH, N_KEYS)
        val = sb("key_vals", PH, 2, TOPK)
        ix = sb("key_idx", PH, 2, TOPK, dt=U32)
        ixf = sb("key_idxf", PH, 2, TOPK)
        cand = sb("cand", PH, TOPK, TOPK)
        cand2 = sb("cand2", PH, TOPK, TOPK)
        sc = sb("cand_vals", PH, TOPK)
        pos = sb("cand_pos", PH, TOPK, dt=U32)
        part = sb("cand_part", 2, PH, TOPK, dt=U32)
        partf = sb("cand_partf", 2, PH, TOPK)
        pick = sb("pick", 2, PH, TOPK)
        flat = sb("flat_idx", SLOTS)
        ssum = sb("gate_sum", PH)
        rsum = sb("gate_rsum", PH)
        e = sb("gate_e", PH, TOPK)
        idx = sb("expert_idx", TT, SLOTS, dt=U32)
        gate = sb("expert_gate", TT, SLOTS)
        u = sb("u_rows", ROUND, D)
        v = sb("v_rows", ROUND, D)
        ids = sb("expert_ids", 2, ID_SLOTS, dt=U32)
        dot = sb("expert_dots", ROUND)
        act_ = sb("expert_acts", ROUND)
        diag = sb("weight_diagonals", ROUND, P)
        h_now = sb("h_now", D)
        zero = sb("zero_weights", P)
        scores = ctx.enter_context(nc.psum_tensor("score_out", [P, 2 * PH, N_KEYS], F32))
        total = ctx.enter_context(nc.psum_tensor("expert_total", [P, 2, T], F32))

        keys_in, scored, copied, routed, shifted, exped, own, pace = map(signal, (
            "keys_in", "scores_ready", "scores_copied", "tile_routed", "gate_shifted", "gate_exped", "route_own", "pace"))
        u_in = [signal(f"u_rows_in{b}") for b in range(GROUPS)]
        v_in = [signal(f"v_rows_in{b}") for b in range(GROUPS)]
        h_ready, dots, gelus, diagonals, used, ids_out, tile_done, tile_out, zeroed, pace_p = map(signal, (
            "h_now_ready", "dots_ready", "gelus_ready", "diagonals_ready", "rows_used", "ids_laid_out",
            "tile_summed", "tile_stored", "zero_ready", "pace_pool"))
        rounds = SLOTS // ROUND
        per_segment = rounds // SEGMENTS
        groups = SLOTS // SLOTS_IN_GROUP
        block = ctx.enter_context(nc.Block())

        @block.sync
        def _(sp):
            sp.dma_start(kT[:, :, :], keys.rearrange("p (a n) -> p a n", n=P)).then_inc(keys_in, 16)

        @block.gpsimd
        def _(pool):
            halves = 2
            per_half = ID_SLOTS // SLOTS_IN_GROUP
            pool.sem_inc(used, GROUPS)
            with pool.Fori(0, TT) as t:
                hold(pool, routed, t + 2, pace_p)
                with pool.Fori(0, SLOTS // (halves * ID_SLOTS)) as r:
                    for b in range(halves):
                        n = t * (SLOTS // ID_SLOTS) + r * halves + b
                        nc.gpsimd.tensor_copy(ids[:, b], idx[:, :, :].rearrange("p t s -> p (t s)")[:, DS(n * ID_SLOTS, ID_SLOTS)]
                                              ).then_inc(ids_out, 1)
                        hold(pool, ids_out, n + 1, pace_p)
                        for k in range(per_half):
                            g = n * per_half + k
                            hold(pool, used, g + 1, pace_p)
                            first = k % GROUPS * SLOTS_IN_GROUP
                            for tab, rows, sem in ((u_tab, u, u_in), (v_tab, v, v_in)):
                                for j in range(SLOTS_IN_GROUP):
                                    at = k * SLOTS_IN_GROUP + j
                                    nc.gpsimd.indirect_dma_start(
                                        out=rows[:, first + j], out_offset=None, in_=tab,
                                        in_offset=bass.IndirectOffsetOnAxis(ap=ids[:, b, at:at + 1], axis=0)
                                    ).then_inc(sem[k % GROUPS], 16)

        @block.tensor
        def _(pe):
            def score(t):
                for j in range(2 * PH):
                    mm = nc.tensor.matmul(scores[:, j], qT[:, j, t * P:(t + 1) * P], kT[:, j], start=True, stop=True)
                mm.then_inc(scored, 1)

            def add_zero(**flags):
                for half in range(2):
                    mm = nc.tensor.matmul(total[:, half], zero[:, :], consts("reset"), **flags)
                return mm

            pe.wait_ge(keys_in, 16)
            score(0)
            pe.wait_ge(zeroed, 1)
            for t in range(TT):
                if t + 1 < TT:
                    pe.wait_ge(copied, t + 1)
                    score(t + 1)
                if t:
                    pe.wait_ge(tile_out, t)
                add_zero(start=True, stop=False)
                with pe.Fori(0, rounds) as r:
                    for b in range(GROUPS):
                        pe.wait_ge(diagonals, r * GROUPS + (t * groups + b + 1))
                        pe.wait_ge(v_in[b], (r + (t * rounds + 1)) * (16 * SLOTS_IN_GROUP))
                        for j in range(SLOTS_IN_GROUP):
                            at = b * SLOTS_IN_GROUP + j
                            for half in range(2):
                                mm = nc.tensor.matmul(total[:, half], diag[:, at], v[:, at, half * T:(half + 1) * T],
                                                      start=False, stop=False)
                        mm.then_inc(used, 1)
                add_zero(start=False, stop=True).then_inc(tile_done, 1)

        @block.scalar
        def _(act):
            def take_scores(t):
                act.wait_ge(scored, t + 1)
                for j in range(0, 2 * PH, 4):
                    ins = nc.scalar.copy(s[:, j:j + 4], scores[:, j:j + 4])
                ins.then_inc(copied, 1)

            def exponentials(t):
                act.wait_ge(shifted, t + 1)
                nc.scalar.activation(e[:, :, :], e[:, :, :], ACT.Exp).then_inc(exped, 1)

            def this_h(t):
                nc.scalar.copy(h_now[:, :], h_tok[:, DS(t, 1), :].rearrange("p a d -> p (a d)")).then_inc(h_ready, 1)

            def gelu(t, segment, n):
                with act.Fori(0, per_segment * n) as i:
                    for b in range(GROUPS):
                        g = t * groups + i * GROUPS + (segment * per_segment * GROUPS + b)
                        act.wait_ge(dots, g + 1)
                        at = slice(b * SLOTS_IN_GROUP, (b + 1) * SLOTS_IN_GROUP)
                        nc.scalar.activation(act_[:, at], dot[:, at], ACT.Gelu).then_inc(gelus, 1)

            def store(t):
                hold(act, tile_done, t + 1, pace_p)
                nc.scalar.copy(h_tok[:, DS(t, 1), :].rearrange("p a (b d) -> p (a b) d", b=2), total[:, :, :]).then_inc(tile_out, 1)

            take_scores(0)
            exponentials(0)
            with act.Fori(0, TT - 1) as t:
                this_h(t)
                act.wait_ge(routed, t + 2)
                take_scores(t + 1)
                gelu(t, 0, SEGMENTS - 1)
                exponentials(t + 1)
                gelu(t, SEGMENTS - 1, 1)
                store(t)
            this_h(TT - 1)
            gelu(TT - 1, 0, SEGMENTS)
            store(TT - 1)

        @block.vector
        def _(dve):
            a = nc.vector
            per = 16
            lists = [(h, p) for h in range(PH) for p in range(2)]
            hots = ((0, cand), (1, cand2))

            def row(x, h):
                return x[:, h].rearrange("p a b -> p (a b)")

            def route(t, piece):
                n = [(0, 1, 2, 4, 6, 7, 9, 12)[piece]]

                def step(ins):
                    ins.then_inc(own, 1)
                    n[0] += 1
                    hold(dve, own, t * per + n[0], pace)

                if piece == 0:
                    hold(dve, copied, t + 1, pace)
                    for h, p in lists:
                        ins = a.max(val[:, h, p, 0:8], s[:, 2 * h + p])
                    step(ins)
                elif piece == 1:
                    for h, p in lists:
                        a.max_index(ix[:, h, p, 0:8], val[:, h, p, 0:8], s[:, 2 * h + p])
                        ins = a.match_replace(s2[:, 2 * h + p], val[:, h, p, 0:8], s[:, 2 * h + p], GONE)
                    step(ins)
                elif piece == 2:
                    for h, p in lists:
                        ins = a.max(val[:, h, p, 8:16], s2[:, 2 * h + p])
                    step(ins)
                    for h, p in lists:
                        ins = a.max_index(ix[:, h, p, 8:16], val[:, h, p, 8:16], s2[:, 2 * h + p])
                    step(ins)
                elif piece == 3:
                    a.tensor_copy(ixf[:, :, :, :], ix[:, :, :, :])
                    step(a.tensor_tensor(cand[:, :, :, :], bcast(val[:, :, 0, :], 3, TOPK), bcast(val[:, :, 1, :], 2, TOPK), ALU.add))
                    for h in range(PH):
                        ins = a.max(sc[:, h, 0:8], row(cand, h))
                    step(ins)
                elif piece == 4:
                    for h in range(PH):
                        a.max_index(pos[:, h, 0:8], sc[:, h, 0:8], row(cand, h))
                        ins = a.match_replace(row(cand2, h), sc[:, h, 0:8], row(cand, h), GONE)
                    step(ins)
                elif piece == 5:
                    for h in range(PH):
                        ins = a.max(sc[:, h, 8:16], row(cand2, h))
                    step(ins)
                    a.tensor_tensor(e[:, :, :], sc[:, :, :], bcast(sc[:, :, 0], 2, TOPK), ALU.subtract).then_inc(shifted, 1)
                    for h in range(PH):
                        ins = a.max_index(pos[:, h, 8:16], sc[:, h, 8:16], row(cand2, h))
                    step(ins)
                elif piece == 6:
                    a.tensor_scalar(part[:, 0], pos[:, :, :], 4, None, ALU.logical_shift_right)
                    step(a.tensor_scalar(part[:, 1], pos[:, :, :], 15, None, ALU.bitwise_and))
                    step(a.tensor_copy(partf[:, :, :, :], part[:, :, :, :]))
                    slot = bcast(bcast(consts("slot"), 1, TOPK), 1, PH)
                    for p, hot in hots:
                        ins = a.tensor_tensor(hot[:, :, :, :], bcast(partf[:, p], 3, TOPK), slot, ALU.is_equal)
                    step(ins)
                else:
                    for p, hot in hots:
                        ins = a.tensor_tensor(hot[:, :, :, :], hot[:, :, :, :], bcast(ixf[:, :, p, :], 2, TOPK), ALU.mult)
                    step(ins)
                    for p, hot in hots:
                        ins = a.tensor_reduce(pick[:, p], hot[:, :, :, :], AX.X, ALU.add)
                    hold(dve, exped, t + 1, pace)
                    step(a.tensor_reduce(ssum[:, :], e[:, :, :], AX.X, ALU.add))
                    a.reciprocal(rsum[:, :], ssum[:, :])
                    step(a.scalar_tensor_tensor(out=flat[:, :], in0=pick[:, 0].rearrange("p a b -> p (a b)"), scalar=float(N_KEYS),
                                                in1=pick[:, 1].rearrange("p a b -> p (a b)"), op0=ALU.mult, op1=ALU.add))
                    a.tensor_copy(idx[:, DS(t, 1), :].rearrange("p a s -> p (a s)"), flat[:, :])
                    step(a.tensor_tensor(gate[:, DS(t, 1), :].rearrange("p a (h k) -> p (a h) k", k=TOPK), e[:, :, :],
                                         bcast(rsum[:, :], 2, TOPK), ALU.mult))
                    assert n[0] == per, n
                    dve.sem_inc(routed, 1)
                assert n[0] == (1, 2, 4, 6, 7, 9, 12, 16)[piece], (piece, n)

            def segment(t, k, n):
                with dve.Fori(0, per_segment * n) as i:
                    r = t * rounds + i + k * per_segment
                    for b in range(GROUPS + 1):
                        if b < GROUPS:
                            dve.wait_ge(u_in[b], (r + 1) * (16 * SLOTS_IN_GROUP))
                            for j in range(SLOTS_IN_GROUP):
                                at = b * SLOTS_IN_GROUP + j
                                ins = a.tensor_tensor_reduce(out=u[:, at], in0=u[:, at], in1=h_now[:, :], scale=1.0, scalar=0.0,
                                                             op0=ALU.mult, op1=ALU.add, accum_out=dot[:, at:at + 1])
                            ins.then_inc(dots, 1)
                        if b > 0:
                            g = r * GROUPS + (b - 1)
                            dve.wait_ge(gelus, g + 1)
                            for j in range(SLOTS_IN_GROUP):
                                at = (b - 1) * SLOTS_IN_GROUP + j
                                ins = a.tensor_scalar(diag[:, at], consts("ident"), act_[:, at:at + 1],
                                                      gate[:, :, :].rearrange("p t s -> p (t s)")[:, DS(r * ROUND + at, 1)],
                                                      ALU.mult, ALU.mult)
                            ins.then_inc(diagonals, 1)

            dve.sem_inc(routed, 1)
            a.memset(zero[:, :], 0.0).then_inc(zeroed, 1)
            for piece in range(8):
                route(0, piece)
            with dve.Fori(0, TT - 1) as t:
                hold(dve, h_ready, t + 1, pace)
                for k in range(SEGMENTS):
                    segment(t, k, 1)
                    route(t + 1, k)
            hold(dve, h_ready, TT, pace)
            segment(TT - 1, 0, SEGMENTS)


def add_turned(nc, tag, x, tok, ident):
    with ExitStack() as ctx:
        signal = Signals(nc, ctx)
        out = ctx.enter_context(nc.psum_tensor(f"{tag}_back", [P, 4, T], F32))
        turned = signal(f"{tag}_back_turned")
        added = signal(f"{tag}_back_added")
        block = ctx.enter_context(nc.Block())

        @block.tensor
        def _(pe):
            for k in range(KD):
                if k >= 4:
                    pe.wait_ge(added, k - 3)
                for t in range(TT):
                    mm = nc.tensor.transpose(out[:, k % 4, t * P:(t + 1) * P], tok[:, t, k * P:(k + 1) * P], ident)
                mm.then_inc(turned, 1)

        @block.vector
        def _(dve):
            for k in range(KD):
                dve.wait_ge(turned, k + 1)
                nc.vector.tensor_tensor(x[:, k], out[:, k % 4], x[:, k], ALU.add).then_inc(added, 1)



def rope(nc, pr, swap, tables):
    with ExitStack() as ctx:
        signal = Signals(nc, ctx)
        tab = ctx.enter_context(nc.sbuf_tensor("rope_tab", [P, 2, T], F32))
        tmp = ctx.enter_context(nc.sbuf_tensor("rope_tmp", [P, 2, T], F32))
        out = ctx.enter_context(nc.psum_tensor("rope_out", [P, 2, T], F32))
        got = signal("rope_in")
        swapped = signal("rope_swapped")
        free = signal("rope_free")
        own = signal("rope_own")
        rounds = 5
        first = (C_QB, C_QI)
        block = ctx.enter_context(nc.Block())

        def blk(b, i):
            return pr[:, DS(i + first[b], 1), :].rearrange("p a t -> p (a t)")

        @block.sync
        def _(sp):
            sp.dma_start(tab[:, :, :], tables.rearrange("p (a t) -> p a t", a=2)).then_inc(got, 16)

        @block.tensor
        def _(pe):
            with pe.Fori(0, rounds) as i:
                for b in range(2):
                    pe.wait_ge(free, 2 * i + b + 1)
                    nc.tensor.matmul(out[:, b], swap, blk(b, i), start=True, stop=True).then_inc(swapped, 1)

        @block.vector
        def _(dve):
            dve.sem_inc(free, 2)
            dve.wait_ge(got, 16)
            with dve.Fori(0, rounds) as i:
                for b in range(2):
                    dve.wait_ge(swapped, 2 * i + b + 1)
                    nc.vector.tensor_tensor(tmp[:, b], out[:, b], tab[:, 1], ALU.mult).then_inc(free, 1)
                    nc.vector.tensor_tensor(blk(b, i), blk(b, i), tab[:, 0], ALU.mult).then_inc(own, 1)
                for b in range(2):
                    dve.wait_ge(own, 4 * i + 2)
                    nc.vector.tensor_tensor(blk(b, i), blk(b, i), tmp[:, b], ALU.add).then_inc(own, 1)
                dve.wait_ge(own, 4 * i + 4)


def index_mask(nc, pr, w_tok, m):
    with ExitStack() as ctx:
        signal = Signals(nc, ctx)
        score = ctx.enter_context(nc.sbuf_tensor("index_scores", [P, 3, T], F32))
        relu = ctx.enter_context(nc.sbuf_tensor("index_relu", [P, 4, T], F32))
        ws = ctx.enter_context(nc.sbuf_tensor("index_w", [P, TT, 8], F32))
        top = ctx.enter_context(nc.sbuf_tensor("index_top", [P, 3, 8], F32))
        out = ctx.enter_context(nc.psum_tensor("index_out", [P, 4, T], F32))
        dots = signal("index_dots")
        relus = signal("index_relus")
        added = signal("index_added")
        own = signal("index_own")
        pace = signal("index_pace")
        units = [(t, h) for h in range(8) for t in range(1, TT)]
        block = ctx.enter_context(nc.Block())

        @block.tensor
        def _(pe):
            for n, (t, h) in enumerate(units):
                if n >= 4:
                    pe.wait_ge(relus, n - 3)
                rows = slice(HEAD * (h % 2), HEAD * (h % 2) + HEAD)
                keys = P * (t + 1)
                nc.tensor.matmul(out[:, n % 4, 0:keys], pr[rows, C_QI + h // 2, t * P:(t + 1) * P], pr[rows, C_KI, 0:keys],
                                 start=True, stop=True).then_inc(dots, 1)

        @block.scalar
        def _(act):
            for n, (t, h) in enumerate(units):
                act.wait_ge(dots, n + 1)
                if n >= 4:
                    act.wait_ge(added, n - 3)
                keys = P * (t + 1)
                nc.scalar.activation(relu[:, n % 4, 0:keys], out[:, n % 4, 0:keys], ACT.Relu, scale=HEAD ** -0.5).then_inc(relus, 1)

        @block.vector
        def _(dve):
            a = nc.vector
            k = Own(dve, own)
            a.memset(score[:, :, :], 0.0)
            a.memset(m[:, :, :], 0.0)
            k.link(a.tensor_scalar(ws[:, :, :], w_tok[:, :, 0:8], 8 ** -0.5, None, ALU.mult))
            a.memset(m[0:HEAD, 0, HEAD:P], NEG)
            for n, (t, h) in enumerate(units):
                keys = P * (t + 1)
                dve.wait_ge(relus, n + 1)
                if n >= 3:
                    dve.wait_ge(added, n - 2)
                a.scalar_tensor_tensor(out=score[:, t - 1, 0:keys], in0=relu[:, n % 4, 0:keys], scalar=ws[:, t, h:h + 1],
                                       in1=score[:, t - 1, 0:keys], op0=ALU.mult, op1=ALU.add).then_inc(added, 1)
            dve.wait_ge(added, len(units))
            for t in range(1, TT):
                ins = a.memset(score[0:HEAD, t - 1, P * (t + 1) - HEAD:P * (t + 1)], NEG)
            k.link(ins)
            base = k.n
            with dve.Fori(0, IDX_TOPK // 8) as i:
                for t in range(1, TT):
                    ins = a.max(top[:, t - 1], score[:, t - 1, 0:P * (t + 1)])
                ins.then_inc(own, 1)
                hold(dve, own, 2 * i + base + 1, pace)
                for t in range(1, TT):
                    s = score[:, t - 1, 0:P * (t + 1)]
                    ins = a.match_replace(s, top[:, t - 1], s, GONE)
                ins.then_inc(own, 1)
                hold(dve, own, 2 * i + base + 2, pace)
            k.n += 2 * (IDX_TOPK // 8)
            for t in range(1, TT):
                s = score[:, t - 1, 0:P * (t + 1)]
                ins = a.tensor_scalar(s, s, GONE, -1.0, ALU.is_equal, ALU.add)
            k.link(ins)
            for t in range(1, TT):
                s = score[:, t - 1, 0:P * (t + 1)]
                a.tensor_scalar(m[:, t, 0:P * (t + 1)], s, -NEG, None, ALU.mult)


def attention(nc, tag, q_of, k_of, v_of, bias_of, ident, o):
    SB, PB = 4, 4
    with ExitStack() as ctx:
        signal = Signals(nc, ctx)
        qs = ctx.enter_context(nc.sbuf_tensor(f"{tag}_q", [P, T], F32))
        ks = ctx.enter_context(nc.sbuf_tensor(f"{tag}_k", [P, T], F32))
        vs = ctx.enter_context(nc.sbuf_tensor(f"{tag}_v", [P, TT, P], F32))
        prob = ctx.enter_context(nc.sbuf_tensor(f"{tag}_p", [P, SB, T], F32))
        pT = ctx.enter_context(nc.sbuf_tensor(f"{tag}_pT", [P, 2, T], F32))
        mx = ctx.enter_context(nc.sbuf_tensor(f"{tag}_mx", [P, SB], F32))
        nm = ctx.enter_context(nc.sbuf_tensor(f"{tag}_nm", [P, SB], F32))
        sm = ctx.enter_context(nc.sbuf_tensor(f"{tag}_sm", [P, SB], F32))
        rc = ctx.enter_context(nc.sbuf_tensor(f"{tag}_rc", [P, SB], F32))
        s_ps = ctx.enter_context(nc.psum_tensor(f"{tag}_s_ps", [P, PB, T], F32))
        t_ps = ctx.enter_context(nc.psum_tensor(f"{tag}_t_ps", [P, 2, T], F32))
        o_ps = ctx.enter_context(nc.psum_tensor(f"{tag}_o_ps", [P, T], F32))

        def sem(name):
            return signal(f"{tag}_{name}")

        qk_in, v_in, scored, biased, shifted, exped, normed = map(
            sem, ("qk_in", "v_in", "scored", "biased", "shifted", "exped", "normed"))
        turned, taken, summed, stored, own, pace = map(sem, ("turned", "taken", "summed", "stored", "own", "pace"))
        units = [(hh, t) for hh in range(2) for t in range(TT)]
        NU = len(units)
        block = ctx.enter_context(nc.Block())

        @block.gpsimd
        def _(pool):
            def load(i, after=None):
                if after is not None:
                    pool.wait_ge(scored, NU * after + NU)
                nc.gpsimd.tensor_copy(qs[:, :], q_of(i))
                nc.gpsimd.tensor_copy(ks[:, :], k_of(i)).then_inc(qk_in, 1)
                if after is not None:
                    hold(pool, summed, NU * after + NU + 2, pace)
                nc.gpsimd.tensor_copy(vs[:, :, :], v_of(i)).then_inc(v_in, 1)

            load(0)
            with pool.Fori(0, PAIRS - 1) as i:
                load(i + 1, i)

        @block.tensor
        def _(pe):
            pe.sem_inc(turned, SB)
            pe.sem_inc(summed, 2)
            with pe.Fori(0, PAIRS) as i:
                pe.wait_ge(qk_in, i + 1)
                for step in range(NU + 3):
                    if step < NU:
                        u = step
                        hh, t = units[u]
                        rows = slice(HEAD * hh, HEAD * hh + HEAD)
                        keys = P * (t + 1)
                        pe.wait_ge(biased, NU * i + u + 1)
                        nc.tensor.matmul(s_ps[:, u % PB, 0:keys],
                                         qs[rows, t * P:(t + 1) * P], ks[rows, 0:keys],
                                         start=True, stop=True).then_inc(scored, 1)
                    if 2 <= step < NU + 2:
                        u = step - 2
                        hh, t = units[u]
                        pe.wait_ge(normed, NU * i + u + 1)
                        pe.wait_ge(taken, NU * i + u + 1)
                        for j in range(t + 1):
                            mm = nc.tensor.transpose(t_ps[:, u % 2, j * P:(j + 1) * P], prob[:, u % SB, j * P:(j + 1) * P], ident)
                        mm.then_inc(turned, 1)
                    if 3 <= step:
                        u = step - 3
                        hh, t = units[u]
                        rows = slice(HEAD * hh, HEAD * hh + HEAD)
                        if u == 0:
                            pe.wait_ge(v_in, i + 1)
                            pe.wait_ge(stored, i + 1)
                        pe.wait_ge(taken, NU * i + u + 3)
                        for j in range(t + 1):
                            mm = nc.tensor.matmul(o_ps[rows, t * P:(t + 1) * P], vs[:, j, rows], pT[:, u % 2, j * P:(j + 1) * P],
                                                  start=(j == 0), stop=(j == t))
                        mm.then_inc(summed, 1)

        @block.scalar
        def _(act):
            act.sem_inc(taken, 2)
            act.sem_inc(stored, 1)
            with act.Fori(0, PAIRS) as i:
                for step in range(NU + 2):
                    if step < NU:
                        u = step
                        hh, t = units[u]
                        keys = P * (t + 1)
                        act.wait_ge(shifted, NU * i + u + 1)
                        nc.scalar.activation(prob[:, u % SB, 0:keys], prob[:, u % SB, 0:keys], ACT.Exp,
                                             bias=nm[:, u % SB:u % SB + 1], accum_out=sm[:, u % SB:u % SB + 1]).then_inc(exped, 1)
                    if 2 <= step:
                        u = step - 2
                        hh, t = units[u]
                        keys = P * (t + 1)
                        act.wait_ge(turned, NU * i + u + SB + 1)
                        act.wait_ge(summed, NU * i + u + 1)
                        nc.scalar.copy(pT[:, u % 2, 0:keys], t_ps[:, u % 2, 0:keys]).then_inc(taken, 1)
                act.wait_ge(summed, NU * i + NU + 2)
                nc.scalar.copy(o[:, DS(i, 1), :].rearrange("p a t -> p (a t)"), o_ps[:, :]).then_inc(stored, 1)

        @block.vector
        def _(dve):
            dve.sem_inc(biased, PB)
            per = 2 * NU
            with dve.Fori(0, PAIRS) as i:
                n = 0
                for step in range(NU + 1):
                    if step < NU:
                        u = step
                        hh, t = units[u]
                        keys = P * (t + 1)
                        c = slice(u % SB, u % SB + 1)
                        dve.wait_ge(scored, NU * i + u + 1)
                        dve.wait_ge(turned, NU * i + u + 1)
                        nc.vector.scalar_tensor_tensor(out=prob[:, u % SB, 0:keys], in0=s_ps[:, u % PB, 0:keys],
                                                       scalar=HEAD ** -0.5, in1=bias_of(i, hh, t), op0=ALU.mult,
                                                       op1=ALU.add).then_inc(biased, 1)
                        dve.wait_ge(biased, NU * i + u + 1 + PB)
                        nc.vector.tensor_reduce(mx[:, c], prob[:, u % SB, 0:keys], AX.X, ALU.max).then_inc(own, 1)
                        n += 1
                        dve.wait_ge(own, per * i + n)
                        nc.vector.tensor_scalar(nm[:, c], mx[:, c], -1.0, None, ALU.mult).then_inc(shifted, 1)
                    if 1 <= step:
                        u = step - 1
                        hh, t = units[u]
                        keys = P * (t + 1)
                        c = slice(u % SB, u % SB + 1)
                        dve.wait_ge(exped, NU * i + u + 1)
                        nc.vector.reciprocal(rc[:, c], sm[:, c]).then_inc(own, 1)
                        n += 1
                        dve.wait_ge(own, per * i + n)
                        nc.vector.tensor_scalar(prob[:, u % SB, 0:keys], prob[:, u % SB, 0:keys], rc[:, c], None,
                                                ALU.mult).then_inc(normed, 1)
                assert n == per



def load(nc, tag, *copies):
    with ExitStack() as ctx:
        signal = Signals(nc, ctx)
        got = signal(f"{tag}_loaded")
        block = ctx.enter_context(nc.Block())

        @block.sync
        def _(sp):
            for dst, src in copies:
                sp.dma_start(dst, src).then_inc(got, 16)
            sp.wait_ge(got, 16 * len(copies))


def parts(nc, ctx, tag, blocks):
    return [ctx.enter_context(nc.sbuf_tensor(f"{tag}_{n}", [P, blocks, T], F32R)) for n in ("hi", "lo")]


def swiglu_ffn(nc, tag, x, weight, consts, w_in, w_out):
    with ExitStack() as ctx:
        a = parts(nc, ctx, f"{tag}_a", KF)
        with ExitStack() as inner:
            h = parts(nc, inner, f"{tag}_h", KD)
            rmsnorm(nc, f"{tag}_norm", x, weight, consts("ones"), RMS_EPS2, parts=h)
            silu = inner.enter_context(nc.sbuf_tensor(f"{tag}_silu", [P, 2, T], F32))
            product = inner.enter_context(nc.sbuf_tensor(f"{tag}_product", [P, 2, T], F32))
            gemm(nc, f"{tag}_in", w_in, KD, lambda b: h, 2 * KF, Swiglu(*a, silu, product))
        gemm(nc, f"{tag}_out", w_out, KF, lambda b: a, KD, AddTo(x, 0.5))


def token_groups(src, blocks, dst):
    n = dst.shape[-1]
    return [([src[:, b, t * P:(t + 1) * P] for t in range(TT)], dst[:, :, j * P:min(n, (j + 1) * P)])
            for j, b in enumerate(blocks)]


def build(nc, io):
    out = io["out"]
    gate_dram = nc.dram_tensor("gate_kept", [P, PAIRS * T], F32).ap()
    bonus_dram = nc.dram_tensor("bonus_kept", [P, PAIRS * T], F32).ap()
    pool_dram = nc.dram_tensor("pool_kept", [P, PAIRS * T], F32).ap()
    x_in = io["x"].rearrange("p (k t) -> p k t", k=KD)

    with ExitStack() as whole:
        const_sb = whole.enter_context(nc.sbuf_tensor("const_sb", [P, N_CONST], F32))
        vec_sb = whole.enter_context(nc.sbuf_tensor("vec_sb", [P, N_VEC], F32))

        def consts(name):
            at, n = C_AT[name]
            return const_sb[:, at:at + n]

        def vec(name):
            at, n = V_AT[name]
            return vec_sb[:, at:at + n]

        x = whole.enter_context(nc.sbuf_tensor("x", [P, KD, T], F32))
        load(nc, "start", (const_sb[:, :], io["consts"]), (vec_sb[:, :], io["vec"]), (x[:, :, :], x_in))
        with ExitStack() as s1:
            ar = s1.enter_context(nc.sbuf_tensor("ar", [P, 2, 2, PAIRS, T], F32))
            bk = s1.enter_context(nc.sbuf_tensor("bk", [P, 2, 2, PAIRS, T], F32))
            v = s1.enter_context(nc.sbuf_tensor("v_kept", [P, PAIRS, T], F32))
            w_end = s1.enter_context(nc.sbuf_tensor("w_end", [P, 2, NCHUNK, PAIRS], F32))
            with nc.sbuf_tensor("p_in", [P, N_IN1, T + 2], F32) as p:
                with ExitStack() as s0:
                    h = parts(nc, s0, "h1", KD)
                    rmsnorm(nc, "norm1", x, vec("norm1"), consts("ones"), RMS_EPS1, parts=h)
                    gemm(nc, "w_in", io["w_in"], KD, lambda b: h, N_IN1,
                         Keep(lambda n: p[:, DS(n, 1), 1:T + 1].rearrange("p a t -> p (a t)")))
                token_shift(nc, p, vec("mu0"), vec("mu1"))
                pool_branch(nc, p, io["pool_w"], io["inv_counts"], vec("pool_scale"), pool_dram)
                q = p[:, :, 1:T + 1]
                with nc.sbuf_tensor("kd_sum", [P, PAIRS, T], F32) as kd_sum:
                    with nc.sbuf_tensor("kk", [P, PAIRS, T], F32) as kk, nc.sbuf_tensor("lora", [P, 2, PAIRS * P], F32) as lora:
                        load(nc, "lora", (lora[:, :, :], io["lora"].rearrange("p (a n) -> p a n", a=2)))
                        rwkv_operands(nc, q, lora, vec, consts, ar, bk, kk, kd_sum, w_end)
                    gate_and_bonus(nc, q, kd_sum, io["g_up"], vec("r_k"), consts, v, gate_dram, bonus_dram)
            o = ar[:, :, 0]
            recurrence(nc, ar, bk, v, w_end, consts, o)
            y = s1.enter_context(nc.sbuf_tensor("y", [P, 2 * PAIRS, T], F32))
            head_norm(nc, o, vec("lnw"), vec("lnb"), consts, (gate_dram, bonus_dram, pool_dram), y)
            y_parts = parts(nc, s1, "y", 2 * PAIRS)
            split(nc, "y", y, *y_parts)
            gemm(nc, "w_out", io["w_out"], KD, lambda b: y_parts, KD, AddTo(x))

        with ExitStack() as s2:
            h_tok = s2.enter_context(nc.sbuf_tensor("h_tok", [P, TT, D], F32))
            qT = s2.enter_context(nc.sbuf_tensor("qT", [P, 2 * PH, T], F32))
            with ExitStack() as s0:
                h2 = s0.enter_context(nc.sbuf_tensor("h2", [P, KD, T], F32))
                h = parts(nc, s0, "h2", KD)
                rmsnorm(nc, "norm2", x, vec("norm2"), consts("ones"), RMS_EPS1, out=h2, parts=h)
                gemm(nc, "wq", io["peer_wq"], KD, lambda b: h, 2 * PH, Keep(lambda n: at_block(qT, n)))
                turn(nc, "h", token_groups(h2, range(KD), h_tok), consts("ident"))
            peer(nc, h_tok, qT, io["peer_keys"], consts, io["peer_u"], io["peer_v"])
            add_turned(nc, "peer", x, h_tok, consts("ident"))
            rmsnorm(nc, "norm_f", x, vec("norm_f"), consts("ones"), RMS_EPS1, out=x)

        swiglu_ffn(nc, "ffn1", x, vec("n1"), consts, io["ffn1_w_in"], io["ffn1_w_out"])
        with ExitStack() as s3:
            def sb(name, shape, dt=F32):
                return s3.enter_context(nc.sbuf_tensor(name, shape, dt))

            pr = sb("pr", [P, N_IN2, T])
            va, vb, wi = sb("va_tok", [P, TT, PAIRS * P]), sb("vb_tok", [P, TT, P]), sb("wi_tok", [P, TT, 8])
            oa, ob = sb("oa", [P, PAIRS, T]), sb("ob", [P, PAIRS, T])
            with ExitStack() as s0:
                h = parts(nc, s0, "h3", KD)
                rmsnorm(nc, "n2", x, vec("n2"), consts("ones"), RMS_EPS2, parts=h)
                gemm(nc, "w_in2", io["w_in_2"], KD, lambda b: h, N_IN2, Keep(lambda n: at_block(pr, n)))
            rope(nc, pr, consts("swap"), io["rope"])
            turn(nc, "values", token_groups(pr, range(C_VA, C_VA + 4), va) + token_groups(pr, [C_VB], vb)
                 + token_groups(pr, [C_WI], wi), consts("ident"))
            blk = lambda b: pr[:, b, :].rearrange("p a t -> p (a t)")
            with nc.sbuf_tensor("toeplitz", [P, 8, T], F32) as toe:
                line = io["bias_line"]
                L = line.shape[1]
                lines = nc.dram_tensor("bias_lines", [8 * P, L], F32).ap()
                load(nc, "lines", (bass.AP(lines.tensor, 0, [[P * L, 8], [L, P], [1, L]]),
                                   bass.AP(line.tensor, 0, [[L, 8], [0, P], [1, L]])))
                load(nc, "bias", (toe[:, :, :], bass.AP(lines.tensor, P - 1, [[L - 1, P], [P * L, 8], [1, T]])))
                with nc.Block() as block:
                    @block.vector
                    def _(dve):
                        nc.vector.memset(toe[0:HEAD, :, T - HEAD:T], NEG)
                attention(nc, "atta", lambda i: blk(DS(i + C_QA, 1)), lambda i: blk(DS(i + C_KA, 1)),
                          lambda i: va[:, :, DS(i * P, P)],
                          lambda i, hh, t: toe[:, DS(2 * i + hh, 1), 3 * P - P * t:T].rearrange("p a t -> p (a t)"),
                          consts("ident"), oa)
            with nc.sbuf_tensor("mask_b", [P, TT, T], F32) as m:
                index_mask(nc, pr, wi, m)
                attention(nc, "attb", lambda i: blk(DS(i + C_QB, 1)), lambda i: pr[:, C_KB, :],
                          lambda i: vb[:, :, :], lambda i, hh, t: m[:, t, 0:P * (t + 1)], consts("ident"), ob)
            merged = sb("merged", [P, KD, T])
            with ExitStack() as s0:
                a_parts, b_parts = parts(nc, s0, "oa", PAIRS), parts(nc, s0, "ob", PAIRS)
                split(nc, "oa", oa, *a_parts)
                split(nc, "ob", ob, *b_parts)
                gemm(nc, "branches", io["w_branches"], PAIRS, lambda b: b_parts if b % 2 else a_parts, 2 * KD,
                     Merge(merged, pr))
            m_parts = parts(nc, s3, "merged", KD)
            split(nc, "merged", merged, *m_parts)
            gemm(nc, "w_out2", io["w_out_2"], KD, lambda b: m_parts, KD, AddTo(x))
        swiglu_ffn(nc, "ffn2", x, vec("n3"), consts, io["ffn2_w_in"], io["ffn2_w_out"])
        rmsnorm(nc, "nf", x, vec("nf"), consts("ones"), RMS_EPS2, out=x)
        load(nc, "result", (out, x[:, :, :].rearrange("p k t -> p (k t)")))



def _shape_constants():
    n = np.arange(P)
    head, tok = n // HEAD, n % HEAD
    same = head[:, None] == head[None, :]
    near = (tok[:, None] // SUB) == (tok[None, :] // SUB)
    low = same & (tok[:, None] > tok[None, :])
    up = same & (tok[:, None] < tok[None, :])
    c = np.arange(HEAD)
    swap = np.zeros((P, P))
    for i in range(P):
        j = i % HEAD
        if j < 8:
            swap[i + 8, i] = 1
        elif j < 16:
            swap[i - 8, i] = 1
    parts = {
        "ident": np.eye(P), "ones": np.ones((P, P)), "heads": same,
        "stack": (tok[:, None] == c[None, :]), "swap": swap,
        "low_near": low & near, "low_far": low & ~near, "up_near": up & near, "up_far": up & ~near,
        "low_strict": low, "up_strict": up,
        "low_incl": tok[:, None] >= c[None, :], "up_incl": tok[:, None] <= c[None, :],
        "reset": np.broadcast_to((np.arange(T) % CHUNK != 0)[None, :], (P, T)),
        "slot": np.broadcast_to(np.arange(TOPK)[None, :], (P, TOPK)),
    }
    consts = np.concatenate([np.asarray(parts[k], np.float32) for k, _ in CONSTS], axis=1)
    t = np.arange(T)
    inv = [1.0 / (np.minimum(t + w // 2, T) - np.maximum(t - w // 2, 0)) for w in WINDOWS]
    inv_counts = np.broadcast_to(np.concatenate(inv).astype(np.float32)[None, :], (P, 4 * T))
    freq = np.power(np.float32(500000.0), -np.arange(0, 16, 2, dtype=np.float32) / np.float32(16))
    ang = (t.astype(np.float32)[:, None] * freq[None, :]).astype(np.float32)
    cos, sin = np.cos(ang).T, np.sin(ang).T
    table = np.zeros((P, 2, T), np.float32)
    table[:, 0] = 1
    for h in range(2):
        for half, sign in ((0, -1), (1, 1)):
            rows = slice(HEAD * h + 8 * half, HEAD * h + 8 * half + 8)
            table[rows, 0] = cos
            table[rows, 1] = sign * sin
    return consts, np.ascontiguousarray(inv_counts), table.reshape(P, 2 * T)


def _blocks(w):
    k, n = w.shape
    return np.ascontiguousarray(w.reshape(k // P, P, n // P, P).transpose(2, 1, 0, 3).reshape(n, k))


def _channels(a):
    return a.reshape(-1, P).T


def _widen(w, n):
    return np.concatenate([w, np.zeros((w.shape[0], n - w.shape[1]), w.dtype)], axis=1)


def _layout(inp):
    a = {k: np.asarray(v) for k, v in inp.items()}
    one = {k: v[0] for k, v in a.items() if v.ndim > 1}
    consts, inv_counts, rope = _shape_constants()
    rw = 12 * P + 2 * P + P + GATE_REST
    w_in = one["w_in"]
    w_in1 = np.concatenate([_widen(w_in[:, :rw], N_SHIFT * P), w_in[:, rw:]], axis=1)
    mu = _widen(one["shift_mu"], N_SHIFT * P)
    vectors = dict(norm1=one["norm1_w"], mu0=mu[0], mu1=mu[1], w0=one["w0"], a0=one["a0"], k_k=one["k_k"], k_a=one["k_a"],
                   r_k=one["r_k"], lnw=one["ln_x_w"], lnb=one["ln_x_b"], pool_scale=one["pool_scale"], norm2=one["norm2_w"],
                   norm_f=a["norm_f_w"], n1=one["n1_g_2"], n2=one["n2_g_2"], n3=one["n3_g_2"], nf=a["nf_g_2"])
    io = {
        "x": one["x"].T.reshape(KD, P, T).transpose(1, 0, 2).reshape(P, KD * T),
        "consts": consts, "inv_counts": inv_counts, "rope": rope,
        "vec": np.concatenate([_channels(vectors[k]) for k, _ in VECTORS], axis=1),
        "w_in": _blocks(w_in1),
        "lora": np.concatenate([one["w_up"].reshape(P, -1), one["a_up"].reshape(P, -1)], axis=1),
        "pool_w": one["pool_w"].transpose(1, 0, 2).reshape(P, 4 * P),
        "g_up": np.concatenate([one["g_up"], np.zeros((2 * P - P - GATE_REST, PAIRS * P), np.float32)]).reshape(
            2, P, PAIRS * P).transpose(1, 0, 2).reshape(P, -1),
        "w_out": _blocks(one["w_out"]),
        "peer_wq": _blocks(one["peer_wq"]),
        "peer_keys": one["peer_keys"].transpose(3, 0, 1, 2).reshape(P, -1),
        "peer_u": one["peer_u"], "peer_v": one["peer_v"],
    }
    for f in ("ffn1", "ffn2"):
        w = one[f"{f}_w_in_2"].reshape(D, 2, KF, P).transpose(0, 2, 1, 3).reshape(D, 2 * D_FF)
        io[f"{f}_w_in"] = _blocks(w)
        io[f"{f}_w_out"] = _blocks(one[f"{f}_w_out_2"])
    w = one["w_in_2"]
    sizes = (512, 512, 512, 512, 128, 128, 512, 64, 8, D, D)
    qa, ka, va, qb, kb, vb, qi, ki, wi, ga, gb = np.split(w, np.cumsum(sizes)[:-1], axis=1)
    order = [h * HEAD + c for j in range(4) for h in (j, j + 4) for c in range(HEAD)]
    io["w_in_2"] = _blocks(np.concatenate([qa, ka, va, qb[:, order], kb, vb, qi, ki, ki, _widen(wi, P), ga, gb], axis=1))
    ab = np.stack([_blocks(one["w_branch_a_2"]).reshape(KD, P, -1), _blocks(one["w_branch_b_2"][order]).reshape(KD, P, -1)], axis=1)
    io["w_branches"] = ab.reshape(2 * D, PAIRS * P)
    io["w_out_2"] = _blocks(one["w_out_2"])
    dist = np.clip(511 - np.arange(5 * P - 1), -128, 128) + 128
    io["bias_line"] = one["rel_bias_2"][:, dist]
    return {k: np.ascontiguousarray(v) for k, v in io.items()}


def kernel(**inputs):
    import concourse.bacc as _bacc
    from concourse.bass_utils import run_bass_kernel_spmd as _run

    nc = _bacc.Bacc("TRN2", target_bir_lowering=False, num_devices=1)
    arrays = _layout(inputs)
    io = {k: nc.dram_tensor(f"in_{k}", v.shape, mybir.dt.from_np(v.dtype), kind="ExternalInput").ap() for k, v in arrays.items()}
    io["out"] = nc.dram_tensor("out", (P, KD * T), F32, kind="ExternalOutput").ap()
    build(nc, io)
    r = _run(nc, [{f"in_{k}": v for k, v in arrays.items()}], core_ids=[0])
    y = r.results[0]["out"]
    return np.ascontiguousarray(y.reshape(P, KD, T).transpose(2, 1, 0).reshape(1, T, D))
```

```python
import numpy as np
from contextlib import ExitStack

import concourse.bass as bass
from concourse import mybir

F32 = mybir.dt.float32
F32R = mybir.dt.float32r
U32 = mybir.dt.uint32
ALU = mybir.AluOpType
ACT = mybir.ActivationFunctionType
AX = mybir.AxisListType

P = 128
T = 512
TT = T // P
D = 1024
KD = D // P
HEAD = 64
PAIRS = 4
CHUNK = 64
NCHUNK = T // CHUNK
SUB = 16
DECAY = float(np.exp(-0.5))
GN_EPS = 64e-5
RMS_EPS1 = 1e-5
RMS_EPS2 = 1e-6
N_KEYS = 128
TOPK = 16
PH = 8
SLOTS = PH * TOPK
D_FF = 2816
KF = D_FF // P
IDX_TOPK = 128
NEG = -1.0e30
GONE = -3.0e38
DS = bass.ds

B_R, B_K, B_V, B_WD, B_AD, B_GD, B_POOL, N_IN1 = 0, 4, 8, 12, 13, 14, 16, 20
N_SHIFT = 16
GATE_REST = 32
C_QA, C_KA, C_VA, C_QB, C_KB, C_VB, C_QI, C_KI, C_WI, C_GA, C_GB, N_IN2 = 0, 4, 8, 12, 16, 17, 18, 22, 23, 24, 32, 40
WINDOWS = (2, 4, 8, 16)

VECTORS = [("norm1", 8), ("mu0", 16), ("mu1", 16), ("w0", 8), ("a0", 8), ("k_k", 4), ("k_a", 4),
           ("r_k", 4), ("lnw", 4), ("lnb", 4), ("pool_scale", 4), ("norm2", 8), ("norm_f", 8),
           ("n1", 8), ("n2", 8), ("n3", 8), ("nf", 8)]
V_AT, _at = {}, 0
for _name, _n in VECTORS:
    V_AT[_name] = (_at, _n)
    _at += _n
N_VEC = _at

CONSTS = [("ident", 128), ("ones", 128), ("heads", 128), ("swap", 128),
          ("low_near", 128), ("low_far", 128), ("up_near", 128), ("up_far", 128),
          ("low_strict", 128), ("up_strict", 128), ("low_incl", 64), ("up_incl", 64),
          ("reset", 512), ("slot", 16)]
C_AT, _at = {}, 0
for _name, _n in CONSTS:
    C_AT[_name] = (_at, _n)
    _at += _n
N_CONST = _at


class Signals:

    def __init__(self, nc, ctx):
        self.nc, self.used = nc, []
        ctx.callback(self.close)

    def __call__(self, name):
        self.used.append(self.nc.alloc_semaphore(name))
        return self.used[-1]

    def close(self):
        self.nc.clear_and_free_semaphores(self.used)
        self.nc.all_engine_barrier()


class Own:

    def __init__(self, eng, sem, base=0):
        self.eng, self.sem, self.base, self.n = eng, sem, base, 0

    def add(self, ins):
        ins.then_inc(self.sem, 1)
        self.n += 1

    def wait(self, back=0):
        self.eng.wait_ge(self.sem, self.base + (self.n - back))

    def link(self, ins):
        self.add(ins)
        self.wait()


def hold(eng, sem, value, pace):
    eng.wait_ge(sem, value)
    eng.sem_inc(pace, 1)


def bcast(ap, axis, n):
    dims = [list(x) for x in ap.ap]
    dims.insert(axis, [0, n])
    return bass.AP(ap.tensor, ap.offset, dims)



RING = 4
SLOT = 2


class Operand:

    def __init__(self, hi, lo, src=None, weight=None):
        self.hi, self.lo, self.src, self.weight = hi, lo, src, weight


class Norm:

    def __init__(self, nc, ctx, tag, x, weight, ones, eps, normed=None, sq=None, arrive=()):
        def sb(name, *dims):
            return ctx.enter_context(nc.sbuf_tensor(f"{tag}_{name}", [P, *dims], F32))

        self.x, self.weight, self.ones, self.eps, self.normed = x, weight, ones, eps, normed
        self.arrive = arrive
        self.sq, self.rstd, self.epst = sb("sq", KD, T) if sq is None else sq, sb("rstd", T), sb("eps", 1)


def gemm(nc, tag, w, kt, operands, nblocks, evacuation, norm=None):
    with ExitStack() as ctx:
        signal = Signals(nc, ctx)
        raw = ctx.enter_context(nc.sbuf_tensor(f"{tag}_w", [P, SLOT, kt, P], F32))
        w_hi = ctx.enter_context(nc.sbuf_tensor(f"{tag}_w_hi", [P, SLOT, kt, P], F32R))
        w_lo = ctx.enter_context(nc.sbuf_tensor(f"{tag}_w_lo", [P, SLOT, kt, P], F32R))
        out = ctx.enter_context(nc.psum_tensor(f"{tag}_out", [P, RING, T], F32))
        w_in = [signal(f"{tag}_weights{b}") for b in range(SLOT)]
        rounded = signal(f"{tag}_rounded")
        parted = signal(f"{tag}_parted")
        ev = evacuation
        ev.out, ev.done, ev.free, ev.own, ev.half = out, signal(f"{tag}_products"), signal(f"{tag}_banks_free"), signal(
            f"{tag}_own"), signal(f"{tag}_half")
        done = ev.done
        size = 2 if kt <= 8 else 6
        pieces = [slice(k, min(k + size, kt)) for k in range(0, kt, size)]
        last = len(pieces) - 1
        piece_in = [signal(f"{tag}_piece{q}") for q in range(last)] + [w_in[0]]
        piece_rounded, piece_parted, x_rounded, x_parted = (
            signal(f"{tag}_{n}") for n in ("piece_rounded", "piece_parted", "x_rounded", "x_parted"))
        if norm:
            total = ctx.enter_context(nc.psum_tensor(f"{tag}_total", [P, T], F32))
            squared, squared_p, added, summed, rooted, scaled = (
                signal(f"{tag}_{n}") for n in ("squared", "squared_p", "added", "summed", "rooted", "scaled"))
            x_in = [signal(f"{tag}_x_in{k}") for k in range(len(norm.arrive))]
        rounds = nblocks // RING
        assert rounds * RING == nblocks and rounds > 1 and SLOT == 2
        block = ctx.enter_context(nc.Block())

        def source(n):
            return w[DS(n * P, P), :].rearrange("p (k n) -> p k n", n=P)

        def turns(eng, start, step, first_turn=None):
            start()
            if first_turn:
                first_turn()
            with eng.Fori(1 if first_turn else 0, rounds - 1) as i:
                for b in range(RING):
                    step(i, b, True)
            for b in range(RING):
                step(rounds - 1, b, b + SLOT < RING)

        def part(high):
            for q, piece in enumerate(pieces):
                if operands[0].src is not None:
                    for k in range(piece.start, piece.stop):
                        high(operands[0], k, k)
                high(None, q, None)
            for o, operand in enumerate(operands[1:]):
                if operand.src is not None:
                    for k in range(kt):
                        high(operand, k, (o + 1) * kt + k)
            high(None, None, None)

        @block.sync
        def _(sp):
            def first():
                arrive = list(zip(norm.arrive, x_in)) if norm else []
                for q, piece in enumerate(pieces):
                    for (dst, src), there in arrive[piece]:
                        sp.dma_start(dst, src).then_inc(there, 16)
                    sp.dma_start(raw[:, 0, piece], source(0)[:, piece]).then_inc(piece_in[q], 16)
                sp.dma_start(raw[:, 1], source(1)).then_inc(w_in[1], 16)
                for (dst, src), there in arrive[kt:]:
                    sp.dma_start(dst, src).then_inc(there, 16)

            def step(i, b, more):
                if more:
                    sp.wait_ge(parted, RING * i + b + 1)
                    sp.dma_start(raw[:, b % SLOT], source(i * RING + (b + SLOT))).then_inc(w_in[b % SLOT], 16)

            turns(sp, first, step)

        @block.tensor
        def _(pe):
            def products(i, b, first_turn=False):
                if first_turn and b == 0:
                    pe.wait_ge(ev.free, 1)
                else:
                    pe.wait_ge(parted, RING * i + b + 1)
                    pe.wait_ge(ev.free, RING * i + b + 1)
                operand = operands[b % len(operands)]
                hi, lo = operand.hi, operand.lo
                s = b % SLOT
                for k in range(kt):
                    if first_turn and b == 0 and k % size == 0:
                        q = k // size
                        if q < last:
                            pe.wait_ge(piece_parted, q + 1)
                        else:
                            pe.wait_ge(parted, 1)
                    if first_turn and b < len(operands) and operand.src is not None:
                        pe.wait_ge(x_parted, b * kt + k + 1)
                    nc.tensor.matmul(out[:, b], w_hi[:, s, k], hi[:, k], start=(k == 0), stop=False)
                    nc.tensor.matmul(out[:, b], w_hi[:, s, k], lo[:, k], start=False, stop=False)
                    mm = nc.tensor.matmul(out[:, b], w_lo[:, s, k], hi[:, k], start=False, stop=(k == kt - 1))
                mm.then_inc(done, 1)

            for b in range(RING):
                products(0, b, True)
                if norm and b == 1:
                    if norm.arrive:
                        pe.wait_ge(x_in[KD], 16)
                    pe.wait_ge(added, KD - 1)
                    nc.tensor.matmul(total[:, :], norm.ones, norm.sq[:, 0], start=True, stop=True).then_inc(summed, 1)
            with pe.Fori(1, rounds) as i:
                for b in range(RING):
                    products(i, b)

        @block.gpsimd
        def _(pool):
            if norm:
                for k in range(0, KD, 2):
                    if norm.arrive:
                        pool.wait_ge(x_in[k], 16)
                    nc.gpsimd.tensor_tensor(norm.sq[:, k], norm.x[:, k], norm.x[:, k], ALU.mult).then_inc(squared_p, 1)

        @block.scalar
        def _(act):
            def high(n, turn):
                act.wait_ge(w_in[n % SLOT], 16 * turn)
                nc.scalar.copy(w_hi[:, n % SLOT], raw[:, n % SLOT]).then_inc(rounded, 1)

            def first_high(operand, k, _):
                if operand is None and k is None:
                    high(1, 1)
                elif operand is None:
                    act.wait_ge(piece_in[k], 16)
                    nc.scalar.copy(w_hi[:, 0, pieces[k]], raw[:, 0, pieces[k]]).then_inc(
                        piece_rounded if k < last else rounded, 1)
                elif operand.weight is None:
                    nc.scalar.copy(operand.hi[:, k], operand.src[:, k]).then_inc(x_rounded, 1)
                else:
                    if norm and norm.arrive:
                        act.wait_ge(x_in[k], 16)
                    nc.scalar.activation(operand.hi[:, k], operand.src[:, k], ACT.Copy,
                                         scale=operand.weight[:, k:k + 1]).then_inc(x_rounded, 1)

            def start():
                act.sem_inc(ev.free, RING)
                part(first_high)
                if norm:
                    for k in range(1, KD, 2):
                        nc.scalar.activation(norm.sq[:, k], norm.x[:, k], ACT.Square).then_inc(squared, 1)

            def step(i, b, more):
                act.wait_ge(done, RING * i + b + 1)
                if more:
                    high(b + SLOT, i * (RING // SLOT) + (b // SLOT + 2))
                ev.scalar(nc, act, i, b)

            def first_turn():
                for b in range(2):
                    act.wait_ge(done, b + 1)
                    high(b + SLOT, 2)
                act.wait_ge(scaled, 1)
                act.wait_ge(summed, 1)
                nc.scalar.activation(norm.rstd[:, :], total[:, :], ACT.Sqrt, bias=norm.epst[:, 0:1],
                                     scale=1.0 / D).then_inc(rooted, 1)
                for b in range(2):
                    ev.scalar(nc, act, 0, b)
                for b in range(2, RING):
                    step(0, b, True)

            turns(act, start, step, first_turn if norm else None)

        @block.vector
        def _(dve):
            def low(n, count):
                dve.wait_ge(rounded, count)
                nc.vector.tensor_tensor(w_lo[:, n % SLOT], raw[:, n % SLOT], w_hi[:, n % SLOT].bitcast(F32),
                                        ALU.subtract).then_inc(parted, 1)

            def first_low(operand, k, count):
                if operand is None and k is None:
                    low(1, 2)
                elif operand is None:
                    dve.wait_ge(*((piece_rounded, k + 1) if k < last else (rounded, 1)))
                    nc.vector.tensor_tensor(w_lo[:, 0, pieces[k]], raw[:, 0, pieces[k]], w_hi[:, 0, pieces[k]].bitcast(F32),
                                            ALU.subtract).then_inc(piece_parted if k < last else parted, 1)
                else:
                    dve.wait_ge(x_rounded, count + 1)
                    hi = operand.hi[:, k].bitcast(F32)
                    if operand.weight is None:
                        ins = nc.vector.tensor_tensor(operand.lo[:, k], operand.src[:, k], hi, ALU.subtract)
                    else:
                        ins = nc.vector.scalar_tensor_tensor(out=operand.lo[:, k], in0=operand.src[:, k],
                                                             scalar=operand.weight[:, k:k + 1], in1=hi,
                                                             op0=ALU.mult, op1=ALU.subtract)
                    ins.then_inc(x_parted, 1)

            def start():
                if norm:
                    nc.vector.memset(norm.epst[:, :], norm.eps).then_inc(scaled, 1)
                part(first_low)
                ev.start(nc, dve)
                if norm:
                    n, sq = 0, norm.sq
                    for width in (4, 2, 1):
                        if width == 4:
                            dve.wait_ge(squared_p, KD // 2)
                            dve.wait_ge(squared, KD // 2)
                        for k in range(width):
                            nc.vector.tensor_tensor(sq[:, k], sq[:, k], sq[:, k + width], ALU.add).then_inc(added, 1)
                            n += 1
                        if width > 1:
                            dve.wait_ge(added, n)

            def step(i, b, more):
                dve.wait_ge(done, RING * i + b + 1)
                if more:
                    low(b + SLOT, RING * i + (b + SLOT + 1))
                ev.vector(nc, dve, i, b)

            def first_turn():
                for b in range(2):
                    low(b + SLOT, b + SLOT + 1)
                dve.wait_ge(rooted, 1)
                nc.vector.reciprocal(norm.rstd[:, :], norm.rstd[:, :]).then_inc(scaled, 1)
                dve.wait_ge(scaled, 2)
                for b in range(2):
                    dve.wait_ge(done, b + 1)
                    ev.vector(nc, dve, 0, b)
                for b in range(2, RING):
                    step(0, b, True)
                    if norm.normed is not None:
                        for k in range((b - 2) * KD // 2, (b - 1) * KD // 2):
                            nc.vector.scalar_tensor_tensor(out=norm.normed[:, k], in0=norm.x[:, k], scalar=norm.weight[:, k:k + 1],
                                                           in1=norm.rstd[:, :], op0=ALU.mult, op1=ALU.mult)

            turns(dve, start, step, first_turn if norm else None)


def at_block(x, n):
    return x[:, DS(n, 1), :].rearrange("p a t -> p (a t)")


class Evacuation:

    def start(self, nc, dve):
        pass

    def scalar(self, nc, act, i, b):
        pass


class Scale(Evacuation):

    def __init__(self, dst, scale):
        self.dst, self.factor = dst, scale

    def vector(self, nc, dve, i, b):
        nc.vector.tensor_tensor(self.dst(i * RING + b), self.out[:, b], self.factor, ALU.mult).then_inc(self.free, 1)


class AddTo(Evacuation):

    def __init__(self, x, scale=1.0):
        self.x, self.scale = x, scale

    def vector(self, nc, dve, i, b):
        xb = at_block(self.x, i * RING + b)
        nc.vector.scalar_tensor_tensor(out=xb, in0=self.out[:, b], scalar=float(self.scale), in1=xb,
                                       op0=ALU.mult, op1=ALU.add).then_inc(self.free, 1)


class Swiglu(Evacuation):

    def __init__(self, hi, lo, silu, product, scale):
        self.hi, self.lo, self.silu, self.product, self.factor = hi, lo, silu, product, scale

    def scalar(self, nc, act, i, b):
        if b % 2 == 0:
            act.wait_ge(self.free, RING * i + (RING + b + 1))
            silu = self.silu[:, b // 2]
            nc.scalar.activation(silu, silu, ACT.Silu).then_inc(self.half, 1)

    def vector(self, nc, dve, i, b):
        n, j = i * (RING // 2) + b // 2, b // 2
        if b % 2 == 0:
            nc.vector.tensor_tensor(self.silu[:, j], self.out[:, b], self.factor, ALU.mult).then_inc(self.free, 1)
        else:
            product = self.product[:, j]
            dve.wait_ge(self.half, n + 1)
            nc.vector.tensor_tensor(product, self.out[:, b], self.silu[:, j], ALU.mult).then_inc(self.free, 1)
            dve.wait_ge(self.free, RING * i + (RING + b + 1))
            nc.vector.tensor_tensor(product, product, self.factor, ALU.mult).then_inc(self.own, 1)
            dve.wait_ge(self.own, n * 3 + 1)
            hi = at_block(self.hi, n)
            nc.vector.tensor_copy(hi, product).then_inc(self.own, 1)
            dve.wait_ge(self.own, n * 3 + 2)
            nc.vector.tensor_tensor(at_block(self.lo, n), product, hi.bitcast(F32), ALU.subtract).then_inc(self.own, 1)
            dve.wait_ge(self.own, n * 3 + 3)


class Merge(Evacuation):

    def __init__(self, m, pr):
        self.m, self.pr = m, pr

    def scalar(self, nc, act, i, b):
        if b % 2 == 0:
            n = i * (RING // 2) + b // 2
            for first in (C_GA, C_GB):
                g = at_block(self.pr, n + first)
                ins = nc.scalar.activation(g, g, ACT.Sigmoid)
            ins.then_inc(self.half, 1)

    def vector(self, nc, dve, i, b):
        if b % 2:
            n = i * (RING // 2) + b // 2
            dve.wait_ge(self.half, n + 1)
            ga, gb = at_block(self.pr, n + C_GA), at_block(self.pr, n + C_GB)
            nc.vector.tensor_tensor(ga, self.out[:, b - 1], ga, ALU.mult)
            nc.vector.tensor_tensor(gb, self.out[:, b], gb, ALU.mult).then_inc(self.free, 2)
            dve.wait_ge(self.free, RING * i + (RING + b + 1))
            nc.vector.tensor_tensor(at_block(self.m, n), ga, gb, ALU.add)



def rmsnorm(nc, tag, x, weight, ones, eps, store=None):
    with ExitStack() as ctx:
        signal = Signals(nc, ctx)
        sq = ctx.enter_context(nc.sbuf_tensor(f"{tag}_sq", [P, KD, T], F32))
        rstd = ctx.enter_context(nc.sbuf_tensor(f"{tag}_rstd", [P, T], F32))
        epst = ctx.enter_context(nc.sbuf_tensor(f"{tag}_eps", [P, 1], F32))
        total = ctx.enter_context(nc.psum_tensor(f"{tag}_total", [P, T], F32))
        squared, summed, rooted, own = (signal(f"{tag}_{n}") for n in ("squared", "summed", "rooted", "own"))
        normed, stored = signal(f"{tag}_normed"), signal(f"{tag}_stored")
        block = ctx.enter_context(nc.Block())

        @block.sync
        def _(sp):
            if store is not None:
                for k in range(0, KD, 2):
                    sp.wait_ge(normed, k + 2)
                    sp.dma_start(store[:, k:k + 2], x[:, k:k + 2]).then_inc(stored, 16)
                sp.wait_ge(stored, 16 * (KD // 2))

        @block.scalar
        def _(act):
            for k in range(0, KD, 2):
                nc.scalar.activation(sq[:, k], x[:, k], ACT.Square).then_inc(squared, 1)
            act.wait_ge(summed, 1)
            act.wait_ge(own, 1)
            nc.scalar.activation(rstd[:, :], total[:, :], ACT.Sqrt, bias=epst[:, 0:1], scale=1.0 / D).then_inc(rooted, 1)

        @block.tensor
        def _(pe):
            for k in range(KD):
                if k % 2:
                    pe.wait_ge(own, 1 + (k + 1) // 2)
                else:
                    pe.wait_ge(squared, k // 2 + 1)
                mm = nc.tensor.matmul(total[:, :], ones, sq[:, k], start=(k == 0), stop=(k == KD - 1))
            mm.then_inc(summed, 1)

        @block.vector
        def _(dve):
            nc.vector.memset(epst[:, :], eps).then_inc(own, 1)
            for k in range(1, KD, 2):
                nc.vector.tensor_tensor(sq[:, k], x[:, k], x[:, k], ALU.mult).then_inc(own, 1)
            dve.wait_ge(rooted, 1)
            nc.vector.reciprocal(rstd[:, :], rstd[:, :]).then_inc(own, 1)
            dve.wait_ge(own, 2 + KD // 2)
            for k in range(KD):
                nc.vector.scalar_tensor_tensor(out=x[:, k], in0=x[:, k], scalar=weight[:, k:k + 1],
                                               in1=rstd[:, :], op0=ALU.mult, op1=ALU.mult).then_inc(normed, 1)



class Shift(Evacuation):

    def __init__(self, nc, ctx, dst, scale, mu0, mu1):
        self.dst, self.factor, self.mu0, self.mu1 = dst, scale, mu0, mu1
        self.rest = ctx.enter_context(nc.sbuf_tensor("shift_rest", [P, N_SHIFT], F32))
        self.p = ctx.enter_context(nc.sbuf_tensor("shift_in", [P, RING, T + 2], F32))

    def start(self, nc, dve):
        nc.vector.memset(self.p[:, :, 0:1], 0.0)
        nc.vector.memset(self.p[:, :, T + 1:T + 2], 0.0)
        nc.vector.tensor_tensor(self.rest[:, :], self.mu0, self.mu1, ALU.add).then_inc(self.own, 1)
        dve.wait_ge(self.own, 1)
        nc.vector.tensor_scalar(self.rest[:, :], self.rest[:, :], -1.0, 1.0, ALU.mult, ALU.add).then_inc(self.own, 1)
        dve.wait_ge(self.own, 2)

    def scalar(self, nc, act, i, b):
        n = i * RING + b
        act.wait_ge(self.free, n + (RING + 1))
        if isinstance(i, int) and n >= N_SHIFT:
            nc.scalar.copy(at_block(self.dst, n), self.p[:, b, 1:T + 1])
        else:
            nc.scalar.activation(at_block(self.dst, n), self.p[:, b, 1:T + 1], ACT.Copy,
                                 scale=self.rest[:, DS(n, 1)]).then_inc(self.half, 1)

    def vector(self, nc, dve, i, b):
        n = i * RING + b
        nc.vector.tensor_tensor(self.p[:, b, 1:T + 1], self.out[:, b], self.factor, ALU.mult).then_inc(self.free, 1)
        if not (isinstance(i, int) and n >= N_SHIFT):
            for mu, first, count in ((self.mu0, 0, 1), (self.mu1, 2, 2)):
                if count == 1:
                    dve.wait_ge(self.half, n + 1)
                else:
                    dve.wait_ge(self.own, n * 2 + 3)
                nc.vector.scalar_tensor_tensor(out=at_block(self.dst, n), in0=self.p[:, b, first:first + T],
                                               scalar=mu[:, DS(n, 1)], in1=at_block(self.dst, n),
                                               op0=ALU.mult, op1=ALU.add).then_inc(self.own, 1)


def rwkv_operands(nc, q, lora, lora_dram, vec, consts, ar, bk, kk, kd_sum, w_end):
    with ExitStack() as ctx:
        signal = Signals(nc, ctx)
        DEPTH = 4
        units = [(i, d) for i in range(PAIRS) for d in range(2)]
        omk = ctx.enter_context(nc.sbuf_tensor("omk", [P, PAIRS], F32))
        nrm = ctx.enter_context(nc.sbuf_tensor("nrm", [P, T], F32))
        sq = ctx.enter_context(nc.sbuf_tensor("kk_sq", [P, PAIRS, T], F32))
        cum, wt, winv = (ctx.enter_context(nc.sbuf_tensor(n, [P, DEPTH, T], F32)) for n in ("cum", "wt", "winv"))
        zp = ctx.enter_context(nc.psum_tensor("zp", [P, 2, 2, T], F32))
        np_ = ctx.enter_context(nc.psum_tensor("np_", [P, PAIRS, T], F32))
        tanhed = signal("tanhed")
        squares = signal("kk_squares")
        norms = signal("kk_norms")
        roots = signal("kk_roots")
        kk_done = signal("kk_done")
        zs = signal("lora_products")
        sigs = signal("lora_sigmoids")
        sums = signal("decay_sums")
        exps = signal("decay_exps")
        used = signal("operands_made")
        own = signal("operands_own")
        pooled = signal("operands_by_pool")
        summed = signal("kd_summed")
        base, per = 4 * PAIRS, 4
        lora_in = signal("lora_in")
        reset = consts("reset")
        block = ctx.enter_context(nc.Block())

        @block.sync
        def _(sp):
            sp.dma_start(lora[:, :, :], lora_dram.rearrange("p (a n) -> p a n", a=2)).then_inc(lora_in, 16)

        def sg(i, d): return ar[:, d, 1, i]
        def cpre(i, d): return ar[:, d, 0, i]
        def aa(i, d): return bk[:, d, 0, i]
        def kt_(i, d): return bk[:, d, 1, i]

        @block.scalar
        def _(act):
            nc.scalar.activation(q[:, B_WD], q[:, B_WD], ACT.Tanh).then_inc(tanhed, 1)
            act.wait_ge(squares, PAIRS)
            for p in range(PAIRS):
                act.wait_ge(norms, p + 1)
                nc.scalar.activation(sq[:, p], np_[:, p], ACT.Sqrt).then_inc(roots, 1)
            for u, (i, d) in enumerate(units):
                act.wait_ge(zs, u + 1)
                at = i + PAIRS * d
                nc.scalar.activation(sg(i, d), zp[:, d, 0], ACT.Sigmoid, bias=vec("w0")[:, at:at + 1])
                nc.scalar.activation(aa(i, d), zp[:, d, 1], ACT.Sigmoid, bias=vec("a0")[:, at:at + 1]).then_inc(sigs, 1)
            for u, (i, d) in enumerate(units):
                act.wait_ge(sums, u + 1)
                if u >= DEPTH:
                    act.wait_ge(used, u - DEPTH + 1)
                    act.wait_ge(pooled, u - DEPTH + 1)
                b = u % DEPTH
                nc.scalar.activation(wt[:, b], cum[:, b], ACT.Exp, scale=-DECAY)
                nc.scalar.activation(cpre(i, d), cpre(i, d), ACT.Exp, scale=-DECAY)
                nc.scalar.activation(winv[:, b], cum[:, b], ACT.Exp, scale=DECAY).then_inc(exps, 1)

        @block.tensor
        def _(pe):
            for p in range(PAIRS):
                pe.wait_ge(squares, p + 1)
                nc.tensor.matmul(np_[:, p], consts("heads"), sq[:, p], start=True, stop=True).then_inc(norms, 1)
            pe.wait_ge(tanhed, 1)
            pe.wait_ge(lora_in, 16)
            for p in range(PAIRS):
                for d in range(2):
                    n = 2 * p + d
                    if n >= 2:
                        pe.wait_ge(sigs, n - 1)
                    rows = slice(HEAD * d, HEAD * d + HEAD)
                    nc.tensor.matmul(zp[:, d, 0], lora[rows, 0, p * P:(p + 1) * P], q[rows, B_WD], start=True, stop=True)
                    nc.tensor.matmul(zp[:, d, 1], lora[rows, 1, p * P:(p + 1) * P], q[rows, B_AD],
                                     start=True, stop=True).then_inc(zs, 1)

        @block.gpsimd
        def _(pool):
            pool.wait_ge(own, base)
            for u, (i, d) in enumerate(units):
                pool.wait_ge(exps, u + 1)
                nc.gpsimd.tensor_tensor(ar[:, d, 0, i], cpre(i, d), kk[:, i], ALU.mult)
                nc.gpsimd.tensor_tensor(ar[:, d, 1, i], wt[:, u % DEPTH], q[:, B_R + i], ALU.mult).then_inc(pooled, 1)

        @block.vector
        def _(dve):
            nc.vector.tensor_scalar(omk[:, :], vec("k_a"), -1.0, 1.0, ALU.mult, ALU.add)
            for p in range(PAIRS):
                nc.vector.tensor_scalar(kk[:, p], q[:, B_K + p], vec("k_k")[:, p:p + 1], None, ALU.mult).then_inc(own, 1)
            for p in range(PAIRS):
                dve.wait_ge(own, p + 1)
                nc.vector.tensor_tensor(sq[:, p], kk[:, p], kk[:, p], ALU.mult).then_inc(squares, 1)
            n = PAIRS
            for p in range(PAIRS):
                dve.wait_ge(roots, p + 1)
                nc.vector.tensor_scalar(sq[:, p], sq[:, p], 1e-12, None, ALU.max).then_inc(own, 1)
                n += 1
                dve.wait_ge(own, n)
                nc.vector.reciprocal(nrm[:, :], sq[:, p]).then_inc(own, 1)
                n += 1
                dve.wait_ge(own, n)
                nc.vector.tensor_tensor(kk[:, p], kk[:, p], nrm[:, :], ALU.mult).then_inc(own, 1)
                n += 1
            dve.wait_ge(own, n)
            assert n == base, n

            def before(u, i, d):
                way = slice(None) if d == 0 else slice(None, None, -1)
                dve.wait_ge(sigs, u + 1)
                if u >= DEPTH:
                    dve.wait_ge(exps, u - DEPTH + 1)
                b = u % DEPTH
                nc.vector.tensor_tensor_scan(out=cum[:, b, way], data0=reset, data1=sg(i, d)[:, way], initial=0.0,
                                             op0=ALU.mult, op1=ALU.add).then_inc(own, 1)
                nc.vector.tensor_scalar(kt_(i, d), aa(i, d), vec("k_a")[:, i:i + 1], omk[:, i:i + 1],
                                        ALU.mult, ALU.add).then_inc(own, 1)
                dve.wait_ge(own, per * u + base + 1)
                nc.vector.tensor_tensor(cpre(i, d), cum[:, b], sg(i, d), ALU.subtract).then_inc(sums, 1)
                dve.wait_ge(own, per * u + base + 2)
                nc.vector.tensor_tensor(kt_(i, d), kt_(i, d), q[:, B_K + i], ALU.mult).then_inc(own, 1)
                nc.vector.tensor_tensor(aa(i, d), aa(i, d), kk[:, i], ALU.mult).then_inc(own, 1)

            def behind(u, i, d):
                if d == 0:
                    dve.wait_ge(own, per * (u + 2) + base)
                    nc.vector.tensor_tensor(kd_sum[:, i], kt_(i, 0), kt_(i, 1), ALU.add).then_inc(summed, 1)
                dve.wait_ge(exps, u + 1)
                b = u % DEPTH
                nc.vector.scalar_tensor_tensor(out=bk[:, d, 0, i], in0=aa(i, d), scalar=-1.0, in1=winv[:, b],
                                               op0=ALU.mult, op1=ALU.mult)
                dve.wait_ge(summed, i + 1)
                nc.vector.tensor_tensor(bk[:, d, 1, i], kt_(i, d), winv[:, b], ALU.mult)
                ends = wt[:, b, CHUNK - 1::CHUNK] if d == 0 else wt[:, b, 0::CHUNK]
                nc.vector.tensor_copy(w_end[:, d, :, i:i + 1].rearrange("p c a -> p (c a)"), ends).then_inc(used, 1)

            lag = 2
            for u in range(len(units) + lag):
                if u < len(units):
                    before(u, *units[u])
                if u >= lag:
                    behind(u - lag, *units[u - lag])


def recurrence(nc, ar, bk, v, w_end, consts, o):
    with ExitStack() as ctx:
        signal = Signals(nc, ctx)
        def sb(name, *shape):
            return ctx.enter_context(nc.sbuf_tensor(name, [P, 2, PAIRS, *shape], F32))

        a_w, b_w, k_w = (sb(f"{n}_wide_c", P) for n in "abk")
        a_n, b_n, k_n, v_n = (sb(f"{n}_narrow_c", P) for n in "abkv")
        DT, Dm, E, LkT = sb("DT", P), sb("Dm", P), sb("E", P), sb("LkT", P)
        PbB, PkT, V = sb("PbB", 2, HEAD), sb("PkT", HEAD), sb("V", HEAD)
        PbT, B = PbB[:, :, :, 0], PbB[:, :, :, 1]
        Vw, Bw, Kw = sb("Vw", P), sb("Bw", P), sb("Kw", P)
        D2, D2T, R1, R2, X = sb("D2", P), sb("D2T", P), sb("R1", P), sb("R2", P), sb("X", P)
        D4, D4T, D8, N, NT, N2T, X1, X2, Y = Dm, DT, D2, D2T, Dm, DT, LkT, E, R1
        Aw, Uw, MTw, RT = sb("Aw", P), sb("Uw", P), sb("MTw", P), sb("RT", HEAD)
        S, Sw, Sn = sb("S", HEAD), sb("Sw", P), sb("Sn", HEAD)
        banks = ctx.enter_context(nc.psum_tensor("rec_banks", [P, 2, 4, PAIRS, P], F32))

        pe_done = [signal(f"rec_products{d}") for d in range(2)]
        by_dve = [signal(f"rec_by_vector{d}") for d in range(2)]
        by_act = [signal(f"rec_by_scalar{d}") for d in range(2)]
        loaded = [signal(f"rec_wide{d}") for d in range(2)]
        sw_done = [signal(f"rec_state_wide{d}") for d in range(2)]
        own = signal("rec_own")

        STEPS = [("LbT", "v"), ("LkT", "v"), ("Lb", "v"), ("VB", "a"), ("KG", "a"), ("D2", "a"), ("D2T", "a"),
                 ("R2", "v"), ("D4", "a"), ("D4T", "a"), ("R3", "v"), ("D8", "a"), ("R4", "v"),
                 ("N", "a"), ("NT", "a"), ("X1", "a"), ("N2T", "a"), ("X2", "v"), ("Y", "v"),
                 ("RtM", "v"), ("out", "a"), ("S", "v")]
        AT = {name: n for n, (name, _) in enumerate(STEPS)}
        NS = len(STEPS)
        ORD, PER = {}, {"v": 0, "a": 0}
        for name, e in STEPS:
            PER[e] += 1
            ORD[name] = (e, PER[e])
        for e, name, last in (("a", "WideU", "N2T"), ("a", "M", "WideU"), ("v", "WideA", "Y")):
            for other, (f, n) in ORD.items():
                if f == e and n > ORD[last][1]:
                    ORD[other] = (f, n + 1)
            ORD[name] = (e, ORD[last][1] + 1)
            PER[e] += 1

        with nc.Block() as block:
            @block.vector
            def _(dve):
                for w in (Vw, Bw, Kw, Aw, Uw, MTw):
                    nc.vector.memset(w[:, :, :, :], 0.0)

            @block.gpsimd
            def _(pool):
                for w in (a_w, b_w, k_w, Sw, S):
                    nc.gpsimd.memset(w[:, :, :, :], 0.0)

        block = ctx.enter_context(nc.Block())

        def chunk(c, d):
            return c * CHUNK if d == 0 else c * -CHUNK + (NCHUNK - 1) * CHUNK

        halves = [(slice(0, HEAD), slice(0, HEAD)), (slice(HEAD, P), slice(HEAD, P))]
        TURNED = None

        @block.gpsimd
        def _(pool):
            def widen(c, d):
                at = chunk(c, d)
                sources = {"b": bk[:, d, 0], "a": ar[:, d, 0], "k": bk[:, d, 1], "v": v}
                for w, src in ((b_w, "b"), (k_w, "k"), (a_w, "a")):
                    for rows, cols in halves:
                        nc.gpsimd.tensor_copy(w[rows, d, :, cols], sources[src][rows, :, DS(at, CHUNK)])
                for w, src in ((a_n, "a"), (v_n, "v"), (b_n, "b"), (k_n, "k")):
                    for rows, cols in halves:
                        ins = nc.gpsimd.tensor_copy(w[0:HEAD, d, :, cols], sources[src][rows, :, DS(at, CHUNK)])
                ins.then_inc(loaded[d], 1)

            for d in range(2):
                widen(0, d)
            with pool.Fori(0, NCHUNK - 1) as c:
                for d in range(2):
                    pool.wait_ge(pe_done[d], NS * c + AT["KG"] + 1)
                    widen(c + 1, d)

        @block.tensor
        def _(pe):
            def after(c, d, name):
                e, n = ORD[name]
                pe.wait_ge((by_dve if e == "v" else by_act)[d], PER[e] * c + (PER[e] + n))

            def bank_free(c, d, name):
                e, n = ORD[name]
                pe.wait_ge((by_dve if e == "v" else by_act)[d], PER[e] * c + n)

            with pe.Fori(0, NCHUNK) as c:
                def each(name, d, parts):
                    n = AT[name]
                    for p in range(PAIRS):
                        for cols, products in parts(p):
                            for j, (lhs, rhs) in enumerate(products):
                                if rhs is TURNED:
                                    mm = nc.tensor.transpose(banks[:, d, n % 4, p, cols], lhs, consts("ident")[0:HEAD, 0:HEAD])
                                else:
                                    mm = nc.tensor.matmul(banks[:, d, n % 4, p, cols], lhs, rhs,
                                                          start=(j == 0), stop=(j == len(products) - 1))
                    mm.then_inc(pe_done[d], 1)

                full, left, right = slice(0, P), slice(0, HEAD), slice(HEAD, P)
                both = (0, 1)
                for d in both:
                    at = chunk(c, d)
                    pe.wait_ge(loaded[d], c + 1)
                    bank_free(c, d, "out")
                    each("LbT", d, lambda p: [(full, [(b_w[:, d, p], ar[:, d, :, p, DS(at, CHUNK)])])])
                    bank_free(c, d, "S")
                    each("LkT", d, lambda p: [(full, [(k_w[:, d, p], ar[:, d, :, p, DS(at, CHUNK)])])])
                    each("Lb", d, lambda p: [(left, [(a_w[:, d, p], bk[:, d, 0, p, DS(at, CHUNK)])]),
                                             (right, [(a_n[0:HEAD, d, p], TURNED)])])
                    each("VB", d, lambda p: [(left, [(v_n[0:HEAD, d, p], TURNED)]), (right, [(b_n[0:HEAD, d, p], TURNED)])])
                for d in both:
                    after(c, d, "LbT")
                    after(c, d, "LkT")
                    after(c, d, "VB")
                    each("KG", d, lambda p: [(right, [(LkT[:, d, p], V[:, d, p])]), (left, [(k_n[0:HEAD, d, p], TURNED)])])
                for d in both:
                    after(c, d, "Lb")
                    each("D2", d, lambda p: [(full, [(DT[:, d, p], Dm[:, d, p])])])
                    each("D2T", d, lambda p: [(full, [(Dm[:, d, p], DT[:, d, p])])])
                for d in both:
                    after(c, d, "D2")
                    each("R2", d, lambda p: [(full, [(D2[:, d, p], R1[:, d, p])])])
                    after(c, d, "D2T")
                    each("D4", d, lambda p: [(full, [(D2T[:, d, p], D2[:, d, p])])])
                    each("D4T", d, lambda p: [(full, [(D2[:, d, p], D2T[:, d, p])])])
                for d in both:
                    after(c, d, "R2")
                    after(c, d, "D4")
                    each("R3", d, lambda p: [(full, [(D4[:, d, p], R2[:, d, p])])])
                    after(c, d, "D4T")
                    each("D8", d, lambda p: [(full, [(D4T[:, d, p], D4[:, d, p])])])
                for d in both:
                    after(c, d, "R3")
                    after(c, d, "D8")
                    each("R4", d, lambda p: [(full, [(D8[:, d, p], R1[:, d, p])])])
                for d in both:
                    after(c, d, "R4")
                    each("N", d, lambda p: [(full, [(R2[:, d, p], E[:, d, p])])])
                    each("NT", d, lambda p: [(full, [(E[:, d, p], R2[:, d, p])])])
                    after(c, d, "KG")
                    each("X1", d, lambda p: [(full, [(R2[:, d, p], X[:, d, p])])])
                for d in both:
                    after(c, d, "NT")
                    each("N2T", d, lambda p: [(full, [(N[:, d, p], NT[:, d, p])])])
                for d in both:
                    after(c, d, "N2T")
                    each("X2", d, lambda p: [(full, [(N2T[:, d, p], X1[:, d, p])])])
                for d in both:
                    after(c, d, "X2")
                    each("Y", d, lambda p: [(full, [(NT[:, d, p], X2[:, d, p])])])
                for d in both:
                    after(c, d, "WideA")
                    each("RtM", d, lambda p: [(full, [(Aw[:, d, p], PbB[:, d, p].rearrange("q a s -> q (a s)"))])])
                for d in both:
                    after(c, d, "RtM")
                    after(c, d, "WideU")
                    pe.wait_ge(sw_done[d], c + 1)
                    each("out", d, lambda p: [(left, [(Sw[:, d, p], RT[:, d, p]), (Uw[:, d, p], PbT[:, d, p]),
                                                      (Vw[:, d, p], PkT[:, d, p])])])
                    after(c, d, "M")
                    each("S", d, lambda p: [(left, [(MTw[:, d, p], S[:, d, p]), (Bw[:, d, p], Y[:, d, p, HEAD:P]),
                                                    (Kw[:, d, p], V[:, d, p])])])

        @block.scalar
        def _(act):
            for d in range(2):
                act.sem_inc(by_act[d], PER["a"])
            with act.Fori(0, NCHUNK) as c:
                def ready(d, name):
                    act.wait_ge(pe_done[d], NS * c + AT[name] + 1)

                def bank(d, name):
                    return banks[:, d, AT[name] % 4]

                def wide(dst, src, d):
                    for rows, cols in halves:
                        ins = nc.scalar.copy(dst[rows, d, :, cols], src[rows])
                    return ins

                def plain(dst, name, d):
                    ready(d, name)
                    nc.scalar.copy(dst[:, d], bank(d, name)).then_inc(by_act[d], 1)

                both = (0, 1)
                for d in both:
                    ready(d, "VB")
                    b = bank(d, "VB")
                    nc.scalar.copy(V[:, d], b[:, :, 0:HEAD])
                    nc.scalar.copy(B[:, d], b[:, :, HEAD:P]).then_inc(by_act[d], 1)
                for d in both:
                    ready(d, "KG")
                    b = bank(d, "KG")
                    wide(Kw, b[:, :, 0:HEAD], d)
                    nc.scalar.copy(X[:, d, :, HEAD:P], b[:, :, HEAD:P]).then_inc(by_act[d], 1)
                for d in both:
                    plain(D2, "D2", d)
                    plain(D2T, "D2T", d)
                for d in both:
                    plain(D4, "D4", d)
                    plain(D4T, "D4T", d)
                for d in both:
                    plain(D8, "D8", d)
                for d in both:
                    plain(N, "N", d)
                    plain(NT, "NT", d)
                    plain(X1, "X1", d)
                for d in both:
                    plain(N2T, "N2T", d)
                for d in both:
                    act.wait_ge(by_dve[d], PER["v"] * c + PER["v"] + ORD["Y"][1])
                    wide(Uw, Y[:, d, :, HEAD:P], d).then_inc(by_act[d], 1)
                for d in both:
                    act.wait_ge(by_dve[d], PER["v"] * c + PER["v"] + ORD["RtM"][1])
                    wide(MTw, bank(d, "RtM")[:, :, HEAD:P], d).then_inc(by_act[d], 1)
                for d in both:
                    ready(d, "out")
                    nc.scalar.copy(o[:, d, :, DS(chunk(c, d), CHUNK)], bank(d, "out")[:, :, 0:HEAD]).then_inc(by_act[d], 1)
                for d in both:
                    act.wait_ge(by_dve[d], PER["v"] * c + PER["v"] + PER["v"])
                    act.wait_ge(pe_done[d], NS * c + NS)
                    wide(Sw, S[:, d], d).then_inc(sw_done[d], 1)

        @block.vector
        def _(dve):
            for d in range(2):
                dve.sem_inc(sw_done[d], 1)
                dve.sem_inc(by_dve[d], PER["v"])
            per_own = 2
            with dve.Fori(0, NCHUNK) as c:
                k = [0]

                def link(ins):
                    ins.then_inc(own, 1)
                    k[0] += 1
                    dve.wait_ge(own, per_own * c + k[0])

                def ready(d, name):
                    dve.wait_ge(pe_done[d], NS * c + AT[name] + 1)

                def bank(d, name):
                    return banks[:, d, AT[name] % 4]

                def spread(src):
                    return bcast(src, 2, 2)

                def mask(m, n=P):
                    m = consts(m)
                    if n == P:
                        return bcast(m, 1, PAIRS).rearrange("p a (b s) -> p a b s", b=2)
                    return bcast(m, 1, PAIRS)

                def wide(t, d):
                    return t[:, d].rearrange("p a (b s) -> p a b s", b=2)

                both = (0, 1)
                for d in both:
                    lt, l, inc = (("up", "low", "up_incl") if d == 0 else ("low", "up", "low_incl"))
                    ready(d, "LbT")
                    b = bank(d, "LbT")
                    nc.vector.tensor_tensor(wide(DT, d), spread(b[:, :, 0:HEAD]), mask(lt + "_near"), ALU.mult)
                    nc.vector.tensor_tensor(PbT[:, d], b[:, :, HEAD:P], mask(inc, HEAD), ALU.mult).then_inc(by_dve[d], 1)
                    ready(d, "LkT")
                    b = bank(d, "LkT")
                    nc.vector.tensor_tensor(wide(LkT, d), spread(b[:, :, 0:HEAD]), mask(lt + "_strict"), ALU.mult)
                    nc.vector.tensor_tensor(PkT[:, d], b[:, :, HEAD:P], mask(inc, HEAD), ALU.mult).then_inc(by_dve[d], 1)
                    dve.wait_ge(by_dve[d], PER["v"] * c + PER["v"] + 1)
                    nc.vector.tensor_tensor(R1[:, d], DT[:, d], bcast(consts("ident"), 1, PAIRS), ALU.add)
                    ready(d, "Lb")
                    b = bank(d, "Lb")
                    nc.vector.tensor_tensor(wide(Dm, d), spread(b[:, :, 0:HEAD]), mask(l + "_near"), ALU.mult)
                    nc.vector.tensor_tensor(wide(E, d), spread(b[:, :, 0:HEAD]), mask(l + "_far"), ALU.mult)
                    nc.vector.tensor_copy(X[:, d, :, 0:HEAD], b[:, :, HEAD:P]).then_inc(by_dve[d], 1)

                for d in both:
                    dve.wait_ge(by_act[d], PER["a"] * c + PER["a"] + ORD["VB"][1])
                    for rows, cols in halves:
                        nc.vector.tensor_copy(Vw[rows, d, :, cols], V[rows, d])
                        nc.vector.tensor_copy(Bw[rows, d, :, cols], B[rows, d])
                for name, old, new in (("R2", R1, R2), ("R3", R2, R1), ("R4", R1, R2)):
                    for d in both:
                        ready(d, name)
                        nc.vector.tensor_tensor(new[:, d], bank(d, name), old[:, d], ALU.add).then_inc(by_dve[d], 1)
                for name, old, new in (("X2", X1, X2), ("Y", X2, Y)):
                    for d in both:
                        ready(d, name)
                        nc.vector.tensor_tensor(new[:, d], bank(d, name), old[:, d], ALU.add).then_inc(by_dve[d], 1)
                        if name == "Y":
                            dve.wait_ge(by_dve[d], PER["v"] * c + PER["v"] + ORD["Y"][1])
                            for rows, cols in halves:
                                ins = nc.vector.tensor_copy(Aw[rows, d, :, cols], Y[rows, d, :, 0:HEAD])
                            ins.then_inc(by_dve[d], 1)
                for d in both:
                    ready(d, "RtM")
                    nc.vector.tensor_tensor(RT[:, d], bank(d, "RtM")[:, :, 0:HEAD],
                                            ar[:, d, 1, :, DS(chunk(c, d), CHUNK)], ALU.add).then_inc(by_dve[d], 1)
                for d in both:
                    ready(d, "S")
                    link(nc.vector.tensor_tensor(Sn[:, d], bank(d, "S")[:, :, 0:HEAD], S[:, d], ALU.add))
                    ends = bcast(w_end[:, d, DS(c if d == 0 else c * -1 + (NCHUNK - 1), 1), :].rearrange("p a b -> p (a b)"), 2, HEAD)
                    nc.vector.tensor_tensor(S[:, d], Sn[:, d], ends, ALU.mult).then_inc(by_dve[d], 1)
                assert k[0] == per_own


def gate_bonus_pool(nc, q, kd_sum, r_k, consts, v, pool_scale, io, saved):
    pad = max(WINDOWS) // 2
    gate_dram, bonus_dram, pool_dram = saved
    with ExitStack() as ctx:
        signal = Signals(nc, ctx)

        def sb(name, *dims):
            return ctx.enter_context(nc.sbuf_tensor(name, [P, *dims], F32))

        L = T + 2 * pad
        up = sb("g_up_sb", 2, PAIRS * P)
        gate = sb("gate_sb", PAIRS, T)
        rk = sb("rk", PAIRS, T)
        wide = sb("pool_in", 4, L)
        s = sb("pool_sums", 2, L)
        pooled = sb("pooled", 4, T)
        w_sb = sb("pool_w_sb", 4, P)
        ic = sb("inv_counts_sb", 4, T)
        out = ctx.enter_context(nc.psum_tensor("gb_out", [P, 2, PAIRS, T], F32))
        up_in, pool_in, sig, gates, sums, made, rks, bonuses, stored = map(signal, (
            "g_up_in", "pool_constants", "gate_sigmoids", "gate_products", "bonus_sums", "gates_made", "bonus_terms",
            "bonuses_made", "saved_stored"))
        padded, pooled_s, mixed_s, scaled, own = map(signal, (
            "pool_padded", "pool_pooled", "pool_products", "pool_scaled", "pool_own"))
        block = ctx.enter_context(nc.Block())

        @block.sync
        def _(sp):
            sp.dma_start(up[:, :, :], io["g_up"].rearrange("p (a n) -> p a n", a=2)).then_inc(up_in, 16)
            sp.dma_start(ic[:, :, :], io["inv_counts"].rearrange("p (g n) -> p g n", g=4)).then_inc(pool_in, 16)
            sp.dma_start(w_sb[:, :, :], io["pool_w"].rearrange("p (g n) -> p g n", g=4)).then_inc(pool_in, 16)
            sp.wait_ge(made, PAIRS)
            sp.dma_start(gate_dram, gate[:, :, :].rearrange("p a t -> p (a t)")).then_inc(stored, 16)
            sp.wait_ge(bonuses, PAIRS)
            sp.dma_start(bonus_dram, rk[:, :, :].rearrange("p a t -> p (a t)")).then_inc(stored, 16)
            for g in range(0, 4, 2):
                sp.wait_ge(scaled, g + 2)
                sp.dma_start(pool_dram[:, g * T:(g + 2) * T], pooled[:, g:g + 2].rearrange("p g t -> p (g t)")).then_inc(stored, 16)
            sp.wait_ge(stored, 64)

        @block.scalar
        def _(act):
            act.wait_ge(own, 1)
            nc.scalar.copy(wide[:, :, pad:pad + T], q[:, B_POOL:B_POOL + 4, :]).then_inc(padded, 1)
            nc.scalar.activation(q[:, B_GD:B_GD + 2], q[:, B_GD:B_GD + 2], ACT.Sigmoid).then_inc(sig, 1)
            nc.scalar.copy(v[:, :, :], q[:, B_V:B_V + PAIRS])
            for p in range(PAIRS):
                act.wait_ge(gates, p + 1)
                nc.scalar.copy(gate[:, p], out[:, 0, p]).then_inc(made, 1)
            for g in range(4):
                act.wait_ge(mixed_s, g + 1)
                nc.scalar.activation(pooled[:, g], out[:, 0, g], ACT.Copy, scale=pool_scale[:, g:g + 1]).then_inc(scaled, 1)

        @block.tensor
        def _(pe):
            pe.wait_ge(up_in, 16)
            pe.wait_ge(sig, 1)
            for p in range(PAIRS):
                cols = slice(p * P, (p + 1) * P)
                nc.tensor.matmul(out[:, 0, p], up[:, 0, cols], q[:, B_GD], start=True, stop=False)
                nc.tensor.matmul(out[:, 0, p], up[0:GATE_REST, 1, cols], q[0:GATE_REST, B_GD + 1],
                                 start=False, stop=True).then_inc(gates, 1)
            for p in range(PAIRS):
                pe.wait_ge(rks, p + 1)
                nc.tensor.matmul(out[:, 1, p], consts("heads"), rk[:, p], start=True, stop=True).then_inc(sums, 1)
            pe.wait_ge(pool_in, 32)
            for g in range(4):
                pe.wait_ge(made, g + 1)
                pe.wait_ge(pooled_s, g + 1)
                nc.tensor.matmul(out[:, 0, g], w_sb[:, g], pooled[:, g], start=True, stop=True).then_inc(mixed_s, 1)

        @block.vector
        def _(dve):
            o = Own(dve, own)
            nc.vector.memset(wide[:, :, 0:pad], 0.0)
            o.add(nc.vector.memset(wide[:, :, pad + T:L], 0.0))
            for p in range(PAIRS):
                nc.vector.scalar_tensor_tensor(out=rk[:, p], in0=q[:, B_R + p], scalar=r_k[:, p:p + 1], in1=kd_sum[:, p],
                                               op0=ALU.mult, op1=ALU.mult).then_inc(rks, 1)

            def pool(g):
                src, n, step, j = wide[:, g], L, 1, 0
                while step < WINDOWS[g]:
                    n -= step
                    dst = s[:, j]
                    o.link(nc.vector.tensor_tensor(dst[:, 0:n], src[:, 0:n], src[:, step:step + n], ALU.add))
                    src, j, step = dst, 1 - j, 2 * step
                first = pad - WINDOWS[g] // 2
                o.link(nc.vector.tensor_tensor(pooled[:, g], src[:, first:first + T], ic[:, g], ALU.mult))
                nc.vector.tensor_tensor(pooled[:, g], pooled[:, g], wide[:, g, pad:pad + T], ALU.subtract).then_inc(pooled_s, 1)

            dve.wait_ge(padded, 1)
            dve.wait_ge(pool_in, 32)
            for g in range(3):
                pool(g)
            for p in range(PAIRS):
                dve.wait_ge(sums, p + 1)
                nc.vector.tensor_tensor(rk[:, p], out[:, 1, p], q[:, B_V + p], ALU.mult).then_inc(bonuses, 1)
            pool(3)


def head_norm(nc, o, lnw, lnb, consts, saved, y):
    with ExitStack() as ctx:
        signal = Signals(nc, ctx)
        c = ctx.enter_context(nc.sbuf_tensor("centred", [P, PAIRS, T], F32))
        sq = ctx.enter_context(nc.sbuf_tensor("centred_sq", [P, PAIRS, T], F32))
        gate = ctx.enter_context(nc.sbuf_tensor("gate_again", [P, PAIRS, T], F32))
        bonus = ctx.enter_context(nc.sbuf_tensor("bonus_again", [P, PAIRS, T], F32))
        epst = ctx.enter_context(nc.sbuf_tensor("gn_eps", [P, 1], F32))
        out = ctx.enter_context(nc.psum_tensor("gn_out", [P, 2, PAIRS, T], F32))
        got = signal("saved_in")
        added = signal("directions_added")
        means = signal("head_means")
        squares = signal("head_squares")
        variances = signal("head_variances")
        roots = signal("head_roots")
        own = signal("gn_own")
        block = ctx.enter_context(nc.Block())

        @block.sync
        def _(sp):
            for dst, src in ((gate[:, :, :], saved[0]), (bonus[:, :, :], saved[1]), (y[:, PAIRS:2 * PAIRS], saved[2])):
                sp.dma_start(dst, src.rearrange("p (a t) -> p a t", a=PAIRS)).then_inc(got, 16)
            sp.wait_ge(got, 48)

        @block.tensor
        def _(pe):
            for p in range(PAIRS):
                pe.wait_ge(added, p + 1)
                nc.tensor.matmul(out[:, 0, p], consts("heads"), o[:, 0, p], start=True, stop=True).then_inc(means, 1)
            for p in range(PAIRS):
                pe.wait_ge(squares, p + 1)
                nc.tensor.matmul(out[:, 1, p], consts("heads"), sq[:, p], start=True, stop=True).then_inc(variances, 1)

        @block.scalar
        def _(act):
            act.wait_ge(own, 1)
            for p in range(PAIRS):
                act.wait_ge(variances, p + 1)
                nc.scalar.activation(sq[:, p], out[:, 1, p], ACT.Sqrt, bias=epst[:, 0:1], scale=1.0 / HEAD).then_inc(roots, 1)

        @block.vector
        def _(dve):
            k = Own(dve, own)
            k.add(nc.vector.memset(epst[:, :], GN_EPS))
            for p in range(PAIRS):
                nc.vector.tensor_tensor(o[:, 0, p], o[:, 0, p], o[:, 1, p], ALU.add).then_inc(added, 1)
            for p in range(PAIRS):
                dve.wait_ge(means, p + 1)
                k.link(nc.vector.scalar_tensor_tensor(out=c[:, p], in0=out[:, 0, p], scalar=-1.0 / HEAD, in1=o[:, 0, p],
                                                      op0=ALU.mult, op1=ALU.add))
                nc.vector.tensor_tensor(sq[:, p], c[:, p], c[:, p], ALU.mult).then_inc(squares, 1)
            dve.wait_ge(got, 48)
            for p in range(PAIRS):
                dve.wait_ge(roots, p + 1)
                k.link(nc.vector.reciprocal(o[:, 0, p], sq[:, p]))
                k.link(nc.vector.tensor_tensor(c[:, p], c[:, p], o[:, 0, p], ALU.mult))
                k.link(nc.vector.scalar_tensor_tensor(out=c[:, p], in0=c[:, p], scalar=lnw[:, p:p + 1], in1=bonus[:, p],
                                                      op0=ALU.mult, op1=ALU.add))
                nc.vector.scalar_tensor_tensor(out=y[:, p], in0=c[:, p], scalar=lnb[:, p:p + 1], in1=gate[:, p],
                                               op0=ALU.add, op1=ALU.mult)



def turn(nc, tag, pairs, ident, width=P):
    groups = len(pairs)
    with ExitStack() as ctx:
        signal = Signals(nc, ctx)
        out = ctx.enter_context(nc.psum_tensor(f"{tag}_turned", [P, 4, 4, P], F32))
        turned = signal(f"{tag}_turned_s")
        taken = [signal(f"{tag}_taken{e}") for e in range(2)]
        block = ctx.enter_context(nc.Block())

        @block.tensor
        def _(pe):
            for g, (srcs, _) in enumerate(pairs):
                if g >= 4:
                    pe.wait_ge(taken[g % 2], (g - 4) // 2 + 1)
                for j, s in enumerate(srcs):
                    mm = nc.tensor.transpose(out[:, g % 4, j, :], s, ident)
                mm.then_inc(turned, 1)

        def take(e):
            def body(eng):
                for g in range(e, groups, 2):
                    eng.wait_ge(turned, g + 1)
                    dst = pairs[g][1]
                    src = out[:, g % 4, :, 0:dst.shape[-1]]
                    (nc.scalar.copy if e else nc.vector.tensor_copy)(dst, src).then_inc(taken[e], 1)
            return body

        block.vector(take(0))
        block.scalar(take(1))


SLOTS_IN_GROUP = 2
GROUPS = 4
ROUND = SLOTS_IN_GROUP * GROUPS
SEGMENTS = 8
HALVES = (slice(0, PH // 2), slice(PH // 2, PH))
ID_SLOTS = 16


def peer(nc, h_tok, qT, keys, consts, u_tab, v_tab):
    with ExitStack() as ctx:
        signal = Signals(nc, ctx)

        def sb(name, *shape, dt=F32):
            return ctx.enter_context(nc.sbuf_tensor(name, [P, *shape], dt))

        kT = sb("keys_sb", 2 * PH, P)
        s = sb("key_scores", 2 * PH, N_KEYS)
        s2 = sb("key_scores2", 2 * PH, N_KEYS)
        val = sb("key_vals", PH, 2, TOPK)
        ix = sb("key_idx", PH, 2, TOPK, dt=U32)
        ixf = sb("key_idxf", PH, 2, TOPK)
        cand = sb("cand", PH, TOPK, TOPK)
        cand2 = sb("cand2", PH, TOPK, TOPK)
        sc = sb("cand_vals", PH, TOPK)
        pos = sb("cand_pos", PH, TOPK, dt=U32)
        part = sb("cand_part", 2, PH, TOPK, dt=U32)
        partf = sb("cand_partf", 2, PH, TOPK)
        pick = sb("pick", 2, PH, TOPK)
        flat = sb("flat_idx", SLOTS)
        ssum = sb("gate_sum", PH)
        rsum = sb("gate_rsum", PH)
        e = sb("gate_e", PH, TOPK)
        idx = sb("expert_idx", TT, SLOTS, dt=U32)
        gate = sb("expert_gate", TT, SLOTS)
        u = sb("u_rows", ROUND, D)
        v = sb("v_rows", ROUND, D)
        ids = sb("expert_ids", 2, ID_SLOTS, dt=U32)
        dot = sb("expert_dots", ROUND)
        act_ = sb("expert_acts", ROUND)
        diag = sb("weight_diagonals", ROUND, P)
        h_now = sb("h_now", D)
        zero = sb("zero_weights", P)
        scores = ctx.enter_context(nc.psum_tensor("score_out", [P, 2 * PH, N_KEYS], F32))
        total = ctx.enter_context(nc.psum_tensor("expert_total", [P, 2, T], F32))

        keys_in, scored, copied, routed, shifted, exped, own, pace = map(signal, (
            "keys_in", "scores_ready", "scores_copied", "tile_routed", "gate_shifted", "gate_exped", "route_own", "pace"))
        u_in = [signal(f"u_rows_in{b}") for b in range(GROUPS)]
        v_in = [signal(f"v_rows_in{b}") for b in range(GROUPS)]
        h_ready, dots, gelus, diagonals, used, ids_out, tile_done, tile_out, zeroed, pace_p = map(signal, (
            "h_now_ready", "dots_ready", "gelus_ready", "diagonals_ready", "rows_used", "ids_laid_out",
            "tile_summed", "tile_stored", "zero_ready", "pace_pool"))
        rounds = SLOTS // ROUND
        per_segment = rounds // SEGMENTS
        groups = SLOTS // SLOTS_IN_GROUP
        block = ctx.enter_context(nc.Block())

        @block.sync
        def _(sp):
            sp.dma_start(kT[:, :, :], keys.rearrange("p (a n) -> p a n", n=P)).then_inc(keys_in, 16)

        @block.gpsimd
        def _(pool):
            halves = 2
            per_half = ID_SLOTS // SLOTS_IN_GROUP
            pool.sem_inc(used, GROUPS)
            turns = SLOTS // (2 * halves * ID_SLOTS)
            with pool.Fori(0, 2 * TT) as ht:
                hold(pool, routed, ht + 2, pace_p)
                with pool.Fori(0, turns) as r:
                    for b in range(halves):
                        n = ht * (turns * halves) + r * halves + b
                        nc.gpsimd.tensor_copy(ids[:, b], idx[:, :, :].rearrange("p t s -> p (t s)")[:, DS(n * ID_SLOTS, ID_SLOTS)]
                                              ).then_inc(ids_out, 1)
                        hold(pool, ids_out, n + 1, pace_p)
                        for k in range(per_half):
                            g = n * per_half + k
                            hold(pool, used, g + 1, pace_p)
                            first = k % GROUPS * SLOTS_IN_GROUP
                            for tab, rows, sem in ((u_tab, u, u_in), (v_tab, v, v_in)):
                                for j in range(SLOTS_IN_GROUP):
                                    at = k * SLOTS_IN_GROUP + j
                                    nc.gpsimd.indirect_dma_start(
                                        out=rows[:, first + j], out_offset=None, in_=tab,
                                        in_offset=bass.IndirectOffsetOnAxis(ap=ids[:, b, at:at + 1], axis=0)
                                    ).then_inc(sem[k % GROUPS], 16)

        @block.tensor
        def _(pe):
            def score(t):
                for j in range(2 * PH):
                    mm = nc.tensor.matmul(scores[:, j], qT[:, j, t * P:(t + 1) * P], kT[:, j], start=True, stop=True)
                mm.then_inc(scored, 1)

            def add_zero(**flags):
                for half in range(2):
                    mm = nc.tensor.matmul(total[:, half], zero[:, :], consts("reset"), **flags)
                return mm

            pe.wait_ge(keys_in, 16)
            score(0)
            pe.wait_ge(zeroed, 1)
            for t in range(TT):
                if t + 1 < TT:
                    pe.wait_ge(copied, t + 1)
                    score(t + 1)
                if t:
                    pe.wait_ge(tile_out, t)
                add_zero(start=True, stop=False)
                with pe.Fori(0, rounds) as r:
                    for b in range(GROUPS):
                        pe.wait_ge(diagonals, r * GROUPS + (t * groups + b + 1))
                        pe.wait_ge(v_in[b], (r + (t * rounds + 1)) * (16 * SLOTS_IN_GROUP))
                        for j in range(SLOTS_IN_GROUP):
                            at = b * SLOTS_IN_GROUP + j
                            for half in range(2):
                                mm = nc.tensor.matmul(total[:, half], diag[:, at], v[:, at, half * T:(half + 1) * T],
                                                      start=False, stop=False)
                        mm.then_inc(used, 1)
                add_zero(start=False, stop=True).then_inc(tile_done, 1)

        @block.scalar
        def _(act):
            def take_scores(t):
                act.wait_ge(scored, t + 1)
                for j in range(0, 2 * PH, 4):
                    ins = nc.scalar.copy(s[:, j:j + 4], scores[:, j:j + 4])
                ins.then_inc(copied, 1)

            def exponentials(count, heads=slice(0, PH)):
                act.wait_ge(shifted, count)
                nc.scalar.activation(e[:, heads], e[:, heads], ACT.Exp).then_inc(exped, 1)

            def this_h(t):
                nc.scalar.copy(h_now[:, :], h_tok[:, DS(t, 1), :].rearrange("p a d -> p (a d)")).then_inc(h_ready, 1)

            def gelu(t, segment, n):
                with act.Fori(0, per_segment * n) as i:
                    for b in range(GROUPS):
                        g = t * groups + i * GROUPS + (segment * per_segment * GROUPS + b)
                        act.wait_ge(dots, g + 1)
                        at = slice(b * SLOTS_IN_GROUP, (b + 1) * SLOTS_IN_GROUP)
                        nc.scalar.activation(act_[:, at], dot[:, at], ACT.Gelu).then_inc(gelus, 1)

            def store(t):
                hold(act, tile_done, t + 1, pace_p)
                nc.scalar.copy(h_tok[:, DS(t, 1), :].rearrange("p a (b d) -> p (a b) d", b=2), total[:, :, :]).then_inc(tile_out, 1)

            take_scores(0)
            this_h(0)
            for n, heads in enumerate(HALVES):
                exponentials(n + 1, heads)
            with act.Fori(0, TT - 1) as t:
                act.wait_ge(routed, 2 * t + 3)
                take_scores(t + 1)
                gelu(t, 0, SEGMENTS - 1)
                exponentials(t + 3)
                gelu(t, SEGMENTS - 1, 1)
                this_h(t + 1)
                store(t)
            gelu(TT - 1, 0, SEGMENTS)
            store(TT - 1)

        @block.vector
        def _(dve):
            a = nc.vector
            per = 16
            hots = ((0, cand), (1, cand2))

            def row(x, h):
                return x[:, h].rearrange("p a b -> p (a b)")

            def route(t, piece, heads=slice(0, PH), base=None):
                n = [(0, 1, 2, 4, 6, 7, 9, 12)[piece]]
                base = (t + 1) * per if base is None else base
                some = range(heads.start, heads.stop)
                lists = [(h, p) for h in some for p in range(2)]
                slots = slice(heads.start * TOPK, heads.stop * TOPK)

                def step(ins):
                    ins.then_inc(own, 1)
                    n[0] += 1
                    hold(dve, own, base + n[0], pace)

                if piece == 0:
                    hold(dve, copied, t + 1, pace)
                    for h, p in lists:
                        ins = a.max(val[:, h, p, 0:8], s[:, 2 * h + p])
                    step(ins)
                elif piece == 1:
                    for h, p in lists:
                        a.max_index(ix[:, h, p, 0:8], val[:, h, p, 0:8], s[:, 2 * h + p])
                        ins = a.match_replace(s2[:, 2 * h + p], val[:, h, p, 0:8], s[:, 2 * h + p], GONE)
                    step(ins)
                elif piece == 2:
                    for h, p in lists:
                        ins = a.max(val[:, h, p, 8:16], s2[:, 2 * h + p])
                    step(ins)
                    for h, p in lists:
                        ins = a.max_index(ix[:, h, p, 8:16], val[:, h, p, 8:16], s2[:, 2 * h + p])
                    step(ins)
                elif piece == 3:
                    a.tensor_copy(ixf[:, heads], ix[:, heads])
                    step(a.tensor_tensor(cand[:, heads], bcast(val[:, heads, 0, :], 3, TOPK), bcast(val[:, heads, 1, :], 2, TOPK), ALU.add))
                    for h in some:
                        ins = a.max(sc[:, h, 0:8], row(cand, h))
                    step(ins)
                elif piece == 4:
                    for h in some:
                        a.max_index(pos[:, h, 0:8], sc[:, h, 0:8], row(cand, h))
                        ins = a.match_replace(row(cand2, h), sc[:, h, 0:8], row(cand, h), GONE)
                    step(ins)
                elif piece == 5:
                    for h in some:
                        ins = a.max(sc[:, h, 8:16], row(cand2, h))
                    step(ins)
                    a.tensor_tensor(e[:, heads], sc[:, heads], bcast(sc[:, heads, 0], 2, TOPK), ALU.subtract).then_inc(shifted, 1)
                    for h in some:
                        ins = a.max_index(pos[:, h, 8:16], sc[:, h, 8:16], row(cand2, h))
                    step(ins)
                elif piece == 6:
                    a.tensor_scalar(part[:, 0, heads], pos[:, heads], 4, None, ALU.logical_shift_right)
                    step(a.tensor_scalar(part[:, 1, heads], pos[:, heads], 15, None, ALU.bitwise_and))
                    step(a.tensor_copy(partf[:, :, heads], part[:, :, heads]))
                    slot = bcast(bcast(consts("slot"), 1, TOPK), 1, len(some))
                    for p, hot in hots:
                        ins = a.tensor_tensor(hot[:, heads], bcast(partf[:, p, heads], 3, TOPK), slot, ALU.is_equal)
                    step(ins)
                else:
                    for p, hot in hots:
                        ins = a.tensor_tensor(hot[:, heads], hot[:, heads], bcast(ixf[:, heads, p, :], 2, TOPK), ALU.mult)
                    step(ins)
                    for p, hot in hots:
                        ins = a.tensor_reduce(pick[:, p, heads], hot[:, heads], AX.X, ALU.add)
                    hold(dve, exped, t + 2 if heads.stop - heads.start == PH else heads.stop * 2 // PH, pace)
                    step(a.tensor_reduce(ssum[:, heads], e[:, heads], AX.X, ALU.add))
                    a.reciprocal(rsum[:, heads], ssum[:, heads])
                    step(a.scalar_tensor_tensor(out=flat[:, slots], in0=pick[:, 0, heads].rearrange("p a b -> p (a b)"), scalar=float(N_KEYS),
                                                in1=pick[:, 1, heads].rearrange("p a b -> p (a b)"), op0=ALU.mult, op1=ALU.add))
                    a.tensor_copy(idx[:, DS(t, 1), slots].rearrange("p a s -> p (a s)"), flat[:, slots])
                    step(a.tensor_tensor(gate[:, DS(t, 1), slots].rearrange("p a (h k) -> p (a h) k", k=TOPK), e[:, heads],
                                         bcast(rsum[:, heads], 2, TOPK), ALU.mult))
                    assert n[0] == per, n
                    dve.sem_inc(routed, 2 if len(some) == PH else 1)
                assert n[0] == (1, 2, 4, 6, 7, 9, 12, 16)[piece], (piece, n)

            def segment(t, k, n):
                with dve.Fori(0, per_segment * n) as i:
                    r = t * rounds + i + k * per_segment
                    for b in range(GROUPS + 1):
                        if b < GROUPS:
                            dve.wait_ge(u_in[b], (r + 1) * (16 * SLOTS_IN_GROUP))
                            for j in range(SLOTS_IN_GROUP):
                                at = b * SLOTS_IN_GROUP + j
                                ins = a.tensor_tensor_reduce(out=u[:, at], in0=u[:, at], in1=h_now[:, :], scale=1.0, scalar=0.0,
                                                             op0=ALU.mult, op1=ALU.add, accum_out=dot[:, at:at + 1])
                            ins.then_inc(dots, 1)
                        if b > 0:
                            g = r * GROUPS + (b - 1)
                            dve.wait_ge(gelus, g + 1)
                            for j in range(SLOTS_IN_GROUP):
                                at = (b - 1) * SLOTS_IN_GROUP + j
                                ins = a.tensor_scalar(diag[:, at], consts("ident"), act_[:, at:at + 1],
                                                      gate[:, :, :].rearrange("p t s -> p (t s)")[:, DS(r * ROUND + at, 1)],
                                                      ALU.mult, ALU.mult)
                            ins.then_inc(diagonals, 1)

            dve.sem_inc(routed, 1)
            a.memset(zero[:, :], 0.0).then_inc(zeroed, 1)
            for half, heads in enumerate(HALVES):
                for piece in range(8):
                    route(0, piece, heads, half * per)
            with dve.Fori(0, TT - 1) as t:
                hold(dve, h_ready, t + 1, pace)
                for k in range(SEGMENTS):
                    segment(t, k, 1)
                    for piece in ((0, 1), (2,), (3,), (4,), (5,), (6,), (7,), ())[k]:
                        route(t + 1, piece)
            hold(dve, h_ready, TT, pace)
            segment(TT - 1, 0, SEGMENTS)


def add_turned(nc, tag, x, tok, ident):
    with ExitStack() as ctx:
        signal = Signals(nc, ctx)
        out = ctx.enter_context(nc.psum_tensor(f"{tag}_back", [P, 4, T], F32))
        turned = signal(f"{tag}_back_turned")
        added = signal(f"{tag}_back_added")
        block = ctx.enter_context(nc.Block())

        @block.tensor
        def _(pe):
            for k in range(KD):
                if k >= 4:
                    pe.wait_ge(added, k - 3)
                for t in range(TT):
                    mm = nc.tensor.transpose(out[:, k % 4, t * P:(t + 1) * P], tok[:, t, k * P:(k + 1) * P], ident)
                mm.then_inc(turned, 1)

        @block.vector
        def _(dve):
            for k in range(KD):
                dve.wait_ge(turned, k + 1)
                nc.vector.tensor_tensor(x[:, k], out[:, k % 4], x[:, k], ALU.add).then_inc(added, 1)



def rope(nc, pr, swap, tables):
    with ExitStack() as ctx:
        signal = Signals(nc, ctx)
        tab = ctx.enter_context(nc.sbuf_tensor("rope_tab", [P, 2, T], F32))
        tmp = ctx.enter_context(nc.sbuf_tensor("rope_tmp", [P, 2, T], F32))
        out = ctx.enter_context(nc.psum_tensor("rope_out", [P, 2, T], F32))
        got = signal("rope_in")
        swapped = signal("rope_swapped")
        free = signal("rope_free")
        own = signal("rope_own")
        scaled = signal("rope_scaled")
        pace = signal("rope_pace")
        rounds = 5
        first = (C_QB, C_QI)
        block = ctx.enter_context(nc.Block())

        def blk(b, i):
            return pr[:, DS(i + first[b], 1), :].rearrange("p a t -> p (a t)")

        @block.sync
        def _(sp):
            sp.dma_start(tab[:, :, :], tables.rearrange("p (a t) -> p a t", a=2)).then_inc(got, 16)

        @block.tensor
        def _(pe):
            with pe.Fori(0, rounds) as i:
                for b in range(2):
                    pe.wait_ge(free, 2 * i + b + 1)
                    nc.tensor.matmul(out[:, b], swap, blk(b, i), start=True, stop=True).then_inc(swapped, 1)

        @block.vector
        def _(dve):
            dve.sem_inc(free, 2)
            dve.wait_ge(got, 16)
            with dve.Fori(0, rounds) as i:
                for b in range(2):
                    dve.wait_ge(swapped, 2 * i + b + 1)
                    nc.vector.tensor_tensor(tmp[:, b], out[:, b], tab[:, 1], ALU.mult).then_inc(free, 1)
                for b in range(2):
                    dve.wait_ge(free, 2 * i + b + 3)
                    dve.wait_ge(scaled, 2 * i + b + 1)
                    nc.vector.tensor_tensor(blk(b, i), blk(b, i), tmp[:, b], ALU.add).then_inc(own, 1)
                dve.wait_ge(own, 2 * i + 2)

        @block.gpsimd
        def _(pool):
            pool.wait_ge(got, 16)
            with pool.Fori(0, rounds) as i:
                for b in range(2):
                    hold(pool, swapped, 2 * i + b + 1, pace)
                    nc.gpsimd.tensor_tensor(blk(b, i), blk(b, i), tab[:, 0], ALU.mult).then_inc(scaled, 1)


def index_scores(nc, pr, w_tok, score, m, line, lines, toe):
    with ExitStack() as ctx:
        signal = Signals(nc, ctx)
        relu = ctx.enter_context(nc.sbuf_tensor("index_relu", [P, 4, T], F32))
        ws = ctx.enter_context(nc.sbuf_tensor("index_w", [P, TT, 8], F32))
        out = ctx.enter_context(nc.psum_tensor("index_out", [P, 4, T], F32))
        dots = signal("index_dots")
        relus = signal("index_relus")
        added = signal("index_added")
        weighted = signal("index_weighted")
        spread = signal("bias_spread")
        turned = signal("bias_in")
        units = [(t, h) for h in range(8) for t in range(1, TT)]
        L = line.shape[1]
        block = ctx.enter_context(nc.Block())

        @block.sync
        def _(sp):
            sp.dma_start(bass.AP(lines.tensor, 0, [[P * L, 8], [L, P], [1, L]]),
                         bass.AP(line.tensor, 0, [[L, 8], [0, P], [1, L]])).then_inc(spread, 16)
            sp.wait_ge(spread, 16)
            sp.dma_start(toe[:, :, :], bass.AP(lines.tensor, P - 1, [[L - 1, P], [P * L, 8], [1, T]])).then_inc(turned, 16)

        @block.tensor
        def _(pe):
            for n, (t, h) in enumerate(units):
                if n >= 4:
                    pe.wait_ge(relus, n - 3)
                rows = slice(HEAD * (h % 2), HEAD * (h % 2) + HEAD)
                keys = P * (t + 1)
                nc.tensor.matmul(out[:, n % 4, 0:keys], pr[rows, C_QI + h // 2, t * P:(t + 1) * P], pr[rows, C_KI, 0:keys],
                                 start=True, stop=True).then_inc(dots, 1)

        @block.scalar
        def _(act):
            for n, (t, h) in enumerate(units):
                act.wait_ge(dots, n + 1)
                if n >= 4:
                    act.wait_ge(added, n - 3)
                keys = P * (t + 1)
                nc.scalar.activation(relu[:, n % 4, 0:keys], out[:, n % 4, 0:keys], ACT.Relu, scale=HEAD ** -0.5).then_inc(relus, 1)

        @block.vector
        def _(dve):
            a = nc.vector
            a.memset(score[:, :, :], 0.0)
            a.memset(m[:, :, :], 0.0)
            a.tensor_scalar(ws[:, :, :], w_tok[:, :, 0:8], 8 ** -0.5, None, ALU.mult).then_inc(weighted, 1)
            dve.wait_ge(weighted, 1)
            a.memset(m[0:HEAD, 0, HEAD:P], NEG)
            for n, (t, h) in enumerate(units):
                keys = P * (t + 1)
                dve.wait_ge(relus, n + 1)
                if n >= 3:
                    dve.wait_ge(added, n - 2)
                a.scalar_tensor_tensor(out=score[:, t - 1, 0:keys], in0=relu[:, n % 4, 0:keys], scalar=ws[:, t, h:h + 1],
                                       in1=score[:, t - 1, 0:keys], op0=ALU.mult, op1=ALU.add).then_inc(added, 1)
            dve.wait_ge(added, len(units))
            for t in range(1, TT):
                a.memset(score[0:HEAD, t - 1, P * (t + 1) - HEAD:P * (t + 1)], NEG)
            dve.wait_ge(turned, 16)
            a.memset(toe[0:HEAD, :, T - HEAD:T], NEG)


class BestKeys:

    PIECES = 2 * (IDX_TOPK // 8) // PAIRS

    def __init__(self, nc, ctx, score, m):
        self.score, self.m = score, m
        self.top = ctx.enter_context(nc.sbuf_tensor("index_top", [P, 3, 8], F32))

    def signals(self, signal):
        self.own, self.pace = signal("index_own"), signal("index_pace")

    def start(self, nc, dve):
        dve.sem_inc(self.own, 1)

    def piece(self, nc, dve, i, step):
        hold(dve, self.own, self.PIECES * i + step + 1, self.pace)
        for t in range(1, TT):
            s, top = self.score[:, t - 1, 0:P * (t + 1)], self.top[:, t - 1]
            if step % 2 == 0:
                ins = nc.vector.max(top, s)
            else:
                ins = nc.vector.match_replace(s, top, s, GONE)
        ins.then_inc(self.own, 1)

    def finish(self, nc, dve):
        dve.wait_ge(self.own, self.PIECES * PAIRS + 1)
        for t in range(1, TT):
            s = self.score[:, t - 1, 0:P * (t + 1)]
            ins = nc.vector.tensor_scalar(s, s, GONE, -1.0, ALU.is_equal, ALU.add)
        ins.then_inc(self.own, 1)
        dve.wait_ge(self.own, self.PIECES * PAIRS + 2)
        for t in range(1, TT):
            nc.vector.tensor_scalar(self.m[:, t, 0:P * (t + 1)], self.score[:, t - 1, 0:P * (t + 1)], -NEG, None, ALU.mult)


def attention(nc, tag, q_of, k_of, v_of, bias_of, ident, o, aside=None):
    SB, PB = 4, 4
    with ExitStack() as ctx:
        signal = Signals(nc, ctx)
        qs = ctx.enter_context(nc.sbuf_tensor(f"{tag}_q", [P, T], F32))
        ks = ctx.enter_context(nc.sbuf_tensor(f"{tag}_k", [P, T], F32))
        vs = ctx.enter_context(nc.sbuf_tensor(f"{tag}_v", [P, TT, P], F32))
        prob = ctx.enter_context(nc.sbuf_tensor(f"{tag}_p", [P, SB, T], F32))
        pT = ctx.enter_context(nc.sbuf_tensor(f"{tag}_pT", [P, 2, T], F32))
        mx = ctx.enter_context(nc.sbuf_tensor(f"{tag}_mx", [P, SB], F32))
        nm = ctx.enter_context(nc.sbuf_tensor(f"{tag}_nm", [P, SB], F32))
        sm = ctx.enter_context(nc.sbuf_tensor(f"{tag}_sm", [P, SB], F32))
        rc = ctx.enter_context(nc.sbuf_tensor(f"{tag}_rc", [P, SB], F32))
        s_ps = ctx.enter_context(nc.psum_tensor(f"{tag}_s_ps", [P, PB, T], F32))
        t_ps = ctx.enter_context(nc.psum_tensor(f"{tag}_t_ps", [P, 2, T], F32))
        o_ps = ctx.enter_context(nc.psum_tensor(f"{tag}_o_ps", [P, T], F32))

        def sem(name):
            return signal(f"{tag}_{name}")

        qk_in, v_in, scored, biased, shifted, exped, normed = map(
            sem, ("qk_in", "v_in", "scored", "biased", "shifted", "exped", "normed"))
        turned, taken, summed, stored, own, pace = map(sem, ("turned", "taken", "summed", "stored", "own", "pace"))
        units = [(hh, t) for hh in range(2) for t in range(TT)]
        NU = len(units)
        if aside:
            aside.signals(signal)
        block = ctx.enter_context(nc.Block())

        @block.gpsimd
        def _(pool):
            def load(i, after=None):
                if after is not None:
                    pool.wait_ge(scored, NU * after + NU)
                nc.gpsimd.tensor_copy(qs[:, :], q_of(i))
                nc.gpsimd.tensor_copy(ks[:, :], k_of(i)).then_inc(qk_in, 1)
                if after is not None:
                    hold(pool, summed, NU * after + NU + 2, pace)
                nc.gpsimd.tensor_copy(vs[:, :, :], v_of(i)).then_inc(v_in, 1)

            load(0)
            with pool.Fori(0, PAIRS - 1) as i:
                load(i + 1, i)

        @block.tensor
        def _(pe):
            pe.sem_inc(turned, SB)
            pe.sem_inc(summed, 2)
            with pe.Fori(0, PAIRS) as i:
                pe.wait_ge(qk_in, i + 1)
                for step in range(NU + 3):
                    if step < NU:
                        u = step
                        hh, t = units[u]
                        rows = slice(HEAD * hh, HEAD * hh + HEAD)
                        keys = P * (t + 1)
                        pe.wait_ge(biased, NU * i + u + 1)
                        nc.tensor.matmul(s_ps[:, u % PB, 0:keys],
                                         qs[rows, t * P:(t + 1) * P], ks[rows, 0:keys],
                                         start=True, stop=True).then_inc(scored, 1)
                    if 2 <= step < NU + 2:
                        u = step - 2
                        hh, t = units[u]
                        pe.wait_ge(normed, NU * i + u + 1)
                        pe.wait_ge(taken, NU * i + u + 1)
                        for j in range(t + 1):
                            mm = nc.tensor.transpose(t_ps[:, u % 2, j * P:(j + 1) * P], prob[:, u % SB, j * P:(j + 1) * P], ident)
                        mm.then_inc(turned, 1)
                    if 3 <= step:
                        u = step - 3
                        hh, t = units[u]
                        rows = slice(HEAD * hh, HEAD * hh + HEAD)
                        if u == 0:
                            pe.wait_ge(v_in, i + 1)
                            pe.wait_ge(stored, i + 1)
                        pe.wait_ge(taken, NU * i + u + 3)
                        for j in range(t + 1):
                            mm = nc.tensor.matmul(o_ps[rows, t * P:(t + 1) * P], vs[:, j, rows], pT[:, u % 2, j * P:(j + 1) * P],
                                                  start=(j == 0), stop=(j == t))
                        mm.then_inc(summed, 1)

        @block.scalar
        def _(act):
            act.sem_inc(taken, 2)
            act.sem_inc(stored, 1)
            with act.Fori(0, PAIRS) as i:
                for step in range(NU + 2):
                    if step < NU:
                        u = step
                        hh, t = units[u]
                        keys = P * (t + 1)
                        act.wait_ge(shifted, NU * i + u + 1)
                        nc.scalar.activation(prob[:, u % SB, 0:keys], prob[:, u % SB, 0:keys], ACT.Exp,
                                             bias=nm[:, u % SB:u % SB + 1], accum_out=sm[:, u % SB:u % SB + 1]).then_inc(exped, 1)
                    if 2 <= step:
                        u = step - 2
                        hh, t = units[u]
                        keys = P * (t + 1)
                        act.wait_ge(turned, NU * i + u + SB + 1)
                        act.wait_ge(summed, NU * i + u + 1)
                        nc.scalar.copy(pT[:, u % 2, 0:keys], t_ps[:, u % 2, 0:keys]).then_inc(taken, 1)
                act.wait_ge(summed, NU * i + NU + 2)
                nc.scalar.copy(o[:, DS(i, 1), :].rearrange("p a t -> p (a t)"), o_ps[:, :]).then_inc(stored, 1)

        @block.vector
        def _(dve):
            dve.sem_inc(biased, PB)
            if aside:
                aside.start(nc, dve)
            per = 2 * NU
            with dve.Fori(0, PAIRS) as i:
                n = 0
                for step in range(NU + 1):
                    if step < NU:
                        u = step
                        hh, t = units[u]
                        keys = P * (t + 1)
                        c = slice(u % SB, u % SB + 1)
                        dve.wait_ge(scored, NU * i + u + 1)
                        dve.wait_ge(turned, NU * i + u + 1)
                        nc.vector.scalar_tensor_tensor(out=prob[:, u % SB, 0:keys], in0=s_ps[:, u % PB, 0:keys],
                                                       scalar=HEAD ** -0.5, in1=bias_of(i, hh, t), op0=ALU.mult,
                                                       op1=ALU.add).then_inc(biased, 1)
                        dve.wait_ge(biased, NU * i + u + 1 + PB)
                        nc.vector.tensor_reduce(mx[:, c], prob[:, u % SB, 0:keys], AX.X, ALU.max).then_inc(own, 1)
                        n += 1
                        dve.wait_ge(own, per * i + n)
                        nc.vector.tensor_scalar(nm[:, c], mx[:, c], -1.0, None, ALU.mult).then_inc(shifted, 1)
                    if 1 <= step:
                        u = step - 1
                        hh, t = units[u]
                        keys = P * (t + 1)
                        c = slice(u % SB, u % SB + 1)
                        dve.wait_ge(exped, NU * i + u + 1)
                        nc.vector.reciprocal(rc[:, c], sm[:, c]).then_inc(own, 1)
                        n += 1
                        dve.wait_ge(own, per * i + n)
                        nc.vector.tensor_scalar(prob[:, u % SB, 0:keys], prob[:, u % SB, 0:keys], rc[:, c], None,
                                                ALU.mult).then_inc(normed, 1)
                    if aside and step < aside.PIECES:
                        aside.piece(nc, dve, i, step)
                assert n == per
            if aside:
                aside.finish(nc, dve)



def load(nc, tag, *copies):
    with ExitStack() as ctx:
        signal = Signals(nc, ctx)
        got = signal(f"{tag}_loaded")
        block = ctx.enter_context(nc.Block())

        @block.sync
        def _(sp):
            for dst, src in copies:
                sp.dma_start(dst, src).then_inc(got, 16)
            sp.wait_ge(got, 16 * len(copies))


def parts(nc, ctx, tag, blocks):
    return [ctx.enter_context(nc.sbuf_tensor(f"{tag}_{n}", [P, blocks, T], F32R)) for n in ("hi", "lo")]


def swiglu_ffn(nc, tag, x, weight, consts, w_in, w_out):
    with ExitStack() as ctx:
        a = parts(nc, ctx, f"{tag}_a", KF)
        with ExitStack() as inner:
            h = parts(nc, inner, f"{tag}_h", KD)
            norm = Norm(nc, inner, f"{tag}_norm", x, weight, consts("ones"), RMS_EPS2)
            silu = inner.enter_context(nc.sbuf_tensor(f"{tag}_silu", [P, 2, T], F32))
            product = inner.enter_context(nc.sbuf_tensor(f"{tag}_product", [P, 2, T], F32))
            gemm(nc, f"{tag}_in", w_in, KD, [Operand(*h, x, weight)], 2 * KF, Swiglu(*a, silu, product, norm.rstd[:, :]), norm)
        gemm(nc, f"{tag}_out", w_out, KF, [Operand(*a)], KD, AddTo(x, 0.5))


def token_groups(src, blocks, dst):
    n = dst.shape[-1]
    return [([src[:, b, t * P:(t + 1) * P] for t in range(TT)], dst[:, :, j * P:min(n, (j + 1) * P)])
            for j, b in enumerate(blocks)]


def build(nc, io):
    out = io["out"]
    saved = [nc.dram_tensor(f"{n}_kept", [P, PAIRS * T], F32).ap() for n in ("gate", "bonus", "pool")]
    x_in = io["x"].rearrange("p (k t) -> p k t", k=KD)

    with ExitStack() as whole:
        const_sb = whole.enter_context(nc.sbuf_tensor("const_sb", [P, N_CONST], F32))
        vec_sb = whole.enter_context(nc.sbuf_tensor("vec_sb", [P, N_VEC], F32))

        def consts(name):
            at, n = C_AT[name]
            return const_sb[:, at:at + n]

        def vec(name):
            at, n = V_AT[name]
            return vec_sb[:, at:at + n]

        x = whole.enter_context(nc.sbuf_tensor("x", [P, KD, T], F32))
        load(nc, "start", (vec_sb[:, :], io["vec"]))
        with ExitStack() as s1:
            ar = s1.enter_context(nc.sbuf_tensor("ar", [P, 2, 2, PAIRS, T], F32))
            bk = s1.enter_context(nc.sbuf_tensor("bk", [P, 2, 2, PAIRS, T], F32))
            v = s1.enter_context(nc.sbuf_tensor("v_kept", [P, PAIRS, T], F32))
            w_end = s1.enter_context(nc.sbuf_tensor("w_end", [P, 2, NCHUNK, PAIRS], F32))
            with nc.sbuf_tensor("p_in", [P, N_IN1, T], F32) as q:
                with ExitStack() as s0:
                    h = parts(nc, s0, "h1", KD)
                    norm = Norm(nc, s0, "norm1", x, vec("norm1"), consts("ones"), RMS_EPS1,
                                sq=ar[:, 0].rearrange("p a b t -> p (a b) t"),
                                arrive=[(x[:, k], x_in[:, k]) for k in range(KD)] + [(const_sb[:, :], io["consts"])])
                    gemm(nc, "w_in", io["w_in"], KD, [Operand(*h, x, vec("norm1"))], N_IN1,
                         Shift(nc, s0, q, norm.rstd[:, :], vec("mu0"), vec("mu1")), norm)
                with nc.sbuf_tensor("kd_sum", [P, PAIRS, T], F32) as kd_sum:
                    with nc.sbuf_tensor("kk", [P, PAIRS, T], F32) as kk, nc.sbuf_tensor("lora", [P, 2, PAIRS * P], F32) as lora:
                        rwkv_operands(nc, q, lora, io["lora"], vec, consts, ar, bk, kk, kd_sum, w_end)
                    gate_bonus_pool(nc, q, kd_sum, vec("r_k"), consts, v, vec("pool_scale"), io, saved)
            o = ar[:, :, 0]
            recurrence(nc, ar, bk, v, w_end, consts, o)
            y = s1.enter_context(nc.sbuf_tensor("y", [P, 2 * PAIRS, T], F32))
            head_norm(nc, o, vec("lnw"), vec("lnb"), consts, saved, y)
            y_parts = parts(nc, s1, "y", 2 * PAIRS)
            gemm(nc, "w_out", io["w_out"], KD, [Operand(*y_parts, y)], KD, AddTo(x))

        with ExitStack() as s2:
            h_tok = s2.enter_context(nc.sbuf_tensor("h_tok", [P, TT, D], F32))
            qT = s2.enter_context(nc.sbuf_tensor("qT", [P, 2 * PH, T], F32))
            with ExitStack() as s0:
                h2 = s0.enter_context(nc.sbuf_tensor("h2", [P, KD, T], F32))
                h = parts(nc, s0, "h2", KD)
                norm = Norm(nc, s0, "norm2", x, vec("norm2"), consts("ones"), RMS_EPS1, normed=h2)
                gemm(nc, "wq", io["peer_wq"], KD, [Operand(*h, x, vec("norm2"))], 2 * PH,
                     Scale(lambda n: at_block(qT, n), norm.rstd[:, :]), norm)
                turn(nc, "h", token_groups(h2, range(KD), h_tok), consts("ident"))
            peer(nc, h_tok, qT, io["peer_keys"], consts, io["peer_u"], io["peer_v"])
            add_turned(nc, "peer", x, h_tok, consts("ident"))
            rmsnorm(nc, "norm_f", x, vec("norm_f"), consts("ones"), RMS_EPS1)

        swiglu_ffn(nc, "ffn1", x, vec("n1"), consts, io["ffn1_w_in"], io["ffn1_w_out"])
        with ExitStack() as s3:
            def sb(name, shape, dt=F32):
                return s3.enter_context(nc.sbuf_tensor(name, shape, dt))

            pr = sb("pr", [P, N_IN2, T])
            va, vb, wi = sb("va_tok", [P, TT, PAIRS * P]), sb("vb_tok", [P, TT, P]), sb("wi_tok", [P, TT, 8])
            oa, ob = sb("oa", [P, PAIRS, T]), sb("ob", [P, PAIRS, T])
            with ExitStack() as s0:
                h = parts(nc, s0, "h3", KD)
                norm = Norm(nc, s0, "n2", x, vec("n2"), consts("ones"), RMS_EPS2)
                gemm(nc, "w_in2", io["w_in_2"], KD, [Operand(*h, x, vec("n2"))], N_IN2,
                     Scale(lambda n: at_block(pr, n), norm.rstd[:, :]), norm)
            rope(nc, pr, consts("swap"), io["rope"])
            turn(nc, "values", token_groups(pr, range(C_VA, C_VA + 4), va) + token_groups(pr, [C_VB], vb)
                 + token_groups(pr, [C_WI], wi), consts("ident"))
            blk = lambda b: pr[:, b, :].rearrange("p a t -> p (a t)")
            m = s3.enter_context(nc.sbuf_tensor("mask_b", [P, TT, T], F32))
            line = io["bias_line"]
            lines = nc.dram_tensor("bias_lines", [8 * P, line.shape[1]], F32).ap()
            with ExitStack() as s0:
                toe = s0.enter_context(nc.sbuf_tensor("toeplitz", [P, 8, T], F32))
                score = s0.enter_context(nc.sbuf_tensor("index_scores", [P, TT - 1, T], F32))
                index_scores(nc, pr, wi, score, m, line, lines, toe)
                attention(nc, "atta", lambda i: blk(DS(i + C_QA, 1)), lambda i: blk(DS(i + C_KA, 1)),
                          lambda i: va[:, :, DS(i * P, P)],
                          lambda i, hh, t: toe[:, DS(2 * i + hh, 1), 3 * P - P * t:T].rearrange("p a t -> p (a t)"),
                          consts("ident"), oa, BestKeys(nc, s0, score, m))
            attention(nc, "attb", lambda i: blk(DS(i + C_QB, 1)), lambda i: pr[:, C_KB, :],
                      lambda i: vb[:, :, :], lambda i, hh, t: m[:, t, 0:P * (t + 1)], consts("ident"), ob)
            merged = pr[:, C_GA:C_GA + KD, :]
            with ExitStack() as s0:
                a_parts, b_parts = parts(nc, s0, "oa", PAIRS), parts(nc, s0, "ob", PAIRS)
                gemm(nc, "branches", io["w_branches"], PAIRS, [Operand(*a_parts, oa), Operand(*b_parts, ob)], 2 * KD,
                     Merge(merged, pr))
            m_parts = parts(nc, s3, "merged", KD)
            gemm(nc, "w_out2", io["w_out_2"], KD, [Operand(*m_parts, merged)], KD, AddTo(x))
        swiglu_ffn(nc, "ffn2", x, vec("n3"), consts, io["ffn2_w_in"], io["ffn2_w_out"])
        rmsnorm(nc, "nf", x, vec("nf"), consts("ones"), RMS_EPS2, out.rearrange("p (k t) -> p k t", k=KD))



def _shape_constants():
    n = np.arange(P)
    head, tok = n // HEAD, n % HEAD
    same = head[:, None] == head[None, :]
    near = (tok[:, None] // SUB) == (tok[None, :] // SUB)
    low = same & (tok[:, None] > tok[None, :])
    up = same & (tok[:, None] < tok[None, :])
    c = np.arange(HEAD)
    swap = np.zeros((P, P))
    for i in range(P):
        j = i % HEAD
        if j < 8:
            swap[i + 8, i] = 1
        elif j < 16:
            swap[i - 8, i] = 1
    parts = {
        "ident": np.eye(P), "ones": np.ones((P, P)), "heads": same,
        "swap": swap,
        "low_near": low & near, "low_far": low & ~near, "up_near": up & near, "up_far": up & ~near,
        "low_strict": low, "up_strict": up,
        "low_incl": tok[:, None] >= c[None, :], "up_incl": tok[:, None] <= c[None, :],
        "reset": np.broadcast_to((np.arange(T) % CHUNK != 0)[None, :], (P, T)),
        "slot": np.broadcast_to(np.arange(TOPK)[None, :], (P, TOPK)),
    }
    consts = np.concatenate([np.asarray(parts[k], np.float32) for k, _ in CONSTS], axis=1)
    t = np.arange(T)
    inv = [1.0 / (np.minimum(t + w // 2, T) - np.maximum(t - w // 2, 0)) for w in WINDOWS]
    inv_counts = np.broadcast_to(np.concatenate(inv).astype(np.float32)[None, :], (P, 4 * T))
    freq = np.power(np.float32(500000.0), -np.arange(0, 16, 2, dtype=np.float32) / np.float32(16))
    ang = (t.astype(np.float32)[:, None] * freq[None, :]).astype(np.float32)
    cos, sin = np.cos(ang).T, np.sin(ang).T
    table = np.zeros((P, 2, T), np.float32)
    table[:, 0] = 1
    for h in range(2):
        for half, sign in ((0, -1), (1, 1)):
            rows = slice(HEAD * h + 8 * half, HEAD * h + 8 * half + 8)
            table[rows, 0] = cos
            table[rows, 1] = sign * sin
    return consts, np.ascontiguousarray(inv_counts), table.reshape(P, 2 * T)


def _blocks(w):
    k, n = w.shape
    return np.ascontiguousarray(w.reshape(k // P, P, n // P, P).transpose(2, 1, 0, 3).reshape(n, k))


def _channels(a):
    return a.reshape(-1, P).T


def _widen(w, n):
    return np.concatenate([w, np.zeros((w.shape[0], n - w.shape[1]), w.dtype)], axis=1)


def _layout(inp):
    a = {k: np.asarray(v) for k, v in inp.items()}
    one = {k: v[0] for k, v in a.items() if v.ndim > 1}
    consts, inv_counts, rope = _shape_constants()
    rw = 12 * P + 2 * P + P + GATE_REST
    w_in = one["w_in"]
    w_in1 = np.concatenate([_widen(w_in[:, :rw], N_SHIFT * P), w_in[:, rw:]], axis=1)
    mu = _widen(one["shift_mu"], N_SHIFT * P)
    vectors = dict(norm1=one["norm1_w"], mu0=mu[0], mu1=mu[1], w0=one["w0"], a0=one["a0"], k_k=one["k_k"], k_a=one["k_a"],
                   r_k=one["r_k"], lnw=one["ln_x_w"], lnb=one["ln_x_b"], pool_scale=one["pool_scale"], norm2=one["norm2_w"],
                   norm_f=a["norm_f_w"], n1=one["n1_g_2"], n2=one["n2_g_2"], n3=one["n3_g_2"], nf=a["nf_g_2"])
    io = {
        "x": one["x"].T.reshape(KD, P, T).transpose(1, 0, 2).reshape(P, KD * T),
        "consts": consts, "inv_counts": inv_counts, "rope": rope,
        "vec": np.concatenate([_channels(vectors[k]) for k, _ in VECTORS], axis=1),
        "w_in": _blocks(w_in1),
        "lora": np.concatenate([one["w_up"].reshape(P, -1), one["a_up"].reshape(P, -1)], axis=1),
        "pool_w": one["pool_w"].transpose(1, 0, 2).reshape(P, 4 * P),
        "g_up": np.concatenate([one["g_up"], np.zeros((2 * P - P - GATE_REST, PAIRS * P), np.float32)]).reshape(
            2, P, PAIRS * P).transpose(1, 0, 2).reshape(P, -1),
        "w_out": _blocks(one["w_out"]),
        "peer_wq": _blocks(one["peer_wq"]),
        "peer_keys": one["peer_keys"].transpose(3, 0, 1, 2).reshape(P, -1),
        "peer_u": one["peer_u"], "peer_v": one["peer_v"],
    }
    for f in ("ffn1", "ffn2"):
        w = one[f"{f}_w_in_2"].reshape(D, 2, KF, P).transpose(0, 2, 1, 3).reshape(D, 2 * D_FF)
        io[f"{f}_w_in"] = _blocks(w)
        io[f"{f}_w_out"] = _blocks(one[f"{f}_w_out_2"])
    w = one["w_in_2"]
    sizes = (512, 512, 512, 512, 128, 128, 512, 64, 8, D, D)
    qa, ka, va, qb, kb, vb, qi, ki, wi, ga, gb = np.split(w, np.cumsum(sizes)[:-1], axis=1)
    order = [h * HEAD + c for j in range(4) for h in (j, j + 4) for c in range(HEAD)]
    io["w_in_2"] = _blocks(np.concatenate([qa, ka, va, qb[:, order], kb, vb, qi, ki, ki, _widen(wi, P), ga, gb], axis=1))
    ab = np.stack([_blocks(one["w_branch_a_2"]).reshape(KD, P, -1), _blocks(one["w_branch_b_2"][order]).reshape(KD, P, -1)], axis=1)
    io["w_branches"] = ab.reshape(2 * D, PAIRS * P)
    io["w_out_2"] = _blocks(one["w_out_2"])
    dist = np.clip(511 - np.arange(5 * P - 1), -128, 128) + 128
    io["bias_line"] = one["rel_bias_2"][:, dist]
    return {k: np.ascontiguousarray(v) for k, v in io.items()}


def kernel(**inputs):
    import concourse.bacc as _bacc
    from concourse.bass_utils import run_bass_kernel_spmd as _run

    nc = _bacc.Bacc("TRN2", target_bir_lowering=False, num_devices=1)
    arrays = _layout(inputs)
    io = {k: nc.dram_tensor(f"in_{k}", v.shape, mybir.dt.from_np(v.dtype), kind="ExternalInput").ap() for k, v in arrays.items()}
    io["out"] = nc.dram_tensor("out", (P, KD * T), F32, kind="ExternalOutput").ap()
    build(nc, io)
    r = _run(nc, [{f"in_{k}": v for k, v in arrays.items()}], core_ids=[0])
    y = r.results[0]["out"]
    return np.ascontiguousarray(y.reshape(P, KD, T).transpose(2, 1, 0).reshape(1, T, D))
```
